# Optimizing a Trainium2 kernel written in Bass

```python
import math
import jax, jax.numpy as jnp
from jax import lax
import numpy as np

D_MODEL = 1024
BATCH = 1
SEQ = 256
DEPTH = 2

RWKV_HEAD_SIZE = 64
RWKV_HEADS = D_MODEL // RWKV_HEAD_SIZE
DECAY_LORA = 64
AAA_LORA = 64
GATE_LORA = 128
RWKV_GN_EPS = 64e-5
N_LERP = 6
BRANCHES = ((128, 1), (512, 4), (2048, 16))
N_BRANCH = len(BRANCHES)
ATTN_HEAD_DIM = 64
HEADS_PER_BRANCH = 8
Q_DIM = N_BRANCH * HEADS_PER_BRANCH * ATTN_HEAD_DIM
ATTN_OUT_DIM = HEADS_PER_BRANCH * ATTN_HEAD_DIM
Q_BLOCK = 128
ALIBI_MAX = 8.0
FF_DENSE = 2816
N_EXPERTS = 8
TOP_K = 2
FF_EXPERT = 3584
RMS_EPS = 1e-5

kernel_name = "rwkv7_yoco_dilated_moe_block"

def _layer_counts():
    n_a = DEPTH - DEPTH // 2
    n_b = DEPTH // 2
    n_dense = (DEPTH + 1) // 2
    n_moe = DEPTH // 2
    return n_a, n_b, n_dense, n_moe

def rmsnorm(x, g):
    xf = x.astype(jnp.float32)
    y = xf * lax.rsqrt(jnp.mean(xf * xf, axis=-1, keepdims=True) + RMS_EPS)
    return (y * g.astype(jnp.float32)).astype(x.dtype)

def token_shift(h):
    return jnp.pad(h[:, :-1], ((0, 0), (1, 0), (0, 0)))

def wkv7_scan(r, decay, k, v, kk, a):
    b, _, h, n = r.shape

    def step(state, inp):
        r_t, w_t, k_t, v_t, kk_t, a_t = inp
        sa = jnp.einsum('bhvk,bhk->bhv', state, -kk_t)
        state = (state * w_t[:, :, None, :]
                 + sa[..., None] * (kk_t * a_t)[:, :, None, :]
                 + v_t[..., None] * k_t[:, :, None, :])
        y = jnp.einsum('bhvk,bhk->bhv', state, r_t)
        return state, y

    xs = tuple(jnp.moveaxis(t, 1, 0) for t in (r, decay, k, v, kk, a))
    state0 = jnp.zeros((b, h, n, n), jnp.float32)
    _, y = lax.scan(step, state0, xs)
    return jnp.moveaxis(y, 0, 1)

def rwkv7_time_mix(h, mu, wr, wk, wv, w0, w1, w2, a0, a1, a2, g1, g2,
                   k_k, k_a, r_k, lnx_w, lnx_b, wo):
    b, s, d = h.shape
    xx = token_shift(h) - h
    xr, xw, xk, xv, xa, xg = (h + xx * mu[i] for i in range(N_LERP))
    r = xr @ wr
    k = xk @ wk
    v = xv @ wv
    w_log = -jax.nn.softplus(-(w0 + jnp.tanh(xw @ w1) @ w2)) - 0.5
    a = jax.nn.sigmoid(a0 + (xa @ a1) @ a2)
    g = jax.nn.sigmoid(xg @ g1) @ g2

    def heads(t):
        return t.reshape(b, s, RWKV_HEADS, RWKV_HEAD_SIZE).astype(jnp.float32)

    kk = heads(k * k_k)
    kk = kk / jnp.maximum(jnp.sqrt(jnp.sum(kk * kk, axis=-1, keepdims=True)), 1e-12)
    k = k * (1.0 + (a - 1.0) * k_a)
    decay = jnp.exp(-jnp.exp(heads(w_log)))
    rh, kh, vh, ah = heads(r), heads(k), heads(v), heads(a)
    y = wkv7_scan(rh, decay, kh, vh, kk, ah)
    mean = jnp.mean(y, axis=-1, keepdims=True)
    var = jnp.mean(jnp.square(y - mean), axis=-1, keepdims=True)
    yn = ((y - mean) * lax.rsqrt(var + RWKV_GN_EPS)).reshape(b, s, d)
    yn = yn * lnx_w.astype(jnp.float32) + lnx_b.astype(jnp.float32)
    bonus = (jnp.sum(rh * kh * r_k.astype(jnp.float32), axis=-1, keepdims=True) * vh).reshape(b, s, d)
    return ((yn + bonus).astype(h.dtype) * g) @ wo

def dilated_branch(q, k, v, slopes, window, dilation):
    b, s, h, dh = q.shape
    n_keys = window // dilation + 1
    offs = jnp.arange(n_keys, dtype=jnp.int32) * dilation
    dist = offs.astype(jnp.float32)
    scale = 1.0 / math.sqrt(dh)
    slopes = slopes.astype(jnp.float32)

    def block(i):
        t = i * Q_BLOCK + jnp.arange(Q_BLOCK, dtype=jnp.int32)
        pos = t[:, None] - offs[None, :]
        valid = pos >= 0
        idx = jnp.maximum(pos, 0)
        qb = lax.dynamic_slice_in_dim(q, i * Q_BLOCK, Q_BLOCK, axis=1)
        kg = jnp.take(k, idx, axis=1)
        vg = jnp.take(v, idx, axis=1)
        sc = jnp.einsum('bqhd,bqkhd->bhqk', qb, kg).astype(jnp.float32) * scale
        sc = sc - slopes[None, :, None, None] * dist[None, None, None, :]
        sc = jnp.where(valid[None, None], sc, -jnp.inf)
        lse = jax.nn.logsumexp(sc, axis=-1)
        p = jnp.exp(sc - lse[..., None])
        o = jnp.einsum('bhqk,bqkhd->bqhd', p.astype(vg.dtype), vg)
        return o, jnp.transpose(lse, (0, 2, 1))

    o, lse = lax.map(block, jnp.arange(s // Q_BLOCK, dtype=jnp.int32))
    o = jnp.moveaxis(o, 0, 1).reshape(b, s, h, dh)
    lse = jnp.moveaxis(lse, 0, 1).reshape(b, s, h)
    return o, lse

def dilated_attention(h, wq, wo, k_sh, v_sh, slopes):
    b, s, _ = h.shape
    q = (h @ wq).reshape(b, s, N_BRANCH, HEADS_PER_BRANCH, ATTN_HEAD_DIM)
    outs, lses = [], []
    for gi, (window, dilation) in enumerate(BRANCHES):
        o, lse = dilated_branch(q[:, :, gi], k_sh[:, :, gi], v_sh[:, :, gi], slopes[gi], window, dilation)
        outs.append(o)
        lses.append(lse)
    wts = jax.nn.softmax(jnp.stack(lses), axis=0)
    o = jnp.sum(wts[..., None] * jnp.stack(outs).astype(jnp.float32), axis=0)
    return o.reshape(b, s, ATTN_OUT_DIM).astype(h.dtype) @ wo

def swiglu(h, w1, w3, w2):
    return (jax.nn.silu(h @ w1) * (h @ w3)) @ w2

def moe_swiglu(h, router, router_bias, w1, w3, w2):
    b, s, d = h.shape
    t = h.reshape(b * s, d)
    logits = (t @ router + router_bias).astype(jnp.float32)
    top_v, top_i = lax.top_k(logits, TOP_K)
    top_w = jax.nn.softmax(top_v, axis=-1)
    gates = jnp.sum(jax.nn.one_hot(top_i, N_EXPERTS, dtype=jnp.float32) * top_w[..., None], axis=1)
    out = jnp.zeros_like(t)
    for e in range(N_EXPERTS):
        out = out + gates[:, e:e + 1].astype(t.dtype) * swiglu(t, w1[e], w3[e], w2[e])
    return out.reshape(b, s, d)

def alibi_slopes():
    n = N_BRANCH * HEADS_PER_BRANCH
    sl = jnp.exp2(-ALIBI_MAX * (jnp.arange(n, dtype=jnp.float32) + 1.0) / n)
    return sl.reshape(N_BRANCH, HEADS_PER_BRANCH)

def setup_inputs(seed: int = 0) -> dict:
    key = jax.random.key(seed)
    ks = iter(jax.random.split(key, 48))
    n_a, n_b, n_dense, n_moe = _layer_counts()
    D = D_MODEL

    def nrm(shape, scale):
        return jax.random.normal(next(ks), shape, jnp.float32) * scale

    def unif(shape, lo, hi):
        return jax.random.uniform(next(ks), shape, jnp.float32, lo, hi)

    return {
        "x": nrm((BATCH, SEQ, D), 1.0),
        "norm_gain": 1.0 + nrm((DEPTH, 2, D), 0.05),
        "rwkv_mu": unif((n_a, N_LERP, D), 0.0, 1.0),
        "rwkv_wr": nrm((n_a, D, D), D ** -0.5),
        "rwkv_wk": nrm((n_a, D, D), D ** -0.5),
        "rwkv_wv": nrm((n_a, D, D), D ** -0.5),
        "rwkv_w0": unif((n_a, D), -6.0, -1.0),
        "rwkv_w1": nrm((n_a, D, DECAY_LORA), D ** -0.5),
        "rwkv_w2": nrm((n_a, DECAY_LORA, D), 0.5 * DECAY_LORA ** -0.5),
        "rwkv_a0": unif((n_a, D), -1.0, 1.0),
        "rwkv_a1": nrm((n_a, D, AAA_LORA), D ** -0.5),
        "rwkv_a2": nrm((n_a, AAA_LORA, D), 0.5 * AAA_LORA ** -0.5),
        "rwkv_g1": nrm((n_a, D, GATE_LORA), D ** -0.5),
        "rwkv_g2": nrm((n_a, GATE_LORA, D), GATE_LORA ** -0.5),
        "rwkv_k_k": 0.85 + nrm((n_a, D), 0.05),
        "rwkv_k_a": 1.0 + nrm((n_a, D), 0.05),
        "rwkv_r_k": nrm((n_a, RWKV_HEADS, RWKV_HEAD_SIZE), 0.1),
        "rwkv_lnx_w": 1.0 + nrm((n_a, D), 0.05),
        "rwkv_lnx_b": nrm((n_a, D), 0.02),
        "rwkv_wo": nrm((n_a, D, D), D ** -0.5),
        "kv_norm_gain": 1.0 + nrm((D,), 0.05),
        "w_kv": nrm((D, 2 * Q_DIM), D ** -0.5),
        "attn_wq": nrm((n_b, D, Q_DIM), D ** -0.5),
        "attn_wo": nrm((n_b, ATTN_OUT_DIM, D), ATTN_OUT_DIM ** -0.5),
        "ffn_w1": nrm((n_dense, D, FF_DENSE), D ** -0.5),
        "ffn_w3": nrm((n_dense, D, FF_DENSE), D ** -0.5),
        "ffn_w2": nrm((n_dense, FF_DENSE, D), FF_DENSE ** -0.5),
        "moe_router": nrm((n_moe, D, N_EXPERTS), D ** -0.5),
        "moe_router_bias": nrm((n_moe, N_EXPERTS), 0.01),
        "moe_w1": nrm((n_moe, N_EXPERTS, D, FF_EXPERT), D ** -0.5),
        "moe_w3": nrm((n_moe, N_EXPERTS, D, FF_EXPERT), D ** -0.5),
        "moe_w2": nrm((n_moe, N_EXPERTS, FF_EXPERT, D), FF_EXPERT ** -0.5),
        "final_norm_gain": 1.0 + nrm((D,), 0.05),
    }

def reference(x, norm_gain, rwkv_mu, rwkv_wr, rwkv_wk, rwkv_wv, rwkv_w0, rwkv_w1, rwkv_w2,
              rwkv_a0, rwkv_a1, rwkv_a2, rwkv_g1, rwkv_g2, rwkv_k_k, rwkv_k_a, rwkv_r_k,
              rwkv_lnx_w, rwkv_lnx_b, rwkv_wo, kv_norm_gain, w_kv, attn_wq, attn_wo,
              ffn_w1, ffn_w3, ffn_w2, moe_router, moe_router_bias, moe_w1, moe_w3, moe_w2,
              final_norm_gain):
    n_a, n_b, n_dense, n_moe = _layer_counts()
    b, s, _ = x.shape
    slopes = alibi_slopes()
    k_sh = v_sh = None
    for l in range(DEPTH):
        if l < n_a:
            h = rmsnorm(x, norm_gain[l, 0])
            x = x + rwkv7_time_mix(h, rwkv_mu[l], rwkv_wr[l], rwkv_wk[l], rwkv_wv[l],
                                   rwkv_w0[l], rwkv_w1[l], rwkv_w2[l],
                                   rwkv_a0[l], rwkv_a1[l], rwkv_a2[l],
                                   rwkv_g1[l], rwkv_g2[l], rwkv_k_k[l], rwkv_k_a[l], rwkv_r_k[l],
                                   rwkv_lnx_w[l], rwkv_lnx_b[l], rwkv_wo[l])
        else:
            if l == n_a:
                kv = (rmsnorm(x, kv_norm_gain) @ w_kv).reshape(
                    b, s, 2, N_BRANCH, HEADS_PER_BRANCH, ATTN_HEAD_DIM)
                k_sh, v_sh = kv[:, :, 0], kv[:, :, 1]
            j = l - n_a
            h = rmsnorm(x, norm_gain[l, 0])
            x = x + dilated_attention(h, attn_wq[j], attn_wo[j], k_sh, v_sh, slopes)
        h = rmsnorm(x, norm_gain[l, 1])
        if l % 2 == 0:
            i = l // 2
            x = x + swiglu(h, ffn_w1[i], ffn_w3[i], ffn_w2[i])
        else:
            i = l // 2
            x = x + moe_swiglu(h, moe_router[i], moe_router_bias[i], moe_w1[i], moe_w3[i], moe_w2[i])
    return rmsnorm(x, final_norm_gain)


_drawn_inputs = setup_inputs


def setup_inputs(seed=0):
    import zlib

    import numpy as np

    out = dict(_drawn_inputs(seed))
    spreads = {}
    factors = {}
    for name, (base, spread) in spreads.items():
        noise = np.random.default_rng([zlib.crc32(name.encode()), seed]).standard_normal(out[name].shape)
        drawn = base * np.exp(spread * noise) if base else spread * noise
        out[name] = __import__('jax').numpy.asarray(drawn.astype(out[name].dtype))
    for name, factor in factors.items():
        out[name] = (out[name] * factor).astype(out[name].dtype)
    return out
```

```python
import math
from contextlib import ExitStack

import numpy as np

import concourse.bass as bass
from concourse import mybir

F32 = mybir.dt.float32
I32 = mybir.dt.int32
ALU = mybir.AluOpType
ACT = mybir.ActivationFunctionType
X = mybir.AxisListType.X

P = 128
D = 1024
S = 256
NT = S // P
KC = D // P
HS = 64
CH = 64
NCH = S // CH
GROUPS = 4
LEVELS = 6
FF = 2816
FT = FF // P
FE = 3584
NE = 8
ECH = FE // 512
QD = 1536
QT_N = QD // P
SLOTS = 8
RING = 14
UNIT = 2048
RMS_EPS = 1e-5
GN_EPS = 64e-5
BIG = -3.0e30
DECAY = -math.exp(-0.5)

VECS = ["g00", "g01", "g10", "g11", "kvg", "mu0", "mu1", "mu2", "mu3", "mu4", "mu5",
        "w0", "a0", "k_k", "k_a", "r_k"]
VCOL = {n: 8 * i for i, n in enumerate(VECS)}


def constant_tables():
    p = np.arange(P)
    s = p % CH
    t = np.arange(CH)
    tabs = {}
    tabs["ident"] = np.eye(P)
    tabs["ones"] = np.ones((P, P))
    tabs["headones"] = (p[:, None] // HS == p[None, :] // HS)
    tabs["before"] = s[:, None] < t[None, :]
    tabs["upto"] = s[:, None] <= t[None, :]
    for lev in range(LEVELS):
        m = 1 << lev
        tabs[f"level{lev}"] = ((s[:, None] // (2 * m) == t[None, :] // (2 * m))
                               & (s[:, None] // m % 2 == 1) & (t[None, :] // m % 2 == 0))
    tabs["eye64"] = s[:, None] == t[None, :]
    half = np.stack([p < HS, p >= HS], 1).astype(np.float64)
    tabs["half"] = half
    tabs["minushalf"] = -half
    tabs["half8"] = half * HS ** -0.5
    tabs["earlier"] = p[:, None] < p[None, :]
    tabs["slotid"] = np.tile(p[None, :], (P, 1))
    e = np.arange(NE)
    tabs["tie"] = np.tile((e[None, :] < e[:, None]).reshape(1, -1), (P, 1))
    tabs["carry"] = np.tile((np.arange(512) % CH != 0)[None, :], (P, 1))
    return {k: v.astype(np.float32) for k, v in tabs.items()}


def distance_tables():
    out = []
    for qt in range(NT):
        q = qt * P + np.arange(P)[:, None]
        k = np.arange(P * (qt + 1))[None, :]
        dist = q - k
        for window, dil in ((128, 1), (512, 4), (2048, 16)):
            seen = (dist >= 0) & (dist % dil == 0) & (dist <= window)
            out.append(np.where(seen, -dist, BIG))
    return np.concatenate(out, 1).astype(np.float32)


def slopes():
    n = 3 * SLOTS
    return np.exp2(-8.0 * (np.arange(n, dtype=np.float32) + 1.0) / n).reshape(3, SLOTS)


CONST_SHAPES = {k: v.shape[1] for k, v in constant_tables().items()}
CCOL = {}
_at = 0
for _k, _n in CONST_SHAPES.items():
    CCOL[_k] = _at
    _at += _n
NCONST = _at
NDIST = 3 * P + 3 * 2 * P


class Own:

    def __init__(self, eng, sem):
        self.eng, self.sem, self.count = eng, sem, {}
        self.base = {}

    def do(self, ins, sem=None):
        key = sem if sem is not None else self.sem
        name = str(key)
        self.count[name] = self.count.get(name, 0) + 1
        ins.then_inc(key, 1)
        self.eng.wait_ge(key, self.base.get(name, 0) + self.count[name])

    def at(self, sem=None):
        return self.count.get(str(sem if sem is not None else self.sem), 0)


def trunk(nc, A, out):
    ctx = ExitStack()
    with ctx:
        def sb(name, shape, dt=F32):
            return ctx.enter_context(nc.sbuf_tensor(name, shape, dt))

        sems = {}

        def sem(name):
            if name not in sems:
                sems[name] = ctx.enter_context(nc.semaphore(name))
            return sems[name]

        C = sb("consts", [P, NCONST])
        V = sb("vectors", [P, 8 * len(VECS)])
        x = sb("x_residual", [P, NT, D])
        BIGB = sb("ring_and_scan", [P, RING * UNIT + 3072])
        PERS = sb("phase_buffers", [P, 8 * 2048 + 32])
        small = sb("small", [P, 256])
        PS = ctx.enter_context(nc.psum_tensor("psum", [P, 8, 512], F32))

        def cst(name):
            return C[:, CCOL[name]:CCOL[name] + CONST_SHAPES[name]]

        def vec(name):
            return V[:, VCOL[name]:VCOL[name] + 8]

        ident, ones = cst("ident"), cst("ones")

        def half(p):
            return C[:, CCOL["half"] + p:CCOL["half"] + p + 1]

        def minushalf(p):
            return C[:, CCOL["minushalf"] + p:CCOL["minushalf"] + p + 1]

        def half8(p):
            return C[:, CCOL["half8"] + p:CCOL["half8"] + p + 1]

        def pers(at, n):
            return PERS[:, at:at + n]

        HT_, L0_, L1_, R_, K_, A_, LD_, VN_ = [0] + [2080 + 2048 * i for i in range(7)]
        extra = BIGB[:, RING * UNIT:RING * UNIT + 3072]

        hT = pers(HT_, 8 * 257).rearrange("p (c t) -> p c t", c=8)
        lerp = [pers(o, 2048).rearrange("p (c t) -> p c t", c=8) for o in (L0_, L1_)]
        dxT = extra[:, 0:2048].rearrange("p (c t) -> p c t", c=8)
        rT, kT, aT, ldT = [pers(o, 2048).rearrange("p (c t) -> p c t", c=8) for o in (R_, K_, A_, LD_)]
        vN = pers(VN_, 2048).rearrange("p (n d) -> p n d", n=NT)
        vC = pers(L0_, 2048).rearrange("p (c j v) -> p c j v", c=8, j=NCH)
        yC = pers(HT_, 2048).rearrange("p (c j v) -> p c j v", c=8, j=NCH)
        lnx = pers(L1_, 2048).rearrange("p (a d) -> p a d", a=2)

        def nat(at):
            return pers(at, 2048).rearrange("p (n d) -> p n d", n=NT)

        def featT(at):
            return pers(at, 2048).rearrange("p (c t) -> p c t", c=8)

        ss = small[:, 0:2]
        std = small[:, 2:4]
        rstd = small[:, 4:6]
        bonus = small[:, 8:40].rearrange("p (n h) -> p n h", n=NT)
        one_minus_ka = small[:, 40:48]
        gnm = [small[:, 48 + 8 * i:56 + 8 * i] for i in range(2)]
        gns = [small[:, 64 + 8 * i:72 + 8 * i] for i in range(2)]
        decayC = [small[:, 80 + 8 * i:88 + 8 * i] for i in range(2)]
        negmax = small[:, 96:98]
        denom = small[:, 98:100]
        rden = small[:, 100:102]
        loraT = sb("loraT", [P, 3, S])

        def w_slot(n):
            return BIGB[:, (n % RING) * UNIT:(n % RING + 1) * UNIT]

        def kview(w):
            return w.rearrange("(k p) n -> p k n", p=P)

        units = []
        free_at = []

        def cols_units(w, c0, cw, free):
            per = UNIT // cw
            for k0 in range(0, KC, per):
                free_at.append(free)
                units.append([((per, cw), slice(0, per), None, kview(w)[:, k0:k0 + per, c0:c0 + cw])])

        wr, wk, wv, wo_r = (A[n][0] for n in ("rwkv_wr", "rwkv_wk", "rwkv_wv", "rwkv_wo"))
        for iw, w in enumerate((wr, wk)):
            for ch in range(2):
                cols_units(w, 512 * ch, 512, ("proj_done", 4 * iw + 2 * ch + 2))
        U_LORA1 = len(units)
        free_at.append(("proj_done", 11))
        units.append([((8, 256), slice(0, 8), slice(0, 64), kview(A["rwkv_w1"][0])),
                      ((8, 256), slice(0, 8), slice(64, 128), kview(A["rwkv_a1"][0])),
                      ((8, 256), slice(0, 8), slice(128, 256), kview(A["rwkv_g1"][0]))])
        for ch in range(2):
            cols_units(wv, 512 * ch, 512, ("proj_done", 11 + 2 * ch + 2))
        U_LORA2 = len(units)
        free_at.append(("proj_done", 23))
        units.append([("rows64", 0, A["rwkv_w2"][0]), ("rows64", 1, A["rwkv_a2"][0])])
        assert len(units) == RING
        U_G2 = len(units)
        free_at.append(("gate_mm", 4))
        units.append([("rows128", 0, A["rwkv_g2"][0])])
        U_WO = len(units)
        for ch in range(2):
            cols_units(wo_r, 512 * ch, 512, ("x_mm", 2 * ch + 2))
        U_FFN = len(units)
        for c0 in range(0, FF, 512):
            cw = min(512, FF - c0)
            for w in ("ffn_w1", "ffn_w3"):
                cols_units(A[w][0], c0, cw, ("ffn_up_mm", 2 * (c0 + cw) // P))
        U_FFN2 = len(units)
        for f0 in range(0, FT, 2):
            free_at.append(("ffn_down_mm", f0 // 2 + 1) if f0 < FT - 2 else ("x_mm", 8))
            units.append([((2, D), slice(0, 2), None, kview(A["ffn_w2"][0])[:, f0:f0 + 2, :])])
        U_KV = len(units)
        for ch in range(2 * QD // 512):
            cols_units(A["w_kv"], 512 * ch, 512, ("att_proj_done", 2 * ch + 2))
        U_Q = len(units)
        for ch in range(QD // 512):
            cols_units(A["attn_wq"][0], 512 * ch, 512, ("att_proj_done", 12 + 2 * ch + 2))
        U_AWO = len(units)
        for k0 in (0, 2):
            free_at.append(("x_mm", 12))
            units.append([((2, D), slice(0, 2), None, kview(A["attn_wo"][0])[:, k0:k0 + 2, :])])
        U_MOE = len(units)

        slot_sem = [sem(f"slot{i}_loaded") for i in range(RING)]
        loaded_at = []
        slot_total = [0] * RING
        for n, u in enumerate(units):
            slot_total[n % RING] += 16 * len(u)
            loaded_at.append(slot_total[n % RING])

        def unit_cols(n, per, cw):
            return w_slot(n)[:, 0:per * cw].rearrange("p (k n) -> p k n", k=per)

        moe_order = []
        for j in range(ECH):
            moe_order += [("w1", j, 0), ("w1", j, 1), ("w3", j, 0), ("w3", j, 1)]
            if j:
                moe_order += [("w2", j - 1, 0), ("w2", j - 1, 1)]
        moe_order += [("w2", ECH - 1, 0), ("w2", ECH - 1, 1)]
        PER_E = len(moe_order)
        assert PER_E % RING == 0
        moe_at = {key: n for n, key in enumerate(moe_order)}
        REUSE = PER_E // RING

        def moe_free(key):
            w, j, _ = key
            return {"w1": ("up_mm", 2 * ECH, 2 * j + 1), "w3": ("up_mm", 2 * ECH, 2 * j + 2),
                    "w2": ("down_mm", ECH, j + 1)}[w]

        def weights_here(pe, n):
            pe.wait_ge(slot_sem[n % RING], loaded_at[n])

        def moe_slot(key):
            return (U_MOE + moe_at[key]) % RING

        def moe_weights_here(pe, key, i):
            s = moe_slot(key)
            pe.wait_ge(slot_sem[s], 16 * REUSE * i + (slot_total[s] + 16 * (moe_at[key] // RING + 1)))

        class SetBuf:
            pass

        sets = []
        for si in range(2):
            o = [si * ((RING * UNIT + 3072) // 2)]

            def take(n):
                r = BIGB[:, o[0]:o[0] + n]
                o[0] += n
                return r

            b = SetBuf()
            bd = lambda v: v.rearrange("p (m h t) -> p m h t", m=8, h=2)
            cm = lambda v: v.rearrange("p (m t) -> p m t", m=8)
            b.AR = take(1024).rearrange("p (m q t) -> p m q t", m=8, q=2)
            b.Abd, b.Rbd, b.Bbd, b.Kbd, b.BhT, b.KhT = [bd(take(1024)) for _ in range(6)]
            b.BhN, b.KhN = [bd(take(1024)) for _ in range(2)]
            over = take(4096)
            b.sc = [over[:, 512 * i:512 * i + 512] for i in range(8)]
            b.N, b.Lk, b.Mb, b.Mk = [bd(over[:, 1024 * i:1024 * (i + 1)]) for i in range(4)]
            b.X, b.Y, b.Z = [cm(take(512)) for _ in range(3)]
            b.Ybd, b.Zbd = b.Bbd, b.Kbd
            b.S = take(128).rearrange("p (c v) -> p c v", c=2)
            b.U0 = take(128).rearrange("p (c v) -> p c v", c=2)
            b.U = take(128).rearrange("p (c v) -> p c v", c=2)
            sets.append(b)
        assert o[0] <= RING * UNIT + 3072, o[0]

        def flat(v):
            return v.rearrange("p c t -> p (c t)")

        def c8(v):
            return v.rearrange("p c (j t) -> p (c j) t", t=CH)

        def s8(v):
            return v.rearrange("p (m t) -> p m t", t=CH)

        def bc(v, shape):
            return v.to_broadcast(shape)

        def mid(v, n):
            return v.unsqueeze(1).to_broadcast([P, n, v.shape[1]])

        def last(v, n):
            return v.unsqueeze(2).to_broadcast([P, v.shape[1], n])

        yN = nat(R_)
        zT = featT(K_)
        ffn_in = featT(K_)
        silu_sb = pers(R_, 1024).rearrange("p (b t) -> p b t", b=4)
        actT = pers(A_, FT * S).rearrange("p (f t) -> p f t", f=FT)
        kvT = pers(HT_, 2048).rearrange("p (c t) -> p c t", c=8)
        qinT = featT(L0_)
        dist = pers(HT_, NDIST)
        kTa = pers(L1_, QT_N * S).rearrange("p (f t) -> p f t", f=QT_N)
        vNa = pers(L1_ + QT_N * S, NT * QD).rearrange("p (n d) -> p n d", n=NT)
        qTa = pers(L1_ + 2 * QT_N * S, QT_N * 2 * S).rearrange("p (f h t) -> p f h t", f=QT_N, h=2)
        prob = [extra[:, 768 * i:768 * i + 768] for i in range(2)]
        probT = [extra[:, 1536 + 768 * i:1536 + 768 * i + 768] for i in range(2)]
        oN = pers(L0_, NT * 512).rearrange("p (n d) -> p n d", n=NT)
        oT = pers(L0_ + 1024, 4 * S).rearrange("p (c t) -> p c t", c=4)
        hN = nat(L1_)
        hTm = featT(K_)
        router = pers(HT_, 64).rearrange("p (k e) -> p k e", k=KC)
        router_bias = pers(HT_ + 64, 8)
        logits = pers(HT_ + 80, 16).rearrange("p (n e) -> p n e", n=NT)
        expl = pers(HT_ + 96, 16).rearrange("p (n e) -> p n e", n=NT)
        chosen = pers(HT_ + 112, 16).rearrange("p (n e) -> p n e", n=NT)
        gates = pers(HT_ + 128, 17 * NT).rearrange("p (n e) -> p n e", n=NT)
        slotof = pers(HT_ + 168, 17 * NT).rearrange("p (n e) -> p n e", n=NT)
        beats = pers(HT_ + 208, 64).rearrange("p (e j) -> p e j", e=NE)
        ties = pers(HT_ + 272, 64).rearrange("p (e j) -> p e j", e=NE)
        nrank = pers(HT_ + 336, 8)
        top = pers(HT_ + 344, 8)
        overflow = sb("overflow", [P, 1], I32)
        final_gain = pers(HT_ + 1024, 1024)
        onehot = pers(L0_, 256).rearrange("p (n s) -> p n s", n=NT)
        gated = pers(L0_ + 256, 256).rearrange("p (n s) -> p n s", n=NT)
        scatT = pers(L0_ + 512, 256)
        siluE = pers(L0_ + 768, 512)
        hidE = pers(L0_ + 1280, 512)
        out_sb = nat(R_)
        hTe = pers(A_, 1024).rearrange("p (k n) -> p k n", k=KC)
        hidT = pers(A_ + 1024, 512).rearrange("p (f n) -> p f n", f=4)
        ySB = pers(LD_, 1024)
        NORM_XN = [nat(L0_), nat(L0_), nat(L1_), hN]
        SQ = [PS[:, 4 + 2 * n:6 + 2 * n, :].rearrange("p b n -> p (b n)") for n in range(NT)]

        block = ctx.enter_context(nc.Block())

        @block.sync
        def _(sp):
            sp.dma_start(x[:], A["x"][0].rearrange("(n p) d -> p n d", p=P)).then_inc(sem("x_loaded"), 16)
            sp.dma_start(C[:], A["const_tables"]).then_inc(sem("consts_loaded"), 16)
            sp.dma_start(V[:], A["vectors"]).then_inc(sem("vectors_loaded"), 16)
            for n, u in enumerate(units):
                if n == RING:
                    sp.wait_ge(sem("scan_over"), 1)
                if n >= RING:
                    sp.wait_ge(sem(free_at[n - RING][0]), free_at[n - RING][1])
                for part in u:
                    if part[0] == "rows64":
                        dst = w_slot(n)[0:64, part[1] * D:(part[1] + 1) * D]
                        src = part[2]
                    elif part[0] == "rows128":
                        dst, src = w_slot(n)[:, 0:D], part[2]
                    else:
                        (per, cw), ks, cs, src = part
                        dst = unit_cols(n, per, cw)[:, ks, cs if cs is not None else slice(0, cw)]
                    sp.dma_start(dst, src).then_inc(slot_sem[n % RING], 16)

            wview = {w: A[f"moe_{w}"].rearrange("a e (k p) n -> (a e) p k n", p=P) for w in ("w1", "w3", "w2")}

            def load_unit(e, m):
                w, j, h = moe_order[m]
                s = (U_MOE + m) % RING
                if w == "w2":
                    dst = unit_cols(s, 2, D)
                    src = wview[w][e, :, 4 * j + 2 * h:4 * j + 2 * h + 2, :]
                else:
                    dst = unit_cols(s, 4, 512)
                    src = wview[w][e, :, 4 * h:4 * h + 4, 512 * j:512 * j + 512]
                sp.dma_start(dst, src).then_inc(slot_sem[s], 16)

            def expert_units(e, i, ms):
                for m in ms:
                    name, per, within = moe_free(moe_order[(m - RING) % PER_E])
                    sp.wait_ge(sem(name), per * i + within)
                    load_unit(e, m)

            def stream_experts(i0):
                with sp.Fori(0, NE - 1) as e:
                    i = e + i0 if i0 else e
                    expert_units(e, i, range(RING, PER_E))
                    expert_units(e + 1, i, range(RING))
                expert_units(NE - 1, i0 + NE - 1, range(RING, PER_E))

            for m in range(RING):
                name, value = free_at[U_MOE + m - RING]
                sp.wait_ge(sem(name), value)
                load_unit(0, m)
            stream_experts(0)
            sp.wait_ge(sem("overflow_known"), 1)
            more = sp.value_load(overflow[0:1, 0:1])
            with sp.If(more > 0):
                expert_units(0, NE - 1, range(RING))
                stream_experts(NE)
            for n in range(NT):
                sp.wait_ge(sem("out_ready"), n + 1)
                sp.dma_start(out[0].rearrange("(n p) d -> p n d", p=P)[:, n, :],
                             out_sb[:, n, :]).then_inc(sem("out_stored"), 16)
            sp.wait_ge(sem("out_stored"), 16 * NT)

        @block.gpsimd
        def _(pool):
            pool.wait_ge(sem("proj_evac"), 15)
            pool.wait_ge(sem("proj_done"), 15)
            for p in range(2):
                for j in range(NCH):
                    pool.dma_start(
                        vC[p * 64:p * 64 + 64, :, j, :],
                        vN[(j % 2) * 64:(j % 2) * 64 + 64, j // 2, :].rearrange("t (c h v) -> t c h v", c=8, h=2)[:, :, p, :],
                    ).then_inc(sem("v_paired"), 16)
            pool.dma_start(lnx, A["lnx_rows"].rearrange("p (a d) -> p a d", a=2)).then_inc(sem("lnx_loaded"), 16)
            pool.wait_ge(sem("y_normed"), GROUPS)
            for p in range(2):
                for j in range(NCH):
                    pool.dma_start(
                        yN[(j % 2) * 64:(j % 2) * 64 + 64, j // 2, :].rearrange("t (c h v) -> t c h v", c=8, h=2)[:, :, p, :],
                        yC[p * 64:p * 64 + 64, :, j, :],
                    ).then_inc(sem("y_natural"), 16)
            pool.wait_ge(sem("att_proj_evac"), 12)
            pool.dma_start(dist[:], A["distance_tables"]).then_inc(sem("dist_loaded"), 16)
            pool.wait_ge(sem("x_added"), 12)
            pool.dma_start(router, kview(A["moe_router"][0])).then_inc(sem("router_loaded"), 16)
            pool.dma_start(router_bias, A["router_bias_rows"]).then_inc(sem("router_loaded"), 16)
            pool.dma_start(final_gain, A["final_gain_rows"]).then_inc(sem("final_gain_loaded"), 16)

        @block.tensor
        def _(pe):
            mm = nc.tensor.matmul

            def norm_transposes(k):
                pe.wait_ge(sem("norm_scaled"), k + 1)
                src = NORM_XN[k]
                for b in range(4):
                    for q in range(4):
                        c, n = 2 * b + q // 2, q % 2
                        ins = nc.tensor.transpose(PS[:, b, q * P:(q + 1) * P], src[:, n, c * P:(c + 1) * P], ident)
                    ins.then_inc(sem("norm_transposed"), 1)

            pe.wait_ge(sem("consts_loaded"), 16)
            norm_transposes(0)

            job = [0]

            def job_bank(evac="proj_evac", mod=4):
                if job[0] >= mod:
                    pe.wait_ge(sem(evac), job[0] - mod + 1)
                job[0] += 1
                return (job[0] - 1) % mod

            def proj_T(u0, src, ncols, wait_each, evac, done):
                for ch in range(ncols // 512):
                    for half_ in range(2):
                        weights_here(pe, u0 + 2 * ch + half_)
                    for f2 in range(2):
                        b = job_bank(evac)
                        for fi in range(2):
                            f = 2 * f2 + fi
                            for k in range(KC):
                                w = unit_cols(u0 + 2 * ch + k // 4, 4, 512)
                                ins = mm(PS[:, b, fi * S:(fi + 1) * S], w[:, k % 4, f * P:(f + 1) * P], src[:, k, :],
                                         start=(k == 0), stop=(k == KC - 1))
                        ins.then_inc(sem(done), 1)

            def proj_N(u0, src, ncols, evac, done):
                for ch in range(ncols // 512):
                    for half_ in range(2):
                        weights_here(pe, u0 + 2 * ch + half_)
                    for n in range(NT):
                        b = job_bank(evac)
                        for k in range(KC):
                            w = unit_cols(u0 + 2 * ch + k // 4, 4, 512)
                            ins = mm(PS[:, b, :], src[:, k, n * P:(n + 1) * P], w[:, k % 4, :],
                                     start=(k == 0), stop=(k == KC - 1))
                        ins.then_inc(sem(done), 1)

            pe.wait_ge(sem("lerp_ready"), 1)
            proj_T(0, lerp[0], D, None, "proj_evac", "proj_done")
            pe.wait_ge(sem("lerp_ready"), 2)
            proj_T(4, lerp[1], D, None, "proj_evac", "proj_done")
            weights_here(pe, U_LORA1)
            for i, (lo, hi) in enumerate(((0, 64), (64, 128), (128, 256))):
                pe.wait_ge(sem("lerp_ready"), 3 + i)
                b = job_bank()
                for k in range(KC):
                    ins = mm(PS[0:hi - lo, b, 0:S], unit_cols(U_LORA1, 8, 256)[:, k, lo:hi], lerp[i % 2][:, k, :],
                             start=(k == 0), stop=(k == KC - 1))
                ins.then_inc(sem("proj_done"), 1)
            pe.wait_ge(sem("lerp_ready"), 6)
            proj_N(U_LORA1 + 1, lerp[1], D, "proj_evac", "proj_done")
            weights_here(pe, U_LORA2)
            for i in range(2):
                for f2 in range(4):
                    b = job_bank()
                    for fi in range(2):
                        f = 2 * f2 + fi
                        ins = mm(PS[:, b, fi * S:(fi + 1) * S],
                                 w_slot(U_LORA2)[0:64, i * D + f * P:i * D + (f + 1) * P], loraT[0:64, i, :],
                                 start=True, stop=True)
                    ins.then_inc(sem("proj_done"), 1)

            for gp in range(2):
                gs = [(2 * gp + si, si, sets[si], 4 * si) for si in range(2)]
                for g, si, b, bank in gs:
                    pe.wait_ge(sem("kk_squared"), g + 1)
                    mm(PS[:, bank, :], cst("headones"), b.sc[1], start=True, stop=True).then_inc(sem("kk_norm_mm"), 1)
                for g, si, b, bank in gs:
                    pe.wait_ge(sem("rk_ready"), g + 1)
                    for n in range(NT):
                        for c in range(2):
                            ins = mm(PS[:, bank + 1, n * 4 + 2 * c:n * 4 + 2 * c + 2],
                                     b.sc[3][:, c * S + n * P:c * S + (n + 1) * P], cst("half"),
                                     start=True, stop=True)
                    ins.then_inc(sem("bonus_mm"), 1)
                for g, si, b, bank in gs:
                    pe.wait_ge(sem("tails_ready"), g + 1)
                    for m in range(8):
                        ins = nc.tensor.transpose(PS[:, bank + 2 + m // 4, (m % 4) * P:(m % 4 + 1) * P],
                                                  b.BhT[:, m].rearrange("p h t -> p (h t)"), ident)
                    ins.then_inc(sem("tailsT_mm"), 1)
                    pe.wait_ge(sem("bonus_taken"), g + 1)
                    for m in range(8):
                        ins = nc.tensor.transpose(PS[:, bank + m // 4, (m % 4) * P:(m % 4 + 1) * P],
                                                  b.KhT[:, m].rearrange("p h t -> p (h t)"), ident)
                    ins.then_inc(sem("tailsT_mm"), 1)
                for g, si, b, bank in gs:
                    pe.wait_ge(sem("grams_in"), g + 1)
                    for i, src in enumerate((b.Bbd, b.Kbd)):
                        pe.wait_ge(sem("tails_taken"), 2 * g + 1 + i)
                        for m in range(8):
                            ins = mm(PS[:, bank + (2 - 2 * i) + m // 4, (m % 4) * P:(m % 4 + 1) * P],
                                     src[:, m].rearrange("p h t -> p (h t)"), b.AR[:, m].rearrange("p q t -> p (q t)"),
                                     start=True, stop=True)
                        ins.then_inc(sem("grams_mm"), 1)
                for lev in range(LEVELS):
                    for g, si, b, bank in gs:
                        q = gp * 2 * LEVELS + 2 * lev + si
                        if lev == 0:
                            pe.wait_ge(sem("grams_taken"), g + 1)
                        else:
                            pe.wait_ge(sem("X_ready"), gp * 2 * (LEVELS - 1) + 2 * (lev - 1) + si + 1)
                        rhs = (lambda m: cst("eye64")) if lev == 0 else (lambda m, b=b: b.X[:, m])
                        for m in range(8):
                            ins = mm(PS[:, bank, m * CH:(m + 1) * CH], b.N[:, m].rearrange("p h t -> p (h t)"), rhs(m),
                                     start=True, stop=True)
                        ins.then_inc(sem("LX_mm"), 1)
                    for g, si, b, bank in gs:
                        q = gp * 2 * LEVELS + 2 * lev + si
                        if 0 < lev < LEVELS - 1:
                            pe.wait_ge(sem("Z_ready"), q + 1)
                            if lev > 0:
                                pe.wait_ge(sem("Ybd_ready"), q - 1)
                            for m in range(8):
                                ins = mm(PS[:, bank + 1, m * CH:(m + 1) * CH], b.Ybd[:, m].rearrange("p h t -> p (h t)"),
                                         b.Z[:, m], start=True, stop=True)
                            ins.then_inc(sem("XZ_mm"), 1)
                    for g, si, b, bank in gs:
                        q = gp * 2 * LEVELS + 2 * lev + si
                        pe.wait_ge(sem("Zbd_ready"), q + 1)
                        rhs = (lambda m: cst("eye64")) if lev == 0 else (lambda m, b=b: b.Y[:, m])
                        for m in range(8):
                            ins = mm(PS[:, bank + 2, m * CH:(m + 1) * CH], b.Zbd[:, m].rearrange("p h t -> p (h t)"),
                                     rhs(m), start=True, stop=True)
                        ins.then_inc(sem("ZY_mm"), 1)
                for j in range(NCH):
                    q0 = gp * 2 * NCH + 2 * j
                    for g, si, b, bank in gs:
                        if j == 0:
                            pe.wait_ge(sem("v_paired"), 16 * 8)
                            pe.wait_ge(sem("Ybd_ready"), gp * 2 * LEVELS + 2 * (LEVELS - 1) + si + 1)
                        pe.wait_ge(sem("state_ready"), gp * 2 * (NCH + 1) + 2 * j + si + 1)
                        for c in range(2):
                            m = 4 * c + j
                            o_ = PS[:, bank + 3, c * 64:(c + 1) * 64]
                            mm(o_, b.Abd[:, m].rearrange("p h t -> p (h t)"), b.S[:, c], start=True, stop=False)
                            ins = mm(o_, b.Lk[:, m].rearrange("p h t -> p (h t)"), vC[:, 2 * g + c, j], start=False, stop=True)
                        ins.then_inc(sem("U0_mm"), 1)
                    for g, si, b, bank in gs:
                        pe.wait_ge(sem("U0_ready"), q0 + si + 1)
                        for c in range(2):
                            ins = mm(PS[:, bank + 3, 128 + c * 64:128 + (c + 1) * 64],
                                     b.Ybd[:, 4 * c + j].rearrange("p h t -> p (h t)"), b.U0[:, c], start=True, stop=True)
                        ins.then_inc(sem("U_mm"), 1)
                    for g, si, b, bank in gs:
                        pe.wait_ge(sem("U_ready"), q0 + si + 1)
                        for c in range(2):
                            m = 4 * c + j
                            o_ = PS[:, bank + 3, 384 + c * 64:384 + (c + 1) * 64]
                            mm(o_, b.BhN[:, m].rearrange("p h t -> p (h t)"), b.U[:, c], start=True, stop=False)
                            ins = mm(o_, b.KhN[:, m].rearrange("p h t -> p (h t)"), vC[:, 2 * g + c, j], start=False, stop=True)
                        ins.then_inc(sem("S_mm"), 1)
                        if j:
                            pe.wait_ge(sem("y_taken"), q0 + si - 1)
                        for c in range(2):
                            m = 4 * c + j
                            o_ = PS[:, bank + 2, c * 64:(c + 1) * 64]
                            mm(o_, b.Rbd[:, m].rearrange("p h t -> p (h t)"), b.S[:, c], start=True, stop=False)
                            mm(o_, b.Mb[:, m].rearrange("p h t -> p (h t)"), b.U[:, c], start=False, stop=False)
                            ins = mm(o_, b.Mk[:, m].rearrange("p h t -> p (h t)"), vC[:, 2 * g + c, j], start=False, stop=True)
                        ins.then_inc(sem("y_mm"), 1)

            weights_here(pe, U_G2)
            pe.wait_ge(sem("y_taken"), 2 * NCH * 2)
            for n in range(NT):
                for ch in range(2):
                    ins = mm(PS[:, 2 * n + ch, :], loraT[:, 2, n * P:(n + 1) * P], w_slot(U_G2)[:, ch * 512:(ch + 1) * 512],
                             start=True, stop=True)
                    ins.then_inc(sem("gate_mm"), 1)
            for n in range(NT):
                pe.wait_ge(sem("z_ready"), 2 * n + 2)
                for c in range(KC):
                    ins = nc.tensor.transpose(PS[:, 4 + c // 2, (c % 2) * S + n * P:(c % 2) * S + (n + 1) * P],
                                              yN[:, n, c * P:(c + 1) * P], ident)
            ins.then_inc(sem("zT_mm"), 1)

            def proj_x(u0, src, evac_base):
                for ch in range(2):
                    for half_ in range(2):
                        weights_here(pe, u0 + 2 * ch + half_)
                    for n in range(NT):
                        for k in range(KC):
                            w = unit_cols(u0 + 2 * ch + k // 4, 4, 512)
                            ins = mm(PS[:, 2 * ch + n, :], src[:, k, n * P:(n + 1) * P], w[:, k % 4, :],
                                     start=(k == 0), stop=(k == KC - 1))
                        ins.then_inc(sem("x_mm"), 1)

            pe.wait_ge(sem("zT_ready"), 4)
            proj_x(U_WO, zT, 0)

            norm_transposes(1)
            pe.wait_ge(sem("normT_ready"), 8)
            u = U_FFN
            for f in range(FT):
                if f >= 4:
                    pe.wait_ge(sem("ffn_hidden"), f - 3)
                cw = min(512, FF - f // 4 * 512)
                per = UNIT // cw
                nu = KC // per
                if f % 4 == 0:
                    for i in range(2 * nu):
                        weights_here(pe, u + i)
                for i in range(2):
                    for k in range(KC):
                        w = unit_cols(u + i * nu + k // per, per, cw)
                        ins = mm(PS[:, f % 4, i * S:(i + 1) * S], w[:, k % per, (f % 4) * P:(f % 4 + 1) * P],
                                 ffn_in[:, k, :], start=(k == 0), stop=(k == KC - 1))
                    ins.then_inc(sem("ffn_up_mm"), 1)
                if f % 4 == 3 or f == FT - 1:
                    u += 2 * nu
            for f in range(FT):
                if f % 2 == 0:
                    weights_here(pe, U_FFN2 + f // 2)
                pe.wait_ge(sem("ffn_hidden"), f + 1)
                for n in range(NT):
                    for h in range(2):
                        ins = mm(PS[:, 4 + 2 * h + n, :], actT[:, f, n * P:(n + 1) * P],
                                 unit_cols(U_FFN2 + f // 2, 2, D)[:, f % 2, h * 512:(h + 1) * 512],
                                 start=(f == 0), stop=(f == FT - 1))
                        if f == FT - 1:
                            ins.then_inc(sem("x_mm"), 1)
                        elif f % 2 == 1 and n == NT - 1 and h == 1:
                            ins.then_inc(sem("ffn_down_mm"), 1)

            norm_transposes(2)
            pe.wait_ge(sem("normT_ready"), 16)
            job[0] = 0
            proj_T(U_KV, kvT, QD, None, "att_proj_evac", "att_proj_done")
            proj_N(U_KV + 6, kvT, QD, "att_proj_evac", "att_proj_done")
            proj_T(U_Q, qinT, QD, None, "att_proj_evac", "att_proj_done")
            pe.wait_ge(sem("att_proj_evac"), 18)
            NI = NT * SLOTS

            def scores(i):
                hs, qt = divmod(i, NT)
                nk = (qt + 1) * P
                if i >= 2:
                    pe.wait_ge(sem("scores_taken"), i - 1)
                o_ = PS[:, 2 * (i % 2):2 * (i % 2) + 2, :].rearrange("p b n -> p (b n)")
                for br in range(3):
                    f = 4 * br + hs // 2
                    ins = mm(o_[:, br * nk:(br + 1) * nk], qTa[:, f, hs % 2, qt * P:(qt + 1) * P], kTa[:, f, 0:nk],
                             start=True, stop=True)
                ins.then_inc(sem("scores_mm"), 1)

            def prob_transposes(i):
                nb = 3 * (i % 2 + 1)
                pe.wait_ge(sem("prob_ready"), i + 1)
                if i >= 1:
                    pe.wait_ge(sem("probT_ready"), i)
                o_ = PS[:, 4:6, :].rearrange("p b n -> p (b n)")
                for q in range(nb):
                    ins = nc.tensor.transpose(o_[:, q * P:(q + 1) * P], prob[i % 2][:, q * P:(q + 1) * P], ident)
                ins.then_inc(sem("probT_mm"), 1)

            def values(i):
                hs, qt = divmod(i, NT)
                pe.wait_ge(sem("probT_ready"), i + 1)
                if i >= 2:
                    pe.wait_ge(sem("head_out"), i - 1)
                nb = 3 * (qt + 1)
                for q in range(nb):
                    br, kt = divmod(q, qt + 1)
                    col = (br * SLOTS + hs) * HS
                    ins = mm(PS[:, 6 + i % 2, 0:HS], probT[i % 2][:, q * P:(q + 1) * P], vNa[:, kt, col:col + HS],
                             start=(q == 0), stop=(q == nb - 1))
                ins.then_inc(sem("values_mm"), 1)

            scores(0)
            for i in range(NI):
                if i + 1 < NI:
                    scores(i + 1)
                prob_transposes(i)
                if i >= 1:
                    values(i - 1)
            values(NI - 1)
            pe.wait_ge(sem("head_out"), NI)
            for n in range(NT):
                for c in range(4):
                    ins = nc.tensor.transpose(PS[:, c // 2, (c % 2) * S + n * P:(c % 2) * S + (n + 1) * P],
                                              oN[:, n, c * P:(c + 1) * P], ident)
            ins.then_inc(sem("oT_mm"), 1)
            pe.wait_ge(sem("oT_ready"), 2)
            for i in range(2):
                weights_here(pe, U_AWO + i)
            for n in range(NT):
                for h in range(2):
                    for k in range(4):
                        ins = mm(PS[:, 2 + 2 * h + n, :], oT[:, k, n * P:(n + 1) * P],
                                 unit_cols(U_AWO + k // 2, 2, D)[:, k % 2, h * 512:(h + 1) * 512],
                                 start=(k == 0), stop=(k == 3))
                    ins.then_inc(sem("x_mm"), 1)

            norm_transposes(3)
            pe.wait_ge(sem("normT_ready"), 20)
            pe.wait_ge(sem("router_loaded"), 32)
            for n in range(NT):
                for k in range(KC):
                    ins = mm(PS[:, 4, n * 8:n * 8 + 8], hTm[:, k, n * P:(n + 1) * P], router[:, k, :],
                             start=(k == 0), stop=(k == KC - 1))
            ins.then_inc(sem("logits_mm"), 1)
            pe.wait_ge(sem("chosen_ready"), 1)
            mm(PS[:, 5, 0:8], cst("earlier"), chosen[:, 0, :], start=True, stop=True)
            mm(PS[:, 5, 8:16], cst("earlier"), chosen[:, 1, :], start=True, stop=False)
            mm(PS[:, 5, 8:16], ones, chosen[:, 0, :], start=False, stop=True)
            mm(PS[:, 5, 16:24], ones, chosen[:, 0, :], start=True, stop=False)
            mm(PS[:, 5, 16:24], ones, chosen[:, 1, :], start=False, stop=True).then_inc(sem("ranks_mm"), 1)

            def gather(i, part):
                bank = 7 - part
                for k in range(4):
                    for n in range(NT):
                        ins = mm(PS[:, bank, k * P:(k + 1) * P], hN[:, n, (4 * part + k) * P:(4 * part + k + 1) * P],
                                 onehot[:, n, :], start=(n == 0), stop=(n == NT - 1))
                ins.then_inc(sem("gather_mm"), 1)

            def scatter_matrix():
                for n in range(NT):
                    ins = nc.tensor.transpose(PS[:, 7, n * P:(n + 1) * P], gated[:, n, :], ident)
                ins.then_inc(sem("scatT_mm"), 1)

            def experts(base):
                with pe.Fori(0, NE) as e:
                    i = e + base if base else e
                    pe.wait_ge(sem("gathered"), 2 * i + 2)

                    def up(j, which):
                        if which == 0:
                            if j >= 2:
                                pe.wait_ge(sem("hidden_ready"), ECH * i + (j - 1))
                            elif j == 1:
                                pe.wait_ge(sem("scatT_ready"), i + 1)
                        w = ("w1", "w3")[which]
                        for k in range(KC):
                            if k % 4 == 0:
                                moe_weights_here(pe, (w, j, k // 4), i)
                            ins = mm(PS[:, 2 * (j % 2) + which, :], hTe[:, k, :],
                                     unit_cols(moe_slot((w, j, k // 4)), 4, 512)[:, k % 4, :],
                                     start=(k == 0), stop=(k == KC - 1))
                        ins.then_inc(sem("up_mm"), 1)

                    def hidden_transposes(j):
                        pe.wait_ge(sem("hidden_ready"), ECH * i + (j + 1))
                        for q in range(4):
                            ins = nc.tensor.transpose(PS[:, 6, q * P:(q + 1) * P], hidE[:, q * P:(q + 1) * P], ident)
                        ins.then_inc(sem("hidT_mm"), 1)

                    def down(j):
                        pe.wait_ge(sem("hidT_ready"), ECH * i + (j + 1))
                        for q in range(4):
                            if q % 2 == 0:
                                moe_weights_here(pe, ("w2", j, q // 2), i)
                            for h in range(2):
                                ins = mm(PS[:, 4 + h, :], hidT[:, q, :],
                                         unit_cols(moe_slot(("w2", j, q // 2)), 2, D)[:, q % 2, h * 512:(h + 1) * 512],
                                         start=(j == 0 and q == 0), stop=(j == ECH - 1 and q == 3))
                        ins.then_inc(sem("down_mm"), 1)

                    for j in range(ECH):
                        up(j, 0)
                        if j:
                            hidden_transposes(j - 1)
                        up(j, 1)
                        if j:
                            down(j - 1)
                    hidden_transposes(ECH - 1)
                    pe.wait_ge(sem("onehot_ready"), i + 2)
                    pe.wait_ge(sem("scatT_ready"), i + 1)
                    gather(i, 0)
                    down(ECH - 1)
                    gather(i, 1)
                    pe.wait_ge(sem("y_ready"), i + 1)
                    for n in range(NT):
                        for h in range(2):
                            mm(PS[:, (4, 5, 2, 3)[2 * n + h], :], scatT[:, n * P:(n + 1) * P], ySB[:, h * 512:(h + 1) * 512],
                               start=True, stop=True).then_inc(sem("scatter_mm"), 1)
                    pe.wait_ge(sem("gathered"), 2 * i + 3)
                    scatter_matrix()

            pe.wait_ge(sem("onehot_ready"), 1)
            gather(0, 0)
            gather(0, 1)
            pe.wait_ge(sem("gathered"), 1)
            scatter_matrix()
            experts(0)
            pe.wait_ge(sem("overflow_known"), 1)
            more = pe.value_load(overflow[0:1, 0:1])
            with pe.If(more > 0):
                experts(NE)

        @block.scalar
        def _(act):
            own = Own(act, sem("act_step"))
            a_ = nc.scalar.activation

            def norm_stats(k):
                for n in range(NT):
                    ins = a_(SQ[n], x[:, n, :], ACT.Square, accum_out=ss[:, n:n + 1])
                ins.then_inc(sem("squares_summed"), 1)
                act.wait_ge(sem("mean_ready"), k + 1)
                a_(std, ss, ACT.Sqrt).then_inc(sem("root_ready"), 1)

            act.wait_ge(sem("x_loaded"), 16)
            norm_stats(0)

            act.wait_ge(sem("vectors_loaded"), 16)
            job = 0

            def take(dst, src, func=ACT.Copy, **kw):
                return a_(dst, src, func, **kw)

            for dst in (rT, kT):
                for f2 in range(4):
                    act.wait_ge(sem("proj_done"), job + 1)
                    take(flat(dst[:, 2 * f2:2 * f2 + 2, :]), PS[:, job % 4, :]).then_inc(sem("proj_evac"), 1)
                    job += 1
            for i, (rows, func) in enumerate(((64, ACT.Tanh), (64, ACT.Copy), (128, ACT.Sigmoid))):
                act.wait_ge(sem("proj_done"), job + 1)
                take(loraT[0:rows, i, :], PS[0:rows, job % 4, 0:S], func).then_inc(sem("proj_evac"), 1)
                job += 1
            for ch in range(2):
                for n in range(NT):
                    act.wait_ge(sem("proj_done"), job + 1)
                    take(vN[:, n, ch * 512:(ch + 1) * 512], PS[:, job % 4, :]).then_inc(sem("proj_evac"), 1)
                    job += 1
            for dst, bias in ((ldT, "w0"), (aT, "a0")):
                for f2 in range(4):
                    act.wait_ge(sem("proj_done"), job + 1)
                    for fi in range(2):
                        c = 2 * f2 + fi
                        ins = take(dst[:, c, :], PS[:, job % 4, fi * S:(fi + 1) * S], ACT.Sigmoid,
                                   bias=vec(bias)[:, c:c + 1])
                    ins.then_inc(sem("proj_evac"), 1)
                    job += 1

            for gp in range(2):
                gs = [(2 * gp + si, si, sets[si], 4 * si) for si in range(2)]
                for g, si, b, bank in gs:
                    act.wait_ge(sem("kk_ready"), g + 1)
                    a_(b.sc[1], b.sc[0], ACT.Square).then_inc(sem("kk_squared"), 1)
                for g, si, b, bank in gs:
                    act.wait_ge(sem("kk_norm_mm"), g + 1)
                    a_(b.sc[1], PS[:, bank, :], ACT.Sqrt).then_inc(sem("kk_root"), 1)
                for g, si, b, bank in gs:
                    act.wait_ge(sem("cum_ready"), g + 1)
                    a_(b.sc[5], b.sc[4], ACT.Exp).then_inc(sem("decays"), 1)
                    a_(b.sc[6], b.sc[4], ACT.Exp, scale=-1.0).then_inc(sem("decays"), 1)
                    a_(decayC[si], s8(b.sc[4])[:, :, CH - 1], ACT.Exp).then_inc(sem("decays"), 1)
                    act.wait_ge(sem("cum_before"), g + 1)
                    a_(b.sc[7], b.sc[7], ACT.Exp).then_inc(sem("decays"), 1)
                    act.wait_ge(sem("cum_after"), g + 1)
                    a_(b.sc[1], b.sc[1], ACT.Exp).then_inc(sem("decays"), 1)
                for g, si, b, bank in gs:
                    act.wait_ge(sem("bonus_mm"), g + 1)
                    a_(bonus[:, :, 4 * g:4 * g + 4], PS[:, bank + 1, 0:8].rearrange("p (n h) -> p n h", n=NT),
                       ACT.Copy).then_inc(sem("bonus_taken"), 1)
                for g, si, b, bank in gs:
                    act.wait_ge(sem("AR_ready"), g + 1)
                    for h in range(2):
                        a_(b.Abd[:, :, h, :], b.AR[:, :, 0, :], ACT.Copy, scale=half(h))
                        ins = a_(b.Rbd[:, :, h, :], b.AR[:, :, 1, :], ACT.Copy, scale=half(h))
                    ins.then_inc(sem("ARbd_ready"), 1)
                for g, si, b, bank in gs:
                    act.wait_ge(sem("tailsT_mm"), 2 * g + 1)
                    a_(b.BhN.rearrange("p m h t -> p (m h t)"), PS[:, bank + 2:bank + 4, :].rearrange("p b n -> p (b n)"),
                       ACT.Copy).then_inc(sem("tails_taken"), 1)
                    act.wait_ge(sem("tailsT_mm"), 2 * g + 2)
                    a_(b.KhN.rearrange("p m h t -> p (m h t)"), PS[:, bank:bank + 2, :].rearrange("p b n -> p (b n)"),
                       ACT.Copy).then_inc(sem("tails_taken"), 1)
                for lev in range(LEVELS):
                    for g, si, b, bank in gs:
                        q = gp * 2 * LEVELS + 2 * lev + si
                        act.wait_ge(sem("Z_ready"), q + 1)
                        for h in range(2):
                            ins = a_(b.Zbd[:, :, h, :], b.Z, ACT.Copy, scale=half(h))
                        ins.then_inc(sem("Zbd_ready"), 1)
                    for g, si, b, bank in gs:
                        q = gp * 2 * LEVELS + 2 * lev + si
                        act.wait_ge(sem("Y_ready"), q + 1)
                        if 0 < lev < LEVELS - 1:
                            act.wait_ge(sem("XZ_mm"), gp * 2 * (LEVELS - 2) + 2 * (lev - 1) + si + 1)
                        for h in range(2):
                            ins = a_(b.Ybd[:, :, h, :], b.Y, ACT.Copy, scale=half(h))
                        ins.then_inc(sem("Ybd_ready"), 1)
                for j in range(NCH):
                    for g, si, b, bank in gs:
                        act.wait_ge(sem("U0_mm"), gp * 2 * NCH + 2 * j + si + 1)
                        a_(b.U0.rearrange("p c v -> p (c v)"), PS[:, bank + 3, 0:128], ACT.Copy).then_inc(sem("U0_ready"), 1)
                    for g, si, b, bank in gs:
                        act.wait_ge(sem("U_mm"), gp * 2 * NCH + 2 * j + si + 1)
                        a_(b.U.rearrange("p c v -> p (c v)"), PS[:, bank + 3, 128:256], ACT.Copy).then_inc(sem("U_ready"), 1)
                    for g, si, b, bank in gs:
                        act.wait_ge(sem("y_mm"), gp * 2 * NCH + 2 * j + si + 1)
                        a_(yC[:, 2 * g:2 * g + 2, j, :], PS[:, bank + 2, 0:128].rearrange("p (c v) -> p c v", c=2),
                           ACT.Copy).then_inc(sem("y_taken"), 1)
                for g, si, b, bank in gs:
                    act.wait_ge(sem("gn_var"), g + 1)
                    a_(gns[si], gns[si], ACT.Sqrt).then_inc(sem("gn_root"), 1)

            act.wait_ge(sem("zT_mm"), 1)
            for b2 in range(4):
                a_(flat(zT[:, 2 * b2:2 * b2 + 2, :]), PS[:, 4 + b2, :], ACT.Copy).then_inc(sem("zT_ready"), 1)

            act.wait_ge(sem("x_added"), 4)
            norm_stats(1)
            for f in range(FT):
                act.wait_ge(sem("ffn_up_mm"), 2 * f + 2)
                if f >= 4:
                    act.wait_ge(sem("ffn_hidden"), f - 3)
                a_(silu_sb[:, f % 4, :], PS[:, f % 4, 0:S], ACT.Silu).then_inc(sem("ffn_silu"), 1)

            act.wait_ge(sem("x_added"), 8)
            norm_stats(2)
            job = 0
            for f2 in range(QT_N // 2):
                act.wait_ge(sem("att_proj_done"), job + 1)
                a_(flat(kTa[:, 2 * f2:2 * f2 + 2, :]), PS[:, job % 4, :], ACT.Copy).then_inc(sem("att_proj_evac"), 1)
                job += 1
            for ch in range(3):
                for n in range(NT):
                    act.wait_ge(sem("att_proj_done"), job + 1)
                    a_(vNa[:, n, ch * 512:(ch + 1) * 512], PS[:, job % 4, :], ACT.Copy).then_inc(sem("att_proj_evac"), 1)
                    job += 1
            for f2 in range(QT_N // 2):
                act.wait_ge(sem("att_proj_done"), job + 1)
                for h in range(2):
                    ins = a_(qTa[:, 2 * f2:2 * f2 + 2, h, :], PS[:, job % 4, :].rearrange("p (f t) -> p f t", f=2),
                             ACT.Copy, scale=half8(h))
                ins.then_inc(sem("att_proj_evac"), 1)
                job += 1

            def softmax_exp(i):
                n = 3 * P * (i % 2 + 1)
                act.wait_ge(sem("max_ready"), i + 1)
                a_(prob[i % 2][:, 0:n], prob[i % 2][:, 0:n], ACT.Exp, bias=negmax[:, i % 2:i % 2 + 1],
                   accum_out=denom[:, i % 2:i % 2 + 1]).then_inc(sem("prob_ready"), 1)

            NI = NT * SLOTS
            for i in range(NI):
                softmax_exp(i)
                n = 3 * P * (i % 2 + 1)
                act.wait_ge(sem("probT_mm"), i + 1)
                if i >= 2:
                    act.wait_ge(sem("values_mm"), i - 1)
                a_(probT[i % 2][:, 0:n], PS[:, 4:6, :].rearrange("p b n -> p (b n)")[:, 0:n],
                   ACT.Copy).then_inc(sem("probT_ready"), 1)
            act.wait_ge(sem("oT_mm"), 1)
            for b2 in range(2):
                a_(flat(oT[:, 2 * b2:2 * b2 + 2, :]), PS[:, b2, :], ACT.Copy).then_inc(sem("oT_ready"), 1)

            act.wait_ge(sem("x_added"), 12)
            norm_stats(3)
            act.wait_ge(sem("topneg_ready"), 1)
            for n in range(NT):
                ins = a_(expl[:, n, :], logits[:, n, :], ACT.Exp, bias=top[:, n:n + 1])
            ins.then_inc(sem("expl_ready"), 1)

            def experts(base):
                with act.Fori(0, NE) as e:
                    i = e + base if base else e
                    for j in range(ECH):
                        act.wait_ge(sem("up_mm"), 2 * ECH * i + (2 * j + 1))
                        if j:
                            act.wait_ge(sem("hidden_ready"), ECH * i + j)
                        a_(siluE, PS[:, 2 * (j % 2), :], ACT.Silu).then_inc(sem("silu_ready"), 1)
                        if j:
                            act.wait_ge(sem("hidT_mm"), ECH * i + j)
                            if j > 1:
                                act.wait_ge(sem("down_mm"), ECH * i + (j - 1))
                            a_(hidT.rearrange("p f n -> p (f n)"), PS[:, 6, :], ACT.Copy).then_inc(sem("hidT_ready"), 1)
                    act.wait_ge(sem("hidT_mm"), ECH * i + ECH)
                    act.wait_ge(sem("down_mm"), ECH * i + (ECH - 1))
                    a_(hidT.rearrange("p f n -> p (f n)"), PS[:, 6, :], ACT.Copy).then_inc(sem("hidT_ready"), 1)
                    act.wait_ge(sem("down_mm"), ECH * i + ECH)
                    a_(ySB, PS[:, 4:6, :].rearrange("p b n -> p (b n)"), ACT.Copy).then_inc(sem("y_ready"), 1)

            experts(0)
            act.wait_ge(sem("overflow_known"), 1)
            more = act.value_load(overflow[0:1, 0:1])
            with act.If(more > 0):
                experts(NE)
            act.wait_ge(sem("experts_over"), 1)
            norm_stats(4)

        @block.vector
        def _(dve):
            v = nc.vector
            own = Own(dve, sem("dve_step"))
            do = own.do

            def norm_scale(k, dst):
                dve.wait_ge(sem("squares_summed"), k + 1)
                do(v.tensor_scalar(ss, ss, 1.0 / D, RMS_EPS, ALU.mult, ALU.add), sem("mean_ready"))
                dve.wait_ge(sem("root_ready"), k + 1)
                do(v.reciprocal(rstd, std))
                for n in range(NT):
                    ins = v.tensor_scalar(dst[:, n, :], x[:, n, :], rstd[:, n:n + 1], None, ALU.mult)
                return ins

            def norm_take(k, targets):
                for b in range(4):
                    dve.wait_ge(sem("norm_transposed"), 4 * k + b + 1)
                    for t, (dst, gain) in enumerate(targets):
                        do(v.tensor_tensor(dst[:, 2 * b:2 * b + 2, :], PS[:, b, :].rearrange("p (c t) -> p c t", c=2),
                                           last(vec(gain)[:, 2 * b:2 * b + 2], S), ALU.mult), sem("normT_ready"))

            do(v.memset(hT[:, :, 0:1], 0.0))
            norm_scale(0, NORM_XN[0]).then_inc(sem("norm_scaled"), 1)
            dve.wait_ge(sem("vectors_loaded"), 16)
            norm_take(0, [(hT[:, :, 1:S + 1], "g00")])
            do(v.tensor_tensor(dxT, hT[:, :, 0:S], hT[:, :, 1:S + 1], ALU.subtract))
            for i, mu in enumerate((0, 2, 1, 4, 5, 3)):
                if i >= 2:
                    dve.wait_ge(sem("proj_done"), (4, 8, 9, 10)[i - 2])
                for c in range(KC):
                    ins = v.scalar_tensor_tensor(out=lerp[i % 2][:, c, :], in0=dxT[:, c, :],
                                                 scalar=vec(f"mu{mu}")[:, c:c + 1], in1=hT[:, c, 1:S + 1],
                                                 op0=ALU.mult, op1=ALU.add)
                ins.then_inc(sem("lerp_ready"), 1)
            do(v.tensor_scalar(one_minus_ka, vec("k_a"), -1.0, 1.0, ALU.mult, ALU.add))
            dve.wait_ge(sem("proj_done"), 23)
            dve.wait_ge(sem("proj_evac"), 23)
            stt = v.scalar_tensor_tensor
            for gp in range(2):
                gs = [(2 * gp + si, si, sets[si], 4 * si) for si in range(2)]
                for g, si, b, bank in gs:
                    G = slice(2 * g, 2 * g + 2)
                    if gp:
                        dve.wait_ge(sem("y_mm"), 2 * NCH * gp)
                    two = lambda w: w.rearrange("p (c t) -> p c t", c=2)
                    do(v.tensor_tensor(two(b.sc[0]), kT[:, G, :], last(vec("k_k")[:, G], S), ALU.mult), sem("kk_ready"))
                    for c in range(2):
                        ins = v.tensor_scalar(b.sc[3][:, c * S:(c + 1) * S], aT[:, 2 * g + c, :],
                                              vec("k_a")[:, 2 * g + c:2 * g + c + 1],
                                              one_minus_ka[:, 2 * g + c:2 * g + c + 1], ALU.mult, ALU.add)
                    do(ins)
                    do(v.tensor_tensor(flat(kT[:, G, :]), flat(kT[:, G, :]), b.sc[3], ALU.mult))
                    do(v.tensor_tensor(b.sc[3], flat(rT[:, G, :]), flat(kT[:, G, :]), ALU.mult))
                    do(v.tensor_tensor(two(b.sc[3]), two(b.sc[3]), last(vec("r_k")[:, G], S), ALU.mult), sem("rk_ready"))
                    do(v.tensor_scalar(flat(ldT[:, G, :]), flat(ldT[:, G, :]), DECAY, None, ALU.mult))
                    do(v.tensor_tensor_scan(b.sc[4], cst("carry"), flat(ldT[:, G, :]), 0.0, ALU.mult, ALU.add), sem("cum_ready"))
                    do(v.tensor_tensor(b.sc[7], b.sc[4], flat(ldT[:, G, :]), ALU.subtract), sem("cum_before"))
                for g, si, b, bank in gs:
                    G = slice(2 * g, 2 * g + 2)
                    dve.wait_ge(sem("kk_root"), g + 1)
                    do(v.tensor_scalar(b.sc[1], b.sc[1], 1e-12, None, ALU.max))
                    do(v.reciprocal(b.sc[1], b.sc[1]))
                    do(v.tensor_tensor(b.sc[0], b.sc[0], b.sc[1], ALU.mult))
                    do(v.tensor_tensor(b.sc[2], b.sc[0], flat(aT[:, G, :]), ALU.mult))
                    do(v.tensor_tensor(s8(b.sc[1]), last(s8(b.sc[4])[:, :, CH - 1], CH), s8(b.sc[4]), ALU.subtract),
                       sem("cum_after"))
                for g, si, b, bank in gs:
                    G = slice(2 * g, 2 * g + 2)
                    dve.wait_ge(sem("decays"), 5 * g + 4)
                    stt(out=b.AR[:, :, 0, :], in0=s8(b.sc[0]), scalar=-1.0, in1=s8(b.sc[7]), op0=ALU.mult, op1=ALU.mult)
                    v.tensor_tensor(b.AR[:, :, 1, :], c8(rT[:, G, :]), s8(b.sc[5]), ALU.mult).then_inc(sem("AR_ready"), 1)
                    for h in range(2):
                        stt(out=b.Bbd[:, :, h, :], in0=s8(b.sc[2]), scalar=half(h), in1=s8(b.sc[6]), op0=ALU.mult, op1=ALU.mult)
                        ins = stt(out=b.Kbd[:, :, h, :], in0=c8(kT[:, G, :]), scalar=half(h), in1=s8(b.sc[6]),
                                  op0=ALU.mult, op1=ALU.mult)
                    ins.then_inc(sem("grams_in"), 1)
                    dve.wait_ge(sem("decays"), 5 * g + 5)
                    for h in range(2):
                        stt(out=b.BhT[:, :, h, :], in0=s8(b.sc[2]), scalar=half(h), in1=s8(b.sc[1]), op0=ALU.mult, op1=ALU.mult)
                        ins = stt(out=b.KhT[:, :, h, :], in0=c8(kT[:, G, :]), scalar=half(h), in1=s8(b.sc[1]),
                                  op0=ALU.mult, op1=ALU.mult)
                    ins.then_inc(sem("tails_ready"), 1)
                    do(v.memset(b.S, 0.0), sem("state_ready"))
                for g, si, b, bank in gs:
                    dve.wait_ge(sem("grams_mm"), 2 * g + 2)
                    dve.wait_ge(sem("bonus_taken"), g + 1)
                    for src, m1, m2 in ((bank + 2, b.N, b.Mb), (bank, b.Lk, b.Mk)):
                        pv = PS[:, src:src + 2, :].rearrange("p b (m q t) -> p (b m) q t", m=4, q=2)
                        for h in range(2):
                            stt(out=m1[:, :, h, :], in0=pv[:, :, 0, :], scalar=half(h), in1=mid(cst("before"), 8),
                                op0=ALU.mult, op1=ALU.mult)
                            ins = stt(out=m2[:, :, h, :], in0=pv[:, :, 1, :], scalar=half(h), in1=mid(cst("upto"), 8),
                                      op0=ALU.mult, op1=ALU.mult)
                    ins.then_inc(sem("grams_taken"), 1)
                for lev in range(LEVELS):
                    for g, si, b, bank in gs:
                        q = gp * 2 * LEVELS + 2 * lev + si
                        dve.wait_ge(sem("LX_mm"), q + 1)
                        if lev:
                            dve.wait_ge(sem("Zbd_ready"), q - 1)
                        do(v.tensor_tensor(b.Z, PS[:, bank, :].rearrange("p (m t) -> p m t", m=8),
                                           mid(cst(f"level{lev}"), 8), ALU.mult), sem("Z_ready"))
                    for g, si, b, bank in gs:
                        q = gp * 2 * LEVELS + 2 * lev + si
                        if lev == 0:
                            do(v.tensor_tensor(b.X, b.Z, mid(cst("eye64"), 8), ALU.add), sem("X_ready"))
                        elif lev < LEVELS - 1:
                            dve.wait_ge(sem("XZ_mm"), gp * 2 * (LEVELS - 2) + 2 * (lev - 1) + si + 1)
                            do(v.tensor_tensor(b.X, b.X, PS[:, bank + 1, :].rearrange("p (m t) -> p m t", m=8), ALU.add),
                               sem("X_ready"))
                    for g, si, b, bank in gs:
                        q = gp * 2 * LEVELS + 2 * lev + si
                        dve.wait_ge(sem("ZY_mm"), q + 1)
                        if lev:
                            dve.wait_ge(sem("Ybd_ready"), q - 1)
                        base = mid(cst("eye64"), 8) if lev == 0 else b.Y
                        do(v.tensor_tensor(b.Y, base, PS[:, bank + 2, :].rearrange("p (m t) -> p m t", m=8), ALU.add),
                           sem("Y_ready"))
                for j in range(NCH):
                    for g, si, b, bank in gs:
                        dve.wait_ge(sem("S_mm"), gp * 2 * NCH + 2 * j + si + 1)
                        dve.wait_ge(sem("y_mm"), gp * 2 * NCH + 2 * j + si + 1)
                        for c in range(2):
                            ins = stt(out=b.S[:, c, :], in0=b.S[:, c, :], scalar=decayC[si][:, 4 * c + j:4 * c + j + 1],
                                      in1=PS[:, bank + 3, 384 + c * 64:384 + (c + 1) * 64], op0=ALU.mult, op1=ALU.add)
                        do(ins, sem("state_ready"))
                for g, si, b, bank in gs:
                    dve.wait_ge(sem("y_taken"), gp * 2 * NCH + 2 * (NCH - 1) + si + 1)
                    yg = yC[:, 2 * g:2 * g + 2, :, :].rearrange("p c j v -> p (c j) v")
                    do(v.tensor_reduce(gnm[si], yg, X, ALU.add))
                    do(v.tensor_scalar(gnm[si], gnm[si], 1.0 / HS, None, ALU.mult))
                    do(v.tensor_tensor(yg, yg, last(gnm[si], HS), ALU.subtract))
                    do(v.tensor_tensor(b.Z, yg, yg, ALU.mult))
                    do(v.tensor_reduce(gns[si], b.Z, X, ALU.add))
                    do(v.tensor_scalar(gns[si], gns[si], 1.0 / HS, GN_EPS, ALU.mult, ALU.add), sem("gn_var"))
                    dve.wait_ge(sem("gn_root"), g + 1)
                    do(v.reciprocal(gns[si], gns[si]))
                    do(v.tensor_tensor(yg, yg, last(gns[si], HS), ALU.mult), sem("y_normed"))
            do(v.engine_nop() if False else v.tensor_copy(negmax[:, 0:1], gnm[0][:, 0:1]), sem("scan_over"))

            dve.wait_ge(sem("y_natural"), 16 * 8)
            dve.wait_ge(sem("lnx_loaded"), 16)
            for n in range(NT):
                do(v.tensor_tensor(yN[:, n, :], yN[:, n, :], lnx[:, 0, :], ALU.mult))
                v3 = vN[:, n, :].rearrange("p (h v) -> p h v", v=HS)
                do(v.tensor_tensor(v3, v3, last(bonus[:, n, :], HS), ALU.mult))
                do(v.tensor_tensor(yN[:, n, :], yN[:, n, :], lnx[:, 1, :], ALU.add))
                do(v.tensor_tensor(yN[:, n, :], yN[:, n, :], vN[:, n, :], ALU.add))
                for ch in range(2):
                    dve.wait_ge(sem("gate_mm"), 2 * n + ch + 1)
                    cs = slice(ch * 512, (ch + 1) * 512)
                    do(v.tensor_tensor(yN[:, n, cs], yN[:, n, cs], PS[:, 2 * n + ch, :], ALU.mult), sem("z_ready"))

            added = [0]

            def add_to_x(banks):
                for q, bank in enumerate(banks):
                    h, n = divmod(q, NT)
                    dve.wait_ge(sem("x_mm"), added[0] + (q + 1))
                    ins = v.tensor_tensor(x[:, n, h * 512:(h + 1) * 512], x[:, n, h * 512:(h + 1) * 512], PS[:, bank, :], ALU.add)
                    do(ins, sem("x_added"))
                added[0] += 4

            add_to_x((0, 1, 2, 3))
            norm_scale(1, NORM_XN[1]).then_inc(sem("norm_scaled"), 1)
            norm_take(1, [(ffn_in, "g01")])
            for f in range(FT):
                dve.wait_ge(sem("ffn_silu"), f + 1)
                dve.wait_ge(sem("ffn_up_mm"), 2 * f + 2)
                v.tensor_tensor(actT[:, f, :], silu_sb[:, f % 4, :], PS[:, f % 4, S:2 * S], ALU.mult).then_inc(sem("ffn_hidden"), 1)
            dve.wait_ge(sem("x_mm"), 8)
            add_to_x((4, 5, 6, 7))
            norm_scale(2, NORM_XN[2]).then_inc(sem("norm_scaled"), 1)
            norm_take(2, [(kvT, "kvg"), (qinT, "g10")])
            sl = slopes()
            NI = NT * SLOTS

            def head_out(i):
                hs, qt = divmod(i, NT)
                dve.wait_ge(sem("prob_ready"), i + 1)
                do(v.reciprocal(rden[:, i % 2:i % 2 + 1], denom[:, i % 2:i % 2 + 1]))
                dve.wait_ge(sem("values_mm"), i + 1)
                v.tensor_scalar(oN[:, qt, hs * HS:(hs + 1) * HS], PS[:, 6 + i % 2, 0:HS], rden[:, i % 2:i % 2 + 1], None,
                                ALU.mult).then_inc(sem("head_out"), 1)

            dve.wait_ge(sem("dist_loaded"), 16)
            for i in range(NI):
                hs, qt = divmod(i, NT)
                nk = (qt + 1) * P
                dve.wait_ge(sem("scores_mm"), i + 1)
                if i >= 2:
                    dve.wait_ge(sem("probT_mm"), i - 1)
                sc = PS[:, 2 * (i % 2):2 * (i % 2) + 2, :].rearrange("p b n -> p (b n)")
                for br in range(3):
                    d0 = (3 * P if qt else 0) + br * nk
                    ins = stt(out=prob[i % 2][:, br * nk:(br + 1) * nk], in0=dist[:, d0:d0 + nk], scalar=float(sl[br, hs]),
                              in1=sc[:, br * nk:(br + 1) * nk], op0=ALU.mult, op1=ALU.add)
                do(ins, sem("scores_taken"))
                do(v.tensor_reduce(negmax[:, i % 2:i % 2 + 1], prob[i % 2][:, 0:3 * nk], X, ALU.max, negate=True), sem("max_ready"))
                if i >= 1:
                    head_out(i - 1)
            head_out(NI - 1)
            dve.wait_ge(sem("x_mm"), 12)
            for q, (n, h) in enumerate(((0, 0), (0, 1), (1, 0), (1, 1))):
                do(v.tensor_tensor(x[:, n, h * 512:(h + 1) * 512], x[:, n, h * 512:(h + 1) * 512], PS[:, 2 + 2 * h + n, :],
                                   ALU.add), sem("x_added"))
            norm_scale(3, hN).then_inc(sem("norm_scaled"), 1)
            norm_take(3, [(hTm, "g11")])
            dve.wait_ge(sem("router_loaded"), 32)
            dve.wait_ge(sem("logits_mm"), 1)
            for n in range(NT):
                l = logits[:, n, :]
                do(v.tensor_tensor(l, PS[:, 4, n * 8:n * 8 + 8], router_bias, ALU.add))
                ins = v.tensor_reduce(top[:, n:n + 1], l, X, ALU.max, negate=True)
            do(ins, sem("topneg_ready"))
            for n in range(NT):
                l = logits[:, n, :]
                do(v.tensor_tensor(beats, mid(l, NE), last(l, NE), ALU.is_gt))
                do(v.tensor_tensor(ties, mid(l, NE), last(l, NE), ALU.is_equal))
                do(v.tensor_tensor(ties, ties, cst("tie").rearrange("p (e j) -> p e j", e=NE), ALU.mult))
                do(v.tensor_tensor(beats, beats, ties, ALU.add))
                do(v.tensor_reduce(nrank, beats, X, ALU.add))
                ins = v.tensor_scalar(chosen[:, n, :], nrank, 2.0, None, ALU.is_lt)
            do(ins, sem("chosen_ready"))
            dve.wait_ge(sem("expl_ready"), 1)
            do(v.memset(gates, 0.0))
            for n in range(NT):
                do(v.tensor_tensor(expl[:, n, :], expl[:, n, :], chosen[:, n, :], ALU.mult))
                do(v.tensor_reduce(top[:, 2 + n:3 + n], expl[:, n, :], X, ALU.add))
                do(v.reciprocal(top[:, 4 + n:5 + n], top[:, 2 + n:3 + n]))
                for r in range(2):
                    do(v.tensor_scalar(gates[:, n, r * NE:(r + 1) * NE], expl[:, n, :], top[:, 4 + n:5 + n], None, ALU.mult))
            dve.wait_ge(sem("ranks_mm"), 1)
            do(v.memset(slotof, -1.0))
            for n in range(NT):
                do(v.tensor_tensor(nrank, PS[:, 5, 8 * n:8 * n + 8], chosen[:, n, :], ALU.mult))
                do(v.tensor_scalar(expl[:, n, :], chosen[:, n, :], 1000.0, -1000.0, ALU.mult, ALU.add))
                do(v.tensor_tensor(slotof[:, n, 0:NE], nrank, expl[:, n, :], ALU.add))
                do(v.tensor_scalar(slotof[:, n, NE:2 * NE], slotof[:, n, 0:NE], -float(P), None, ALU.add))
            do(v.tensor_reduce(top[:, 6:7], PS[:, 5, 16:24], X, ALU.max))
            do(v.tensor_scalar(overflow[:], top[:, 6:7], float(P), None, ALU.is_gt), sem("overflow_known"))

            def one_hot(i):
                for n in range(NT):
                    v.tensor_scalar(onehot[:, n, :], cst("slotid"), slotof[:, n, bass.ds(i, 1)], None, ALU.is_equal)
                    ins = v.tensor_scalar(gated[:, n, :], cst("slotid"), slotof[:, n, bass.ds(i, 1)],
                                          gates[:, n, bass.ds(i, 1)], ALU.is_equal, ALU.mult)
                ins.then_inc(sem("onehot_ready"), 1)

            def take_gathered(i, part):
                dve.wait_ge(sem("gather_mm"), 2 * i + (part + 1))
                v.tensor_tensor(hTe[:, 4 * part:4 * part + 4, :], PS[:, 7 - part, :].rearrange("p (k n) -> p k n", k=4),
                                last(vec("g11")[:, 4 * part:4 * part + 4], P), ALU.mult).then_inc(sem("gathered"), 1)

            def take_scatter_matrix(i):
                dve.wait_ge(sem("scatT_mm"), i + 1)
                v.tensor_copy(scatT, PS[:, 7, 0:2 * P]).then_inc(sem("scatT_ready"), 1)

            one_hot(0)
            take_gathered(0, 0)
            take_gathered(0, 1)
            take_scatter_matrix(0)

            def experts(base):
                with dve.Fori(0, NE) as e:
                    i = e + base if base else e
                    for j in range(ECH):
                        if j == 2:
                            one_hot(i + 1)
                        dve.wait_ge(sem("silu_ready"), ECH * i + (j + 1))
                        dve.wait_ge(sem("up_mm"), 2 * ECH * i + (2 * j + 2))
                        if j:
                            dve.wait_ge(sem("hidT_mm"), ECH * i + j)
                        v.tensor_tensor(hidE, siluE, PS[:, 2 * (j % 2) + 1, :], ALU.mult).then_inc(sem("hidden_ready"), 1)
                    take_gathered(i + 1, 0)
                    take_gathered(i + 1, 1)
                    for n in range(NT):
                        for h in range(2):
                            q = 2 * n + h
                            dve.wait_ge(sem("scatter_mm"), 4 * i + (q + 1))
                            xs = x[:, n, h * 512:(h + 1) * 512]
                            v.tensor_tensor(xs, xs, PS[:, (4, 5, 2, 3)[q], :], ALU.add).then_inc(sem("scattered"), 1)
                    take_scatter_matrix(i + 1)
                    dve.wait_ge(sem("scattered"), 4 * i + 4)
                    dve.wait_ge(sem("scatT_ready"), i + 2)

            experts(0)
            dve.wait_ge(sem("overflow_known"), 1)
            more = dve.value_load(overflow[0:1, 0:1])
            with dve.If(more > 0):
                experts(NE)
            do(v.memset(ss, 0.0), sem("experts_over"))
            norm_scale(4, out_sb)
            do(v.memset(top[:, 7:8], 0.0))
            dve.wait_ge(sem("final_gain_loaded"), 16)
            for n in range(NT):
                v.tensor_tensor(out_sb[:, n, :], out_sb[:, n, :], final_gain, ALU.mult).then_inc(sem("out_ready"), 1)


_DIRECT = ["x", "rwkv_wr", "rwkv_wk", "rwkv_wv", "rwkv_w1", "rwkv_w2", "rwkv_a1", "rwkv_a2", "rwkv_g1", "rwkv_g2",
           "rwkv_wo", "w_kv", "attn_wq", "attn_wo", "ffn_w1", "ffn_w3", "ffn_w2", "moe_router", "moe_w1", "moe_w3", "moe_w2"]


def kernel(**inputs):
    import concourse.bacc as bacc
    from concourse.bass_utils import run_bass_kernel_spmd

    a = {k: np.ascontiguousarray(v) for k, v in inputs.items()}
    arrays = {n: a[n] for n in _DIRECT}
    named = {"g00": a["norm_gain"][0, 0], "g01": a["norm_gain"][0, 1], "g10": a["norm_gain"][1, 0],
             "g11": a["norm_gain"][1, 1], "kvg": a["kv_norm_gain"], "w0": a["rwkv_w0"][0], "a0": a["rwkv_a0"][0],
             "k_k": a["rwkv_k_k"][0], "k_a": a["rwkv_k_a"][0], "r_k": a["rwkv_r_k"][0].reshape(D)}
    for m in range(6):
        named[f"mu{m}"] = a["rwkv_mu"][0, m]
    arrays["vectors"] = np.ascontiguousarray(np.concatenate([named[n].reshape(KC, P).T for n in VECS], axis=1))
    arrays["lnx_rows"] = np.ascontiguousarray(
        np.broadcast_to(np.concatenate([a["rwkv_lnx_w"][0], a["rwkv_lnx_b"][0]]), (P, 2 * D)))
    arrays["final_gain_rows"] = np.ascontiguousarray(np.broadcast_to(a["final_norm_gain"], (P, D)))
    arrays["router_bias_rows"] = np.ascontiguousarray(np.broadcast_to(a["moe_router_bias"][0], (P, NE)))
    arrays["const_tables"] = np.ascontiguousarray(np.concatenate(list(constant_tables().values()), axis=1))
    arrays["distance_tables"] = distance_tables()

    nc = bacc.Bacc("TRN2", target_bir_lowering=False, num_devices=1)
    aps = {n: nc.dram_tensor(f"in_{n}", v.shape, mybir.dt.from_np(v.dtype), kind="ExternalInput").ap()
           for n, v in arrays.items()}
    out = nc.dram_tensor("out_x", (1, S, D), F32, kind="ExternalOutput").ap()
    trunk(nc, aps, out)
    r = run_bass_kernel_spmd(nc, [{f"in_{n}": v for n, v in arrays.items()}], core_ids=[0])
    return r.results[0]["out_x"]
```

```python
import math
from contextlib import ExitStack

import numpy as np

import concourse.bass as bass
from concourse import mybir

F32 = mybir.dt.float32
F32R = mybir.dt.float32r
I32 = mybir.dt.int32
ALU = mybir.AluOpType
ACT = mybir.ActivationFunctionType
X = mybir.AxisListType.X

P = 128
D = 1024
S = 256
NT = S // P
KC = D // P
HS = 64
CH = 64
NCH = S // CH
GROUPS = 4
LEVELS = 6
FF = 2816
FT = FF // P
FE = 3584
NE = 8
ECH = FE // 512
QD = 1536
QT_N = QD // P
SLOTS = 8
RING = 7
PAIRS = 3
UNIT = 2048
RMS_EPS = 1e-5
GN_EPS = 64e-5
BIG = -3.0e30
DECAY = -math.exp(-0.5)

VECS = ["g00", "g01", "g10", "g11", "kvg", "mu0", "mu1", "mu2", "mu3", "mu4", "mu5",
        "w0", "a0", "k_k", "k_a", "r_k", "lnw", "lnb"]
VCOL = {n: 8 * i for i, n in enumerate(VECS)}


def constant_tables():
    p = np.arange(P)
    s = p % CH
    t = np.arange(CH)
    tabs = {}
    tabs["ident"] = np.eye(P)
    tabs["ones"] = np.ones((P, P))
    tabs["headones"] = (p[:, None] // HS == p[None, :] // HS)
    tabs["before"] = s[:, None] < t[None, :]
    tabs["upto"] = s[:, None] <= t[None, :]
    for lev in range(LEVELS):
        m = 1 << lev
        tabs[f"level{lev}"] = ((p[:, None] // (2 * m) == p[None, :] // (2 * m))
                               & (p[:, None] // m % 2 == 1) & (p[None, :] // m % 2 == 0))
    tabs["eye64x2"] = s[:, None] == s[None, :]
    half = np.stack([p < HS, p >= HS], 1).astype(np.float64)
    tabs["half"] = half
    tabs["minushalf"] = -half
    tabs["half8"] = half * HS ** -0.5
    tabs["earlier"] = p[:, None] < p[None, :]
    tabs["slotid"] = np.tile(p[None, :], (P, 1))
    e = np.arange(NE)
    tabs["tie"] = np.tile((e[None, :] < e[:, None]).reshape(1, -1), (P, 1))
    tabs["carry"] = np.tile((np.arange(512) % CH != 0)[None, :], (P, 1))
    return {k: v.astype(np.float32) for k, v in tabs.items()}


def distance_tables():
    out = []
    for qt in range(NT):
        q = qt * P + np.arange(P)[:, None]
        k = np.arange(P * (qt + 1))[None, :]
        dist = q - k
        for window, dil in ((128, 1), (512, 4), (2048, 16)):
            seen = (dist >= 0) & (dist % dil == 0) & (dist <= window)
            out.append(np.where(seen, -dist, BIG))
    return np.concatenate(out, 1).astype(np.float32)


def slopes():
    n = 3 * SLOTS
    return np.exp2(-8.0 * (np.arange(n, dtype=np.float32) + 1.0) / n).reshape(3, SLOTS)


CONST_SHAPES = {k: v.shape[1] for k, v in constant_tables().items()}
CCOL = {}
_at = 0
for _k, _n in CONST_SHAPES.items():
    CCOL[_k] = _at
    _at += _n
NCONST = _at
NDIST = 3 * P + 3 * 2 * P


class Own:

    def __init__(self, eng, sem):
        self.eng, self.sem, self.count = eng, sem, {}
        self.base = {}

    def do(self, ins, sem=None):
        key = sem if sem is not None else self.sem
        name = str(key)
        self.count[name] = self.count.get(name, 0) + 1
        ins.then_inc(key, 1)
        self.eng.wait_ge(key, self.base.get(name, 0) + self.count[name])

    def at(self, sem=None):
        return self.count.get(str(sem if sem is not None else self.sem), 0)


def trunk(nc, A, out):
    ctx = ExitStack()
    with ctx:
        def sb(name, shape, dt=F32):
            return ctx.enter_context(nc.sbuf_tensor(name, shape, dt))

        def sb_at(name, n):
            base = -(-nc.sbuf_base // 32) * 32
            t = sb(name, [P, n])
            return t, base

        def rounded(name, at, n):
            return nc.alloc_sbuf_tensor_at(name, [P, n], F32R, offset=at)

        sems = {}

        def sem(name):
            if name not in sems:
                sems[name] = ctx.enter_context(nc.semaphore(name))
            return sems[name]

        C = sb("consts", [P, NCONST])
        V = sb("vectors", [P, 8 * len(VECS)])
        x = sb("x_residual", [P, NT, D])
        SPLIT_AT = RING * UNIT
        EXTRA_AT = SPLIT_AT + 2 * PAIRS * UNIT
        BIG_N = EXTRA_AT + 5120
        BIGB, big_base = sb_at("ring_and_scan", BIG_N)
        PERS, pers_base = sb_at("phase_buffers", 8 * 2048 + 32)
        small = sb("small", [P, 256])
        PS = ctx.enter_context(nc.psum_tensor("psum", [P, 8, 512], F32))

        def cst(name):
            return C[:, CCOL[name]:CCOL[name] + CONST_SHAPES[name]]

        def vec(name):
            return V[:, VCOL[name]:VCOL[name] + 8]

        ident, ones = cst("ident"), cst("ones")

        def half(p):
            return C[:, CCOL["half"] + p:CCOL["half"] + p + 1]

        def minushalf(p):
            return C[:, CCOL["minushalf"] + p:CCOL["minushalf"] + p + 1]

        def half8(p):
            return C[:, CCOL["half8"] + p:CCOL["half8"] + p + 1]

        def pers(at, n):
            return PERS[:, at:at + n]

        HT_, L0_, L1_, R_, K_, A_, LD_, VN_ = [0] + [2080 + 2048 * i for i in range(7)]
        extra = BIGB[:, EXTRA_AT:BIG_N]

        gateT = sb("gateT", [P, S])
        loraT = [extra[:, 2048:2048 + S], extra[:, 2048 + S:2048 + 2 * S], gateT[:]]
        hT = pers(HT_, 8 * 257).rearrange("p (c t) -> p c t", c=8)
        lerp = [pers(o, 2048).rearrange("p (c t) -> p c t", c=8) for o in (L0_, L1_)]
        dxT = extra[:, 0:2048].rearrange("p (c t) -> p c t", c=8)
        rT, kT, aT, ldT = [pers(o, 2048).rearrange("p (c t) -> p c t", c=8) for o in (R_, K_, A_, LD_)]
        vT = pers(VN_, 2048).rearrange("p (c t) -> p c t", c=8)
        gate_w = pers(L1_, D)

        def nat(at):
            return pers(at, 2048).rearrange("p (n d) -> p n d", n=NT)

        def featT(at):
            return pers(at, 2048).rearrange("p (c t) -> p c t", c=8)

        ss = small[:, 0:2]
        std = small[:, 2:4]
        rstd = small[:, 4:6]
        one_minus_ka = small[:, 40:48]
        decayC = [small[:, 80 + 8 * i:88 + 8 * i] for i in range(2)]
        negmax = small[:, 96:98]
        denom = small[:, 98:100]
        rden = small[:, 100:102]

        def w_slot(n):
            return BIGB[:, (n % RING) * UNIT:(n % RING + 1) * UNIT]

        def kview(w):
            return w.rearrange("(k p) n -> p k n", p=P)

        units = []
        free_at = []

        def cols_units(w, c0, cw, free):
            per = UNIT // cw
            for k0 in range(0, KC, per):
                free_at.append(free)
                units.append([((per, cw), slice(0, per), None, kview(w)[:, k0:k0 + per, c0:c0 + cw])])

        wr, wk, wv, wo_r = (A[n][0] for n in ("rwkv_wr", "rwkv_wk", "rwkv_wv", "rwkv_wo"))
        for iw, w in enumerate((wr, wk)):
            for ch in range(2):
                cols_units(w, 512 * ch, 512, ("proj_done", 4 * iw + 2 * ch + 2))
        U_LORA1 = len(units)
        free_at.append(("proj_done", 11))
        units.append([((8, 256), slice(0, 8), slice(0, 64), kview(A["rwkv_w1"][0])),
                      ((8, 256), slice(0, 8), slice(64, 128), kview(A["rwkv_a1"][0])),
                      ((8, 256), slice(0, 8), slice(128, 256), kview(A["rwkv_g1"][0]))])
        for ch in range(2):
            cols_units(wv, 512 * ch, 512, ("proj_done", 11 + 2 * ch + 2))
        U_LORA2 = len(units)
        free_at.append(("proj_done", 23))
        units.append([("rows64", 0, A["rwkv_w2"][0]), ("rows64", 1, A["rwkv_a2"][0])])
        U_SCAN = len(units)
        U_WO = len(units)
        for ch in range(2):
            cols_units(wo_r, 512 * ch, 512, ("x_mm", 2 * ch + 2))
        U_FFN = len(units)
        for c0 in range(0, FF, 512):
            cw = min(512, FF - c0)
            for w in ("ffn_w1", "ffn_w3"):
                cols_units(A[w][0], c0, cw, ("ffn_up_mm", 2 * (c0 + cw) // P))
        U_FFN2 = len(units)
        for f0 in range(0, FT, 2):
            free_at.append(("ffn_down_mm", f0 // 2 + 1) if f0 < FT - 2 else ("x_mm", 8))
            units.append([((2, D), slice(0, 2), None, kview(A["ffn_w2"][0])[:, f0:f0 + 2, :])])
        U_KV = len(units)
        for ch in range(2 * QD // 512):
            cols_units(A["w_kv"], 512 * ch, 512, ("att_proj_done", 2 * ch + 2))
        U_Q = len(units)
        for ch in range(QD // 512):
            cols_units(A["attn_wq"][0], 512 * ch, 512, ("att_proj_done", 12 + 2 * ch + 2))
        U_AWO = len(units)
        for k0 in (0, 2):
            free_at.append(("x_mm", 12))
            units.append([((2, D), slice(0, 2), None, kview(A["attn_wo"][0])[:, k0:k0 + 2, :])])
        U_MOE = len(units)

        slot_sem = [sem(f"slot{i}_loaded") for i in range(RING)]
        loaded_at = []
        slot_total = [0] * RING
        for n, u in enumerate(units):
            slot_total[n % RING] += 16 * len(u)
            loaded_at.append(slot_total[n % RING])

        def unit_cols(n, per, cw):
            return w_slot(n)[:, 0:per * cw].rearrange("p (k n) -> p k n", k=per)

        moe_order = []
        for j in range(ECH):
            moe_order += [("w1", j, 0), ("w1", j, 1), ("w3", j, 0), ("w3", j, 1)]
            if j:
                moe_order += [("w2", j - 1, 0), ("w2", j - 1, 1)]
        moe_order += [("w2", ECH - 1, 0), ("w2", ECH - 1, 1)]
        PER_E = len(moe_order)
        assert PER_E % RING == 0
        moe_at = {key: n for n, key in enumerate(moe_order)}
        REUSE = PER_E // RING

        def weights_here(pe, n):
            pe.wait_ge(slot_sem[n % RING], loaded_at[n])

        def moe_slot(key):
            return (U_MOE + moe_at[key]) % RING

        def moe_unit(m):
            return unit_cols(U_MOE + m, 2, D) if moe_order[m][0] == "w2" else unit_cols(U_MOE + m, 4, 512)

        def moe_unit_here(eng, m, i):
            s = (U_MOE + m) % RING
            eng.wait_ge(slot_sem[s], 16 * REUSE * i + (slot_total[s] + 16 * (m // RING + 1)))

        class SetBuf:
            pass

        sets = []
        for si in range(2):
            o = [si * (BIG_N // 2)]

            def take(n):
                r = BIGB[:, o[0]:o[0] + n]
                o[0] += n
                return r

            b = SetBuf()
            bd = lambda v: v.rearrange("p (m h t) -> p m h t", m=8, h=2)
            full = lambda v: v.rearrange("p (m n) -> p m n", m=8)
            ar = take(1024)
            b.AR = full(ar)
            b.sq = ar[:, 0:512]
            b.Abd, b.Rbd, b.Bbd, b.Kbd, b.BhT, b.KhT = [take(1024) for _ in range(6)]
            b.BhN, b.KhN = [full(take(1024)) for _ in range(2)]
            over = take(4096)
            b.sc = [over[:, 512 * i:512 * i + 512] for i in range(8)]
            b.N, b.Lk, b.Mb, b.Mk = [over[:, 1024 * i:1024 * (i + 1)] for i in range(4)]
            b.X = full(take(1024))
            b.Y, b.Z = full(b.Bbd), full(b.Kbd)
            b.V, b.Yd = full(b.BhT), full(b.KhT)
            b.S, b.U0, b.U = [take(256).rearrange("p (c n) -> p c n", c=2) for _ in range(3)]
            b.yT = take(512)
            b.bd = bd
            b.full = full
            sets.append(b)
        assert o[0] <= BIG_N, o[0]

        def flat(v):
            return v.rearrange("p c t -> p (c t)")

        def c8(v):
            return v.rearrange("p c (j t) -> p (c j) t", t=CH)

        def s8(v):
            return v.rearrange("p (m t) -> p m t", t=CH)

        def bc(v, shape):
            return v.to_broadcast(shape)

        def mid(v, n):
            return v.unsqueeze(1).to_broadcast([P, n, v.shape[1]])

        def last(v, n):
            return v.unsqueeze(2).to_broadcast([P, v.shape[1], n])

        zT = featT(L0_)
        ffn_in = featT(K_)
        silu_sb = pers(R_, 1024).rearrange("p (b t) -> p b t", b=4)
        actT = pers(A_, FT * S).rearrange("p (f t) -> p f t", f=FT)
        kvT = pers(HT_, 2048).rearrange("p (c t) -> p c t", c=8)
        qinT = featT(L0_)
        dist = pers(HT_, NDIST)
        kTa = pers(L1_, QT_N * S).rearrange("p (f t) -> p f t", f=QT_N)
        vNa = pers(L1_ + QT_N * S, NT * QD).rearrange("p (n d) -> p n d", n=NT)
        qTa = pers(L1_ + 2 * QT_N * S, QT_N * 2 * S).rearrange("p (f h t) -> p f h t", f=QT_N, h=2)
        prob = [extra[:, 768 * i:768 * i + 768] for i in range(2)]
        probT = [extra[:, 1536 + 768 * i:1536 + 768 * i + 768] for i in range(2)]
        oN = pers(L0_, NT * 512).rearrange("p (n d) -> p n d", n=NT)
        oT = pers(L0_ + 1024, 4 * S).rearrange("p (c t) -> p c t", c=4)
        hN = nat(L1_)
        hTm = featT(K_)
        router = pers(HT_, 64).rearrange("p (k e) -> p k e", k=KC)
        router_bias = pers(HT_ + 64, 8)
        logits = pers(HT_ + 80, 16).rearrange("p (n e) -> p n e", n=NT)
        expl = pers(HT_ + 96, 16).rearrange("p (n e) -> p n e", n=NT)
        chosen = pers(HT_ + 112, 16).rearrange("p (n e) -> p n e", n=NT)
        gates = pers(HT_ + 128, 17 * NT).rearrange("p (n e) -> p n e", n=NT)
        slotof = pers(HT_ + 168, 17 * NT).rearrange("p (n e) -> p n e", n=NT)
        beats = pers(HT_ + 208, 64).rearrange("p (e j) -> p e j", e=NE)
        ties = pers(HT_ + 272, 64).rearrange("p (e j) -> p e j", e=NE)
        nrank = pers(HT_ + 336, 8)
        top = pers(HT_ + 344, 8)
        overflow = sb("overflow", [P, 1], I32)
        final_gain = pers(HT_ + 1024, 1024)
        onehot = pers(L0_, 256).rearrange("p (n s) -> p n s", n=NT)
        gated = pers(L0_ + 256, 256).rearrange("p (n s) -> p n s", n=NT)
        scatT = pers(L0_ + 512, 256)
        siluE = pers(L0_ + 768, 512)
        hidE = pers(L0_ + 1280, 512)
        out_sb = nat(R_)
        hTe_high, hTe_low = [rounded(f"tokens_{w}", pers_base + 4 * (A_ + 1024 * q), 1024).rearrange("p (k n) -> p k n", k=KC)
                             for q, w in enumerate(("high", "low"))]
        hidT_high, hidT_low = [rounded(f"hidden_{w}", pers_base + 4 * (A_ + 2048 + 512 * q), 512)
                               .rearrange("p (f n) -> p f n", f=4) for q, w in enumerate(("high", "low"))]
        gathered = [pers(A_ + 3072 + 512 * q, 512).rearrange("p (k n) -> p k n", k=4) for q in range(2)]
        split = [[rounded(f"weights_{w}_{q}", big_base + 4 * (SPLIT_AT + (2 * q + z) * UNIT), UNIT)
                  for z, w in enumerate(("high", "low"))] for q in range(PAIRS)]

        def split_unit(m):
            k = 2 if moe_order[m][0] == "w2" else 4
            return [w[:, :].rearrange("p (k n) -> p k n", k=k) for w in split[m % PAIRS]]
        ySB = pers(LD_, 1024)
        NORM_XN = [nat(L0_), nat(L1_), nat(L1_), hN]
        SQ = [PS[:, 4 + 2 * n:6 + 2 * n, :].rearrange("p b n -> p (b n)") for n in range(NT)]

        block = ctx.enter_context(nc.Block())

        @block.sync
        def _(sp):
            sp.dma_start(x[:], A["x"][0].rearrange("(n p) d -> p n d", p=P)).then_inc(sem("x_loaded"), 16)
            sp.dma_start(C[:], A["const_tables"]).then_inc(sem("consts_loaded"), 16)
            sp.dma_start(V[:], A["vectors"]).then_inc(sem("vectors_loaded"), 16)
            for n, u in enumerate(units):
                if n == U_SCAN:
                    sp.wait_ge(sem("scan_over"), 1)
                if n >= RING:
                    sp.wait_ge(sem(free_at[n - RING][0]), free_at[n - RING][1])
                for part in u:
                    if part[0] == "rows64":
                        dst = w_slot(n)[0:64, part[1] * D:(part[1] + 1) * D]
                        src = part[2]
                    elif part[0] == "rows128":
                        dst, src = w_slot(n)[:, 0:D], part[2]
                    else:
                        (per, cw), ks, cs, src = part
                        dst = unit_cols(n, per, cw)[:, ks, cs if cs is not None else slice(0, cw)]
                    sp.dma_start(dst, src).then_inc(slot_sem[n % RING], 16)

            wview = {w: A[f"moe_{w}"].rearrange("a e (k p) n -> (a e) p k n", p=P) for w in ("w1", "w3")}
            w2_tiles = A["moe_w2"].rearrange("a e (k p) n -> p (a e k) n", p=P)

            def load_unit(e, m, name, value):
                w, j, h = moe_order[m]
                s = (U_MOE + m) % RING
                if w == "w2":
                    dst = unit_cols(s, 2, D)
                    src = w2_tiles[:, bass.ds(e * (FE // P) + 4 * j + 2 * h, 2), :]
                else:
                    dst = unit_cols(s, 4, 512)
                    src = wview[w][e, :, 4 * h:4 * h + 4, 512 * j:512 * j + 512]
                sp.wait_ge(sem(name), value)
                sp.dma_start(dst, src).then_inc(slot_sem[s], 16)

            def expert_units(e, i, ms):
                for m in ms:
                    load_unit(e, m, "low_ready", PER_E * i + (m - RING) % PER_E + 1)

            def stream_experts(i0):
                with sp.Fori(0, NE - 1) as e:
                    i = e + i0 if i0 else e
                    following = sp.snap(e + 1)
                    expert_units(e, i, range(RING, PER_E))
                    expert_units(following, i, range(RING))
                expert_units(NE - 1, i0 + NE - 1, range(RING, PER_E))

            for m in range(RING):
                load_unit(0, m, *free_at[U_MOE + m - RING])
            stream_experts(0)
            sp.wait_ge(sem("overflow_known"), 1)
            more = sp.value_load(overflow[0:1, 0:1])
            with sp.If(more > 0):
                expert_units(0, NE - 1, range(RING))
                stream_experts(NE)
            for n in range(NT):
                sp.wait_ge(sem("out_ready"), n + 1)
                sp.dma_start(out[0].rearrange("(n p) d -> p n d", p=P)[:, n, :],
                             out_sb[:, n, :]).then_inc(sem("out_stored"), 16)
            sp.wait_ge(sem("out_stored"), 16 * NT)

        @block.gpsimd
        def _(pool):
            pool.wait_ge(sem("proj_done"), 15)
            pool.dma_start(gate_w, A["rwkv_g2"][0]).then_inc(sem("gate_w_loaded"), 16)
            pool.wait_ge(sem("att_proj_evac"), 12)
            pool.dma_start(dist[:], A["distance_tables"]).then_inc(sem("dist_loaded"), 16)
            pool.wait_ge(sem("x_added"), 12)
            pool.dma_start(router, kview(A["moe_router"][0])).then_inc(sem("router_loaded"), 16)
            pool.dma_start(router_bias, A["router_bias_rows"]).then_inc(sem("router_loaded"), 16)
            pool.dma_start(final_gain, A["final_gain_rows"]).then_inc(sem("final_gain_loaded"), 16)

        @block.tensor
        def _(pe):
            mm = nc.tensor.matmul

            def norm_transposes(k):
                pe.wait_ge(sem("norm_scaled"), k + 1)
                src = NORM_XN[k]
                for b in range(4):
                    for q in range(4):
                        c, n = 2 * b + q // 2, q % 2
                        ins = nc.tensor.transpose(PS[:, b, q * P:(q + 1) * P], src[:, n, c * P:(c + 1) * P], ident)
                    ins.then_inc(sem("norm_transposed"), 1)

            pe.wait_ge(sem("consts_loaded"), 16)
            norm_transposes(0)

            job = [0]

            def job_bank(evac="proj_evac", mod=4):
                if job[0] >= mod:
                    pe.wait_ge(sem(evac), job[0] - mod + 1)
                job[0] += 1
                return (job[0] - 1) % mod

            def proj_T(u0, src, ncols, wait_each, evac, done):
                for ch in range(ncols // 512):
                    for half_ in range(2):
                        weights_here(pe, u0 + 2 * ch + half_)
                    for f2 in range(2):
                        b = job_bank(evac)
                        for fi in range(2):
                            f = 2 * f2 + fi
                            for k in range(KC):
                                w = unit_cols(u0 + 2 * ch + k // 4, 4, 512)
                                ins = mm(PS[:, b, fi * S:(fi + 1) * S], w[:, k % 4, f * P:(f + 1) * P], src[:, k, :],
                                         start=(k == 0), stop=(k == KC - 1))
                        ins.then_inc(sem(done), 1)

            def proj_N(u0, src, ncols, evac, done):
                for ch in range(ncols // 512):
                    for half_ in range(2):
                        weights_here(pe, u0 + 2 * ch + half_)
                    for n in range(NT):
                        b = job_bank(evac)
                        for k in range(KC):
                            w = unit_cols(u0 + 2 * ch + k // 4, 4, 512)
                            ins = mm(PS[:, b, :], src[:, k, n * P:(n + 1) * P], w[:, k % 4, :],
                                     start=(k == 0), stop=(k == KC - 1))
                        ins.then_inc(sem(done), 1)

            pe.wait_ge(sem("lerp_ready"), 1)
            proj_T(0, lerp[0], D, None, "proj_evac", "proj_done")
            pe.wait_ge(sem("lerp_ready"), 2)
            proj_T(4, lerp[1], D, None, "proj_evac", "proj_done")
            weights_here(pe, U_LORA1)
            for i, (lo, hi) in enumerate(((0, 64), (64, 128), (128, 256))):
                pe.wait_ge(sem("lerp_ready"), 3 + i)
                b = job_bank()
                for k in range(KC):
                    ins = mm(PS[0:hi - lo, b, 0:S], unit_cols(U_LORA1, 8, 256)[:, k, lo:hi], lerp[i % 2][:, k, :],
                             start=(k == 0), stop=(k == KC - 1))
                ins.then_inc(sem("proj_done"), 1)
            pe.wait_ge(sem("lerp_ready"), 6)
            proj_T(U_LORA1 + 1, lerp[1], D, None, "proj_evac", "proj_done")
            weights_here(pe, U_LORA2)
            for i in range(2):
                for f2 in range(4):
                    b = job_bank()
                    for fi in range(2):
                        f = 2 * f2 + fi
                        ins = mm(PS[:, b, fi * S:(fi + 1) * S],
                                 w_slot(U_LORA2)[0:64, i * D + f * P:i * D + (f + 1) * P], loraT[i][0:64, :],
                                 start=True, stop=True)
                    ins.then_inc(sem("proj_done"), 1)

            for gp in range(2):
                gs = [(2 * gp + si, si, sets[si], 4 * si) for si in range(2)]
                for g, si, b, bank in gs:
                    pe.wait_ge(sem("kk_squared"), g + 1)
                    mm(PS[:, bank, :], cst("headones"), b.sc[1], start=True, stop=True).then_inc(sem("kk_norm_mm"), 1)
                for g, si, b, bank in gs:
                    pe.wait_ge(sem("rk_ready"), g + 1)
                    mm(PS[:, bank + 1, :], cst("headones"), b.sc[3], start=True, stop=True).then_inc(sem("bonus_mm"), 1)

                def cols(bank, m):
                    return PS[:, bank + m // 4, (m % 4) * P:(m % 4 + 1) * P]

                def blocks(v, m):
                    return v[:, m * P:(m + 1) * P]

                for g, si, b, bank in gs:
                    pe.wait_ge(sem("tails_ready"), g + 1)
                    for m in range(8):
                        ins = nc.tensor.transpose(cols(bank + 2, m), blocks(b.BhT, m), ident)
                    ins.then_inc(sem("tailsT_mm"), 1)
                    pe.wait_ge(sem("bonus_taken"), g + 1)
                    for m in range(8):
                        ins = nc.tensor.transpose(cols(bank, m), blocks(b.KhT, m), ident)
                    ins.then_inc(sem("tailsT_mm"), 1)
                for g, si, b, bank in gs:
                    pe.wait_ge(sem("vbd_ready"), g + 1)
                    pe.wait_ge(sem("tails_taken"), 2 * g + 1)
                    for m in range(8):
                        ins = nc.tensor.transpose(cols(bank + 2, m), b.X[:, m], ident)
                    ins.then_inc(sem("v_mm"), 1)
                for g, si, b, bank in gs:
                    pe.wait_ge(sem("grams_in"), g + 1)
                    pe.wait_ge(sem("tails_taken"), 2 * g + 2)
                    for m in range(8):
                        ins = mm(cols(bank, m), blocks(b.Bbd, m), b.AR[:, m], start=True, stop=True)
                    ins.then_inc(sem("grams_mm"), 1)
                    pe.wait_ge(sem("v_taken"), g + 1)
                    for m in range(8):
                        ins = mm(cols(bank + 2, m), blocks(b.Kbd, m), b.AR[:, m], start=True, stop=True)
                    ins.then_inc(sem("grams_mm"), 1)
                for lev in range(LEVELS):
                    for g, si, b, bank in gs:
                        if lev == 0:
                            pe.wait_ge(sem("grams_taken"), g + 1)
                        else:
                            pe.wait_ge(sem("X_ready"), gp * 2 * (LEVELS - 1) + 2 * (lev - 1) + si + 1)
                            pe.wait_ge(sem("Y_ready"), gp * 2 * LEVELS + 2 * (lev - 1) + si + 1)
                        for m in range(8):
                            ins = mm(cols(bank, m), blocks(b.N, m), ident if lev == 0 else b.X[:, m],
                                     start=True, stop=True)
                        ins.then_inc(sem("LX_mm"), 1)
                    for g, si, b, bank in gs:
                        if 0 < lev < LEVELS - 1:
                            pe.wait_ge(sem("Z_ready"), gp * 2 * LEVELS + 2 * lev + si + 1)
                            for m in range(8):
                                ins = mm(cols(bank + 2, m), b.Y[:, m], b.Z[:, m], start=True, stop=True)
                            ins.then_inc(sem("XZ_mm"), 1)
                    for g, si, b, bank in gs:
                        pe.wait_ge(sem("Z_ready"), gp * 2 * LEVELS + 2 * lev + si + 1)
                        for m in range(8):
                            ins = mm(cols(bank, m), b.Z[:, m], ident if lev == 0 else b.Y[:, m], start=True, stop=True)
                        ins.then_inc(sem("ZY_mm"), 1)
                for j in range(NCH):
                    q0 = gp * 2 * NCH + 2 * j
                    for g, si, b, bank in gs:
                        if j == 0:
                            pe.wait_ge(sem("Y_ready"), gp * 2 * LEVELS + 2 * (LEVELS - 1) + si + 1)
                        pe.wait_ge(sem("state_ready"), gp * 2 * NCH + 2 * j + si + 1)
                        for c in range(2):
                            m = 4 * c + j
                            o_ = PS[:, bank + 1, c * P:(c + 1) * P]
                            mm(o_, blocks(b.Abd, m), b.S[:, c], start=True, stop=False)
                            ins = mm(o_, blocks(b.Lk, m), b.V[:, m], start=False, stop=True)
                        ins.then_inc(sem("U0_mm"), 1)
                    for g, si, b, bank in gs:
                        if j:
                            pe.wait_ge(sem("y_taken"), q0 + si - 1)
                        pe.wait_ge(sem("U0_ready"), q0 + si + 1)
                        for c in range(2):
                            ins = mm(PS[:, bank + 3, c * P:(c + 1) * P], b.Y[:, 4 * c + j], b.U0[:, c],
                                     start=True, stop=True)
                        ins.then_inc(sem("U_mm"), 1)
                    for g, si, b, bank in gs:
                        pe.wait_ge(sem("U_ready"), q0 + si + 1)
                        if j < NCH - 1:
                            for c in range(2):
                                m = 4 * c + j
                                o_ = PS[:, bank, c * P:(c + 1) * P]
                                mm(o_, b.BhN[:, m], b.U[:, c], start=True, stop=False)
                                ins = mm(o_, b.KhN[:, m], b.V[:, m], start=False, stop=True)
                            ins.then_inc(sem("S_mm"), 1)
                        for c in range(2):
                            m = 4 * c + j
                            o_ = PS[:, bank + 2, c * P:(c + 1) * P]
                            mm(o_, blocks(b.Rbd, m), b.S[:, c], start=True, stop=False)
                            mm(o_, blocks(b.Mb, m), b.U[:, c], start=False, stop=False)
                            ins = mm(o_, blocks(b.Mk, m), b.V[:, m], start=False, stop=True)
                        ins.then_inc(sem("y_mm"), 1)
                for g, si, b, bank in gs:
                    pe.wait_ge(sem("y_taken"), gp * 2 * NCH + 2 * (NCH - 1) + si + 1)
                    for m in range(8):
                        ins = mm(cols(bank, m), b.Yd[:, m], cst("eye64x2"), start=True, stop=True)
                    ins.then_inc(sem("yT_mm"), 1)
                for g, si, b, bank in gs:
                    pe.wait_ge(sem("yT_ready"), g + 1)
                    mm(PS[:, bank + 2, :], cst("headones"), b.yT, start=True, stop=True).then_inc(sem("mean_mm"), 1)
                for g, si, b, bank in gs:
                    if g == 0:
                        pe.wait_ge(sem("gate_w_loaded"), 16)
                    for c in range(2):
                        f = 2 * g + c
                        ins = mm(PS[:, bank + 1, c * S:(c + 1) * S], gate_w[:, f * P:(f + 1) * P], gateT[:],
                                 start=True, stop=True)
                    ins.then_inc(sem("gate_mm"), 1)
                for g, si, b, bank in gs:
                    pe.wait_ge(sem("y_squared"), g + 1)
                    mm(PS[:, bank + 3, :], cst("headones"), b.sq, start=True, stop=True).then_inc(sem("var_mm"), 1)

            def proj_x(u0, src, evac_base):
                for ch in range(2):
                    for half_ in range(2):
                        weights_here(pe, u0 + 2 * ch + half_)
                    for n in range(NT):
                        for k in range(KC):
                            w = unit_cols(u0 + 2 * ch + k // 4, 4, 512)
                            ins = mm(PS[:, 2 * ch + n, :], src[:, k, n * P:(n + 1) * P], w[:, k % 4, :],
                                     start=(k == 0), stop=(k == KC - 1))
                        ins.then_inc(sem("x_mm"), 1)

            pe.wait_ge(sem("z_ready"), GROUPS)
            proj_x(U_WO, zT, 0)

            norm_transposes(1)
            pe.wait_ge(sem("normT_ready"), 8)
            u = U_FFN
            for f in range(FT):
                if f >= 4:
                    pe.wait_ge(sem("ffn_hidden"), f - 3)
                cw = min(512, FF - f // 4 * 512)
                per = UNIT // cw
                nu = KC // per
                if f % 4 == 0:
                    for i in range(2 * nu):
                        weights_here(pe, u + i)
                for i in range(2):
                    for k in range(KC):
                        w = unit_cols(u + i * nu + k // per, per, cw)
                        ins = mm(PS[:, f % 4, i * S:(i + 1) * S], w[:, k % per, (f % 4) * P:(f % 4 + 1) * P],
                                 ffn_in[:, k, :], start=(k == 0), stop=(k == KC - 1))
                    ins.then_inc(sem("ffn_up_mm"), 1)
                if f % 4 == 3 or f == FT - 1:
                    u += 2 * nu
            for f in range(FT):
                if f % 2 == 0:
                    weights_here(pe, U_FFN2 + f // 2)
                pe.wait_ge(sem("ffn_hidden"), f + 1)
                for n in range(NT):
                    for h in range(2):
                        ins = mm(PS[:, 4 + 2 * h + n, :], actT[:, f, n * P:(n + 1) * P],
                                 unit_cols(U_FFN2 + f // 2, 2, D)[:, f % 2, h * 512:(h + 1) * 512],
                                 start=(f == 0), stop=(f == FT - 1))
                        if f == FT - 1:
                            ins.then_inc(sem("x_mm"), 1)
                        elif f % 2 == 1 and n == NT - 1 and h == 1:
                            ins.then_inc(sem("ffn_down_mm"), 1)

            norm_transposes(2)
            pe.wait_ge(sem("normT_ready"), 16)
            job[0] = 0
            proj_T(U_KV, kvT, QD, None, "att_proj_evac", "att_proj_done")
            proj_N(U_KV + 6, kvT, QD, "att_proj_evac", "att_proj_done")
            proj_T(U_Q, qinT, QD, None, "att_proj_evac", "att_proj_done")
            pe.wait_ge(sem("att_proj_evac"), 18)
            NI = NT * SLOTS

            def scores(i):
                hs, qt = divmod(i, NT)
                nk = (qt + 1) * P
                if i >= 2:
                    pe.wait_ge(sem("scores_taken"), i - 1)
                o_ = PS[:, 2 * (i % 2):2 * (i % 2) + 2, :].rearrange("p b n -> p (b n)")
                for br in range(3):
                    f = 4 * br + hs // 2
                    ins = mm(o_[:, br * nk:(br + 1) * nk], qTa[:, f, hs % 2, qt * P:(qt + 1) * P], kTa[:, f, 0:nk],
                             start=True, stop=True)
                ins.then_inc(sem("scores_mm"), 1)

            def prob_transposes(i):
                nb = 3 * (i % 2 + 1)
                pe.wait_ge(sem("prob_ready"), i + 1)
                if i >= 1:
                    pe.wait_ge(sem("probT_ready"), i)
                o_ = PS[:, 4:6, :].rearrange("p b n -> p (b n)")
                for q in range(nb):
                    ins = nc.tensor.transpose(o_[:, q * P:(q + 1) * P], prob[i % 2][:, q * P:(q + 1) * P], ident)
                ins.then_inc(sem("probT_mm"), 1)

            def values(i):
                hs, qt = divmod(i, NT)
                pe.wait_ge(sem("probT_ready"), i + 1)
                if i >= 2:
                    pe.wait_ge(sem("head_out"), i - 1)
                nb = 3 * (qt + 1)
                for q in range(nb):
                    br, kt = divmod(q, qt + 1)
                    col = (br * SLOTS + hs) * HS
                    ins = mm(PS[:, 6 + i % 2, 0:HS], probT[i % 2][:, q * P:(q + 1) * P], vNa[:, kt, col:col + HS],
                             start=(q == 0), stop=(q == nb - 1))
                ins.then_inc(sem("values_mm"), 1)

            scores(0)
            for i in range(NI):
                if i + 1 < NI:
                    scores(i + 1)
                prob_transposes(i)
                if i >= 1:
                    values(i - 1)
            values(NI - 1)
            pe.wait_ge(sem("head_out"), NI)
            for n in range(NT):
                for c in range(4):
                    ins = nc.tensor.transpose(PS[:, c // 2, (c % 2) * S + n * P:(c % 2) * S + (n + 1) * P],
                                              oN[:, n, c * P:(c + 1) * P], ident)
            ins.then_inc(sem("oT_mm"), 1)
            pe.wait_ge(sem("oT_ready"), 2)
            for i in range(2):
                weights_here(pe, U_AWO + i)
            for n in range(NT):
                for h in range(2):
                    for k in range(4):
                        ins = mm(PS[:, 2 + 2 * h + n, :], oT[:, k, n * P:(n + 1) * P],
                                 unit_cols(U_AWO + k // 2, 2, D)[:, k % 2, h * 512:(h + 1) * 512],
                                 start=(k == 0), stop=(k == 3))
                    ins.then_inc(sem("x_mm"), 1)

            norm_transposes(3)
            pe.wait_ge(sem("normT_ready"), 20)
            pe.wait_ge(sem("router_loaded"), 32)
            for n in range(NT):
                for k in range(KC):
                    ins = mm(PS[:, 4, n * 8:n * 8 + 8], hTm[:, k, n * P:(n + 1) * P], router[:, k, :],
                             start=(k == 0), stop=(k == KC - 1))
            ins.then_inc(sem("logits_mm"), 1)
            pe.wait_ge(sem("chosen_ready"), 1)
            mm(PS[:, 5, 0:8], cst("earlier"), chosen[:, 0, :], start=True, stop=True)
            mm(PS[:, 5, 8:16], cst("earlier"), chosen[:, 1, :], start=True, stop=False)
            mm(PS[:, 5, 8:16], ones, chosen[:, 0, :], start=False, stop=True)
            mm(PS[:, 5, 16:24], ones, chosen[:, 0, :], start=True, stop=False)
            mm(PS[:, 5, 16:24], ones, chosen[:, 1, :], start=False, stop=True).then_inc(sem("ranks_mm"), 1)

            def gather(i, part):
                bank = 7 - part
                for k in range(4):
                    for n in range(NT):
                        ins = mm(PS[:, bank, k * P:(k + 1) * P], hN[:, n, (4 * part + k) * P:(4 * part + k + 1) * P],
                                 onehot[:, n, :], start=(n == 0), stop=(n == NT - 1))
                ins.then_inc(sem("gather_mm"), 1)

            def scatter_matrix():
                for n in range(NT):
                    ins = nc.tensor.transpose(PS[:, 7, n * P:(n + 1) * P], gated[:, n, :], ident)
                ins.then_inc(sem("scatT_mm"), 1)

            def experts(base):
                with pe.Fori(0, NE) as e:
                    i = e + base if base else e

                    def product(m, out, highs, lows, first, final):
                        pe.wait_ge(sem("low_ready"), PER_E * i + (m + 1))
                        wh, wl = split_unit(m)
                        for k in range(len(highs)):
                            for h, o_ in enumerate(out):
                                cs = slice(h * 512, (h + 1) * 512)
                                mm(o_, highs[k], wh[:, k, cs], start=(first and k == 0), stop=False)
                                mm(o_, highs[k], wl[:, k, cs], start=False, stop=False)
                                ins = mm(o_, lows[k], wh[:, k, cs], start=False, stop=(final and k == len(highs) - 1))
                        ins.then_inc(sem("unit_used"), 1)

                    def up(j, which):
                        if which == 0:
                            if j == 0:
                                pe.wait_ge(sem("gathered_low"), 2 * i + 2)
                            elif j == 1:
                                pe.wait_ge(sem("scatT_ready"), i + 1)
                            else:
                                pe.wait_ge(sem("hidden_ready"), ECH * i + (j - 1))
                        for h in range(2):
                            ks = range(4 * h, 4 * h + 4)
                            product(moe_at[(("w1", "w3")[which], j, h)], [PS[:, 2 * (j % 2) + which, :]],
                                    [hTe_high[:, k, :] for k in ks], [hTe_low[:, k, :] for k in ks], h == 0, h == 1)

                    def hidden_transposes(j):
                        pe.wait_ge(sem("hidden_ready"), ECH * i + (j + 1))
                        for q in range(4):
                            ins = nc.tensor.transpose(PS[:, 6, q * P:(q + 1) * P], hidE[:, q * P:(q + 1) * P], ident)
                        ins.then_inc(sem("hidT_mm"), 1)

                    def down(j):
                        pe.wait_ge(sem("hidT_low"), ECH * i + (j + 1))
                        for h in range(2):
                            qs = range(2 * h, 2 * h + 2)
                            product(moe_at[("w2", j, h)], [PS[:, 4, :], PS[:, 5, :]],
                                    [hidT_high[:, q, :] for q in qs], [hidT_low[:, q, :] for q in qs],
                                    j == 0 and h == 0, j == ECH - 1 and h == 1)

                    for j in range(ECH):
                        up(j, 0)
                        if j:
                            hidden_transposes(j - 1)
                        up(j, 1)
                        if j:
                            down(j - 1)
                    hidden_transposes(ECH - 1)
                    pe.wait_ge(sem("onehot_ready"), i + 2)
                    gather(i, 0)
                    down(ECH - 1)
                    gather(i, 1)
                    pe.wait_ge(sem("y_ready"), i + 1)
                    for n in range(NT):
                        for h in range(2):
                            mm(PS[:, (4, 5, 2, 3)[2 * n + h], :], scatT[:, n * P:(n + 1) * P], ySB[:, h * 512:(h + 1) * 512],
                               start=True, stop=True).then_inc(sem("scatter_mm"), 1)
                    pe.wait_ge(sem("gathered_low"), 2 * i + 3)
                    scatter_matrix()

            pe.wait_ge(sem("onehot_ready"), 1)
            gather(0, 0)
            gather(0, 1)
            pe.wait_ge(sem("gathered_low"), 1)
            scatter_matrix()
            experts(0)
            pe.wait_ge(sem("overflow_known"), 1)
            more = pe.value_load(overflow[0:1, 0:1])
            with pe.If(more > 0):
                experts(NE)

        @block.scalar
        def _(act):
            own = Own(act, sem("act_step"))
            a_ = nc.scalar.activation

            def norm_stats(k):
                for n in range(NT):
                    ins = a_(SQ[n], x[:, n, :], ACT.Square, accum_out=ss[:, n:n + 1])
                ins.then_inc(sem("squares_summed"), 1)
                act.wait_ge(sem("mean_ready"), k + 1)
                a_(std, ss, ACT.Sqrt).then_inc(sem("root_ready"), 1)

            act.wait_ge(sem("x_loaded"), 16)
            norm_stats(0)

            act.wait_ge(sem("vectors_loaded"), 16)
            job = 0

            def take(dst, src, func=ACT.Copy, **kw):
                return a_(dst, src, func, **kw)

            for dst in (rT, kT):
                for f2 in range(4):
                    act.wait_ge(sem("proj_done"), job + 1)
                    take(flat(dst[:, 2 * f2:2 * f2 + 2, :]), PS[:, job % 4, :]).then_inc(sem("proj_evac"), 1)
                    job += 1
            for i, (rows, func) in enumerate(((64, ACT.Tanh), (64, ACT.Copy), (128, ACT.Sigmoid))):
                act.wait_ge(sem("proj_done"), job + 1)
                take(loraT[i][0:rows, :], PS[0:rows, job % 4, 0:S], func).then_inc(sem("proj_evac"), 1)
                job += 1
            for f2 in range(4):
                act.wait_ge(sem("proj_done"), job + 1)
                take(flat(vT[:, 2 * f2:2 * f2 + 2, :]), PS[:, job % 4, :]).then_inc(sem("proj_evac"), 1)
                job += 1
            for dst, bias in ((ldT, "w0"), (aT, "a0")):
                for f2 in range(4):
                    act.wait_ge(sem("proj_done"), job + 1)
                    for fi in range(2):
                        c = 2 * f2 + fi
                        ins = take(dst[:, c, :], PS[:, job % 4, fi * S:(fi + 1) * S], ACT.Sigmoid,
                                   bias=vec(bias)[:, c:c + 1])
                    ins.then_inc(sem("proj_evac"), 1)
                    job += 1

            for gp in range(2):
                gs = [(2 * gp + si, si, sets[si], 4 * si) for si in range(2)]
                for g, si, b, bank in gs:
                    act.wait_ge(sem("kk_ready"), g + 1)
                    a_(b.sc[1], b.sc[0], ACT.Square).then_inc(sem("kk_squared"), 1)
                for g, si, b, bank in gs:
                    act.wait_ge(sem("kk_norm_mm"), g + 1)
                    a_(b.sc[1], PS[:, bank, :], ACT.Sqrt).then_inc(sem("kk_root"), 1)
                for g, si, b, bank in gs:
                    act.wait_ge(sem("cum_ready"), g + 1)
                    a_(b.sc[5], b.sc[4], ACT.Exp).then_inc(sem("decays"), 1)
                    a_(b.sc[6], b.sc[4], ACT.Exp, scale=-1.0).then_inc(sem("decays"), 1)
                    a_(decayC[si], s8(b.sc[4])[:, :, CH - 1], ACT.Exp).then_inc(sem("decays"), 1)
                    act.wait_ge(sem("cum_before"), g + 1)
                    a_(b.sc[7], b.sc[7], ACT.Exp).then_inc(sem("decays"), 1)
                    act.wait_ge(sem("cum_after"), g + 1)
                    a_(b.sc[1], b.sc[1], ACT.Exp).then_inc(sem("decays"), 1)
                for g, si, b, bank in gs:
                    if gp == 0:
                        act.wait_ge(sem("scan_open"), 1)
                    else:
                        act.wait_ge(sem("LX_mm"), 2 * LEVELS * gp)
                    for h in range(2):
                        ins = a_(b.X[:, :, h * CH:(h + 1) * CH], c8(vT[:, 2 * g:2 * g + 2, :]), ACT.Copy, scale=half(h))
                    ins.then_inc(sem("vbd_ready"), 1)
                for g, si, b, bank in gs:
                    act.wait_ge(sem("AR_ready"), g + 1)
                    for h in range(2):
                        a_(b.bd(b.Abd)[:, :, h, :], b.AR[:, :, 0:CH], ACT.Copy, scale=half(h))
                        ins = a_(b.bd(b.Rbd)[:, :, h, :], b.AR[:, :, CH:2 * CH], ACT.Copy, scale=half(h))
                    ins.then_inc(sem("ARbd_ready"), 1)
                two_banks = lambda bank: PS[:, bank:bank + 2, :].rearrange("p b n -> p (b n)")
                allof = lambda v: v.rearrange("p m n -> p (m n)")
                for g, si, b, bank in gs:
                    act.wait_ge(sem("tailsT_mm"), 2 * g + 1)
                    a_(allof(b.BhN), two_banks(bank + 2), ACT.Copy).then_inc(sem("tails_taken"), 1)
                    act.wait_ge(sem("tailsT_mm"), 2 * g + 2)
                    a_(allof(b.KhN), two_banks(bank), ACT.Copy).then_inc(sem("tails_taken"), 1)
                for g, si, b, bank in gs:
                    act.wait_ge(sem("v_mm"), g + 1)
                    a_(allof(b.V), two_banks(bank + 2), ACT.Copy).then_inc(sem("v_taken"), 1)
                for j in range(NCH):
                    q0 = gp * 2 * NCH + 2 * j
                    for g, si, b, bank in gs:
                        act.wait_ge(sem("U0_mm"), q0 + si + 1)
                        a_(b.U0.rearrange("p c n -> p (c n)"), PS[:, bank + 1, 0:2 * P], ACT.Copy).then_inc(sem("U0_ready"), 1)
                    for g, si, b, bank in gs:
                        act.wait_ge(sem("U_mm"), q0 + si + 1)
                        a_(b.U.rearrange("p c n -> p (c n)"), PS[:, bank + 3, 0:2 * P], ACT.Copy).then_inc(sem("U_ready"), 1)
                    for g, si, b, bank in gs:
                        act.wait_ge(sem("y_mm"), q0 + si + 1)
                        a_(b.Yd.rearrange("p (c j) n -> p c j n", c=2)[:, :, j, :],
                           PS[:, bank + 2, 0:2 * P].rearrange("p (c n) -> p c n", c=2), ACT.Copy).then_inc(sem("y_taken"), 1)
                for g, si, b, bank in gs:
                    act.wait_ge(sem("yT_mm"), g + 1)
                    a_(s8(b.yT), two_banks(bank).rearrange("p (m n) -> p m n", m=8)[:, :, 0:CH],
                       ACT.Copy).then_inc(sem("yT_ready"), 1)
                for g, si, b, bank in gs:
                    act.wait_ge(sem("y_centred"), g + 1)
                    a_(b.sq, b.yT, ACT.Square).then_inc(sem("y_squared"), 1)
                for g, si, b, bank in gs:
                    act.wait_ge(sem("gn_var"), g + 1)
                    a_(b.sq, b.sq, ACT.Sqrt).then_inc(sem("gn_root"), 1)

            act.wait_ge(sem("x_added"), 4)
            norm_stats(1)
            for f in range(FT):
                act.wait_ge(sem("ffn_up_mm"), 2 * f + 2)
                if f >= 4:
                    act.wait_ge(sem("ffn_hidden"), f - 3)
                a_(silu_sb[:, f % 4, :], PS[:, f % 4, 0:S], ACT.Silu).then_inc(sem("ffn_silu"), 1)

            act.wait_ge(sem("x_added"), 8)
            norm_stats(2)
            job = 0
            for f2 in range(QT_N // 2):
                act.wait_ge(sem("att_proj_done"), job + 1)
                a_(flat(kTa[:, 2 * f2:2 * f2 + 2, :]), PS[:, job % 4, :], ACT.Copy).then_inc(sem("att_proj_evac"), 1)
                job += 1
            for ch in range(3):
                for n in range(NT):
                    act.wait_ge(sem("att_proj_done"), job + 1)
                    a_(vNa[:, n, ch * 512:(ch + 1) * 512], PS[:, job % 4, :], ACT.Copy).then_inc(sem("att_proj_evac"), 1)
                    job += 1
            for f2 in range(QT_N // 2):
                act.wait_ge(sem("att_proj_done"), job + 1)
                for h in range(2):
                    ins = a_(qTa[:, 2 * f2:2 * f2 + 2, h, :], PS[:, job % 4, :].rearrange("p (f t) -> p f t", f=2),
                             ACT.Copy, scale=half8(h))
                ins.then_inc(sem("att_proj_evac"), 1)
                job += 1

            def softmax_exp(i):
                n = 3 * P * (i % 2 + 1)
                act.wait_ge(sem("max_ready"), i + 1)
                a_(prob[i % 2][:, 0:n], prob[i % 2][:, 0:n], ACT.Exp, bias=negmax[:, i % 2:i % 2 + 1],
                   accum_out=denom[:, i % 2:i % 2 + 1]).then_inc(sem("prob_ready"), 1)

            NI = NT * SLOTS
            for i in range(NI):
                softmax_exp(i)
                n = 3 * P * (i % 2 + 1)
                act.wait_ge(sem("probT_mm"), i + 1)
                if i >= 2:
                    act.wait_ge(sem("values_mm"), i - 1)
                a_(probT[i % 2][:, 0:n], PS[:, 4:6, :].rearrange("p b n -> p (b n)")[:, 0:n],
                   ACT.Copy).then_inc(sem("probT_ready"), 1)
            act.wait_ge(sem("oT_mm"), 1)
            for b2 in range(2):
                a_(flat(oT[:, 2 * b2:2 * b2 + 2, :]), PS[:, b2, :], ACT.Copy).then_inc(sem("oT_ready"), 1)

            act.wait_ge(sem("x_added"), 12)
            norm_stats(3)
            act.wait_ge(sem("topneg_ready"), 1)
            for n in range(NT):
                ins = a_(expl[:, n, :], logits[:, n, :], ACT.Exp, bias=top[:, n:n + 1])
            ins.then_inc(sem("expl_ready"), 1)

            def gathered_high(i, part):
                act.wait_ge(sem("gathered"), 2 * i + (part + 1))
                a_(hTe_high[:, 4 * part:4 * part + 4, :], gathered[part], ACT.Copy).then_inc(sem("gathered_high"), 1)

            def high(m, i):
                moe_unit_here(act, m, i)
                act.wait_ge(sem("unit_used"), PER_E * i + (m - PAIRS + 1))
                a_(split_unit(m)[0], moe_unit(m), ACT.Copy).then_inc(sem("high_ready"), 1)

            def expert(i, following):
                def take_hidden(j):
                    act.wait_ge(sem("hidT_mm"), ECH * i + (j + 1))
                    if j:
                        act.wait_ge(sem("unit_used"), PER_E * i + (moe_at[("w2", j - 1, 1)] + 1))
                    a_(hidT_high, PS[:, 6, :].rearrange("p (f n) -> p f n", f=4), ACT.Copy).then_inc(sem("hidT_high"), 1)

                for j in range(ECH):
                    for key in (("w1", j, 0), ("w1", j, 1), ("w3", j, 0), ("w3", j, 1)):
                        if moe_at[key] >= PAIRS:
                            high(moe_at[key], i)
                    act.wait_ge(sem("unit_used"), PER_E * i + (moe_at[("w1", j, 1)] + 1))
                    if j:
                        act.wait_ge(sem("hidden_ready"), ECH * i + j)
                    a_(siluE, PS[:, 2 * (j % 2), :], ACT.Silu).then_inc(sem("silu_ready"), 1)
                    if j:
                        take_hidden(j - 1)
                        for h in range(2):
                            high(moe_at[("w2", j - 1, h)], i)
                for h in range(2):
                    high(moe_at[("w2", ECH - 1, h)], i)
                take_hidden(ECH - 1)
                if following:
                    high(0, i + 1)
                gathered_high(i + 1, 0)
                if following:
                    high(1, i + 1)
                act.wait_ge(sem("unit_used"), PER_E * i + PER_E)
                a_(ySB, PS[:, 4:6, :].rearrange("p b n -> p (b n)"), ACT.Copy).then_inc(sem("y_ready"), 1)
                if following:
                    high(2, i + 1)
                gathered_high(i + 1, 1)

            def experts(base):
                for m in range(PAIRS):
                    moe_unit_here(act, m, base)
                    if base:
                        act.wait_ge(sem("unit_used"), PER_E * base)
                    a_(split_unit(m)[0], moe_unit(m), ACT.Copy).then_inc(sem("high_ready"), 1)
                with act.Fori(0, NE - 1) as e:
                    expert(e + base if base else e, True)
                expert(base + NE - 1, False)

            gathered_high(0, 0)
            gathered_high(0, 1)
            experts(0)
            act.wait_ge(sem("overflow_known"), 1)
            more = act.value_load(overflow[0:1, 0:1])
            with act.If(more > 0):
                experts(NE)
            act.wait_ge(sem("experts_over"), 1)
            norm_stats(4)

        @block.vector
        def _(dve):
            v = nc.vector
            own = Own(dve, sem("dve_step"))
            do = own.do

            def norm_scale(k, dst):
                dve.wait_ge(sem("squares_summed"), k + 1)
                do(v.tensor_scalar(ss, ss, 1.0 / D, RMS_EPS, ALU.mult, ALU.add), sem("mean_ready"))
                dve.wait_ge(sem("root_ready"), k + 1)
                do(v.reciprocal(rstd, std))
                for n in range(NT):
                    ins = v.tensor_scalar(dst[:, n, :], x[:, n, :], rstd[:, n:n + 1], None, ALU.mult)
                return ins

            def norm_take(k, targets):
                for b in range(4):
                    dve.wait_ge(sem("norm_transposed"), 4 * k + b + 1)
                    for t, (dst, gain) in enumerate(targets):
                        do(v.tensor_tensor(dst[:, 2 * b:2 * b + 2, :], PS[:, b, :].rearrange("p (c t) -> p c t", c=2),
                                           last(vec(gain)[:, 2 * b:2 * b + 2], S), ALU.mult), sem("normT_ready"))

            do(v.memset(hT[:, :, 0:1], 0.0))
            norm_scale(0, NORM_XN[0]).then_inc(sem("norm_scaled"), 1)
            dve.wait_ge(sem("vectors_loaded"), 16)
            norm_take(0, [(hT[:, :, 1:S + 1], "g00")])
            do(v.tensor_tensor(dxT, hT[:, :, 0:S], hT[:, :, 1:S + 1], ALU.subtract))
            for i, mu in enumerate((0, 2, 1, 4, 5, 3)):
                if i >= 2:
                    dve.wait_ge(sem("proj_done"), (4, 8, 9, 10)[i - 2])
                for c in range(KC):
                    ins = v.scalar_tensor_tensor(out=lerp[i % 2][:, c, :], in0=dxT[:, c, :],
                                                 scalar=vec(f"mu{mu}")[:, c:c + 1], in1=hT[:, c, 1:S + 1],
                                                 op0=ALU.mult, op1=ALU.add)
                ins.then_inc(sem("lerp_ready"), 1)
            do(v.tensor_scalar(one_minus_ka, vec("k_a"), -1.0, 1.0, ALU.mult, ALU.add))
            dve.wait_ge(sem("proj_done"), 23)
            dve.wait_ge(sem("proj_evac"), 23)
            do(v.memset(negmax, 0.0), sem("scan_open"))
            stt = v.scalar_tensor_tensor
            for gp in range(2):
                gs = [(2 * gp + si, si, sets[si], 4 * si) for si in range(2)]
                for g, si, b, bank in gs:
                    G = slice(2 * g, 2 * g + 2)
                    if gp:
                        dve.wait_ge(sem("yT_mm"), 2 * gp)
                    two = lambda w: w.rearrange("p (c t) -> p c t", c=2)
                    do(v.tensor_tensor(two(b.sc[0]), kT[:, G, :], last(vec("k_k")[:, G], S), ALU.mult), sem("kk_ready"))
                    for c in range(2):
                        ins = v.tensor_scalar(b.sc[3][:, c * S:(c + 1) * S], aT[:, 2 * g + c, :],
                                              vec("k_a")[:, 2 * g + c:2 * g + c + 1],
                                              one_minus_ka[:, 2 * g + c:2 * g + c + 1], ALU.mult, ALU.add)
                    do(ins)
                    do(v.tensor_tensor(flat(kT[:, G, :]), flat(kT[:, G, :]), b.sc[3], ALU.mult))
                    do(v.tensor_tensor(b.sc[3], flat(rT[:, G, :]), flat(kT[:, G, :]), ALU.mult))
                    do(v.tensor_tensor(two(b.sc[3]), two(b.sc[3]), last(vec("r_k")[:, G], S), ALU.mult), sem("rk_ready"))
                    do(v.tensor_scalar(flat(ldT[:, G, :]), flat(ldT[:, G, :]), DECAY, None, ALU.mult))
                    do(v.tensor_tensor_scan(b.sc[4], cst("carry"), flat(ldT[:, G, :]), 0.0, ALU.mult, ALU.add), sem("cum_ready"))
                    do(v.tensor_tensor(b.sc[7], b.sc[4], flat(ldT[:, G, :]), ALU.subtract), sem("cum_before"))
                for g, si, b, bank in gs:
                    G = slice(2 * g, 2 * g + 2)
                    dve.wait_ge(sem("kk_root"), g + 1)
                    do(v.tensor_scalar(b.sc[1], b.sc[1], 1e-12, None, ALU.max))
                    do(v.reciprocal(b.sc[1], b.sc[1]))
                    do(v.tensor_tensor(b.sc[0], b.sc[0], b.sc[1], ALU.mult))
                    do(v.tensor_tensor(b.sc[2], b.sc[0], flat(aT[:, G, :]), ALU.mult))
                    do(v.tensor_tensor(s8(b.sc[1]), last(s8(b.sc[4])[:, :, CH - 1], CH), s8(b.sc[4]), ALU.subtract),
                       sem("cum_after"))
                for g, si, b, bank in gs:
                    G = slice(2 * g, 2 * g + 2)
                    dve.wait_ge(sem("decays"), 5 * g + 4)
                    stt(out=b.AR[:, :, 0:CH], in0=s8(b.sc[0]), scalar=-1.0, in1=s8(b.sc[7]), op0=ALU.mult, op1=ALU.mult)
                    v.tensor_tensor(b.AR[:, :, CH:2 * CH], c8(rT[:, G, :]), s8(b.sc[5]), ALU.mult).then_inc(sem("AR_ready"), 1)
                    for h in range(2):
                        stt(out=b.bd(b.Bbd)[:, :, h, :], in0=s8(b.sc[2]), scalar=half(h), in1=s8(b.sc[6]), op0=ALU.mult, op1=ALU.mult)
                        ins = stt(out=b.bd(b.Kbd)[:, :, h, :], in0=c8(kT[:, G, :]), scalar=half(h), in1=s8(b.sc[6]),
                                  op0=ALU.mult, op1=ALU.mult)
                    ins.then_inc(sem("grams_in"), 1)
                    dve.wait_ge(sem("decays"), 5 * g + 5)
                    for h in range(2):
                        stt(out=b.bd(b.BhT)[:, :, h, :], in0=s8(b.sc[2]), scalar=half(h), in1=s8(b.sc[1]), op0=ALU.mult, op1=ALU.mult)
                        ins = stt(out=b.bd(b.KhT)[:, :, h, :], in0=c8(kT[:, G, :]), scalar=half(h), in1=s8(b.sc[1]),
                                  op0=ALU.mult, op1=ALU.mult)
                    ins.then_inc(sem("tails_ready"), 1)
                    do(v.memset(b.S, 0.0), sem("state_ready"))
                for g, si, b, bank in gs:
                    dve.wait_ge(sem("bonus_mm"), g + 1)
                    G = slice(2 * g, 2 * g + 2)
                    v.tensor_tensor(flat(rT[:, G, :]), flat(vT[:, G, :]), PS[:, bank + 1, :], ALU.mult).then_inc(sem("bonus_taken"), 1)
                for g, si, b, bank in gs:
                    for src, m1, m2, i in ((bank, b.N, b.Mb, 1), (bank + 2, b.Lk, b.Mk, 2)):
                        dve.wait_ge(sem("grams_mm"), 2 * g + i)
                        pv = PS[:, src:src + 2, :].rearrange("p b (m q t) -> p (b m) q t", m=4, q=2)
                        for h in range(2):
                            stt(out=b.bd(m1)[:, :, h, :], in0=pv[:, :, 0, :], scalar=half(h), in1=mid(cst("before"), 8),
                                op0=ALU.mult, op1=ALU.mult)
                            ins = stt(out=b.bd(m2)[:, :, h, :], in0=pv[:, :, 1, :], scalar=half(h), in1=mid(cst("upto"), 8),
                                      op0=ALU.mult, op1=ALU.mult)
                    ins.then_inc(sem("grams_taken"), 1)
                product = lambda bank: PS[:, bank:bank + 2, :].rearrange("p b (m n) -> p (b m) n", m=4)
                for lev in range(LEVELS):
                    for g, si, b, bank in gs:
                        dve.wait_ge(sem("LX_mm"), gp * 2 * LEVELS + 2 * lev + si + 1)
                        do(v.tensor_tensor(b.Z, product(bank), mid(cst(f"level{lev}"), 8), ALU.mult), sem("Z_ready"))
                    for g, si, b, bank in gs:
                        if lev == 0:
                            do(v.tensor_tensor(b.X, b.Z, mid(ident, 8), ALU.add), sem("X_ready"))
                        elif lev < LEVELS - 1:
                            dve.wait_ge(sem("XZ_mm"), gp * 2 * (LEVELS - 2) + 2 * (lev - 1) + si + 1)
                            do(v.tensor_tensor(b.X, b.X, product(bank + 2), ALU.add), sem("X_ready"))
                    for g, si, b, bank in gs:
                        dve.wait_ge(sem("ZY_mm"), gp * 2 * LEVELS + 2 * lev + si + 1)
                        do(v.tensor_tensor(b.Y, mid(ident, 8) if lev == 0 else b.Y, product(bank), ALU.add), sem("Y_ready"))
                for j in range(NCH - 1):
                    for g, si, b, bank in gs:
                        dve.wait_ge(sem("S_mm"), gp * 2 * (NCH - 1) + 2 * j + si + 1)
                        dve.wait_ge(sem("y_mm"), gp * 2 * NCH + 2 * j + si + 1)
                        for c in range(2):
                            ins = stt(out=b.S[:, c, :], in0=b.S[:, c, :], scalar=decayC[si][:, 4 * c + j:4 * c + j + 1],
                                      in1=PS[:, bank, c * P:(c + 1) * P], op0=ALU.mult, op1=ALU.add)
                        do(ins, sem("state_ready"))
                for g, si, b, bank in gs:
                    dve.wait_ge(sem("mean_mm"), g + 1)
                    do(stt(out=b.yT, in0=PS[:, bank + 2, :], scalar=-1.0 / HS, in1=b.yT, op0=ALU.mult, op1=ALU.add),
                       sem("y_centred"))
                for g, si, b, bank in gs:
                    dve.wait_ge(sem("var_mm"), g + 1)
                    do(v.tensor_scalar(b.sq, PS[:, bank + 3, :], 1.0 / HS, GN_EPS, ALU.mult, ALU.add), sem("gn_var"))
                for g, si, b, bank in gs:
                    G = slice(2 * g, 2 * g + 2)
                    dve.wait_ge(sem("gn_root"), g + 1)
                    do(v.reciprocal(b.sq, b.sq))
                    do(v.tensor_tensor(b.yT, b.yT, b.sq, ALU.mult))
                    for c in range(2):
                        f = 2 * g + c
                        ins = v.tensor_scalar(b.yT[:, c * S:(c + 1) * S], b.yT[:, c * S:(c + 1) * S],
                                              vec("lnw")[:, f:f + 1], vec("lnb")[:, f:f + 1], ALU.mult, ALU.add)
                    do(ins)
                    do(v.tensor_tensor(b.yT, b.yT, flat(rT[:, G, :]), ALU.add))
                    dve.wait_ge(sem("gate_mm"), g + 1)
                    do(v.tensor_tensor(flat(zT[:, G, :]), b.yT, PS[:, bank + 1, :], ALU.mult), sem("z_ready"))
            do(v.memset(negmax, 0.0), sem("scan_over"))

            added = [0]

            def add_to_x(banks):
                for q, bank in enumerate(banks):
                    h, n = divmod(q, NT)
                    dve.wait_ge(sem("x_mm"), added[0] + (q + 1))
                    ins = v.tensor_tensor(x[:, n, h * 512:(h + 1) * 512], x[:, n, h * 512:(h + 1) * 512], PS[:, bank, :], ALU.add)
                    do(ins, sem("x_added"))
                added[0] += 4

            add_to_x((0, 1, 2, 3))
            norm_scale(1, NORM_XN[1]).then_inc(sem("norm_scaled"), 1)
            norm_take(1, [(ffn_in, "g01")])
            for f in range(FT):
                dve.wait_ge(sem("ffn_silu"), f + 1)
                dve.wait_ge(sem("ffn_up_mm"), 2 * f + 2)
                v.tensor_tensor(actT[:, f, :], silu_sb[:, f % 4, :], PS[:, f % 4, S:2 * S], ALU.mult).then_inc(sem("ffn_hidden"), 1)
            dve.wait_ge(sem("x_mm"), 8)
            add_to_x((4, 5, 6, 7))
            norm_scale(2, NORM_XN[2]).then_inc(sem("norm_scaled"), 1)
            norm_take(2, [(kvT, "kvg"), (qinT, "g10")])
            sl = slopes()
            NI = NT * SLOTS

            def head_out(i):
                hs, qt = divmod(i, NT)
                dve.wait_ge(sem("prob_ready"), i + 1)
                do(v.reciprocal(rden[:, i % 2:i % 2 + 1], denom[:, i % 2:i % 2 + 1]))
                dve.wait_ge(sem("values_mm"), i + 1)
                v.tensor_scalar(oN[:, qt, hs * HS:(hs + 1) * HS], PS[:, 6 + i % 2, 0:HS], rden[:, i % 2:i % 2 + 1], None,
                                ALU.mult).then_inc(sem("head_out"), 1)

            dve.wait_ge(sem("dist_loaded"), 16)
            for i in range(NI):
                hs, qt = divmod(i, NT)
                nk = (qt + 1) * P
                dve.wait_ge(sem("scores_mm"), i + 1)
                if i >= 2:
                    dve.wait_ge(sem("probT_mm"), i - 1)
                sc = PS[:, 2 * (i % 2):2 * (i % 2) + 2, :].rearrange("p b n -> p (b n)")
                for br in range(3):
                    d0 = (3 * P if qt else 0) + br * nk
                    ins = stt(out=prob[i % 2][:, br * nk:(br + 1) * nk], in0=dist[:, d0:d0 + nk], scalar=float(sl[br, hs]),
                              in1=sc[:, br * nk:(br + 1) * nk], op0=ALU.mult, op1=ALU.add)
                do(ins, sem("scores_taken"))
                do(v.tensor_reduce(negmax[:, i % 2:i % 2 + 1], prob[i % 2][:, 0:3 * nk], X, ALU.max, negate=True), sem("max_ready"))
                if i >= 1:
                    head_out(i - 1)
            head_out(NI - 1)
            dve.wait_ge(sem("x_mm"), 12)
            for q, (n, h) in enumerate(((0, 0), (0, 1), (1, 0), (1, 1))):
                do(v.tensor_tensor(x[:, n, h * 512:(h + 1) * 512], x[:, n, h * 512:(h + 1) * 512], PS[:, 2 + 2 * h + n, :],
                                   ALU.add), sem("x_added"))
            norm_scale(3, hN).then_inc(sem("norm_scaled"), 1)
            norm_take(3, [(hTm, "g11")])
            dve.wait_ge(sem("router_loaded"), 32)
            dve.wait_ge(sem("logits_mm"), 1)
            for n in range(NT):
                l = logits[:, n, :]
                do(v.tensor_tensor(l, PS[:, 4, n * 8:n * 8 + 8], router_bias, ALU.add))
                ins = v.tensor_reduce(top[:, n:n + 1], l, X, ALU.max, negate=True)
            do(ins, sem("topneg_ready"))
            for n in range(NT):
                l = logits[:, n, :]
                do(v.tensor_tensor(beats, mid(l, NE), last(l, NE), ALU.is_gt))
                do(v.tensor_tensor(ties, mid(l, NE), last(l, NE), ALU.is_equal))
                do(v.tensor_tensor(ties, ties, cst("tie").rearrange("p (e j) -> p e j", e=NE), ALU.mult))
                do(v.tensor_tensor(beats, beats, ties, ALU.add))
                do(v.tensor_reduce(nrank, beats, X, ALU.add))
                ins = v.tensor_scalar(chosen[:, n, :], nrank, 2.0, None, ALU.is_lt)
            do(ins, sem("chosen_ready"))
            dve.wait_ge(sem("expl_ready"), 1)
            do(v.memset(gates, 0.0))
            for n in range(NT):
                do(v.tensor_tensor(expl[:, n, :], expl[:, n, :], chosen[:, n, :], ALU.mult))
                do(v.tensor_reduce(top[:, 2 + n:3 + n], expl[:, n, :], X, ALU.add))
                do(v.reciprocal(top[:, 4 + n:5 + n], top[:, 2 + n:3 + n]))
                for r in range(2):
                    do(v.tensor_scalar(gates[:, n, r * NE:(r + 1) * NE], expl[:, n, :], top[:, 4 + n:5 + n], None, ALU.mult))
            dve.wait_ge(sem("ranks_mm"), 1)
            do(v.memset(slotof, -1.0))
            for n in range(NT):
                do(v.tensor_tensor(nrank, PS[:, 5, 8 * n:8 * n + 8], chosen[:, n, :], ALU.mult))
                do(v.tensor_scalar(expl[:, n, :], chosen[:, n, :], 1000.0, -1000.0, ALU.mult, ALU.add))
                do(v.tensor_tensor(slotof[:, n, 0:NE], nrank, expl[:, n, :], ALU.add))
                do(v.tensor_scalar(slotof[:, n, NE:2 * NE], slotof[:, n, 0:NE], -float(P), None, ALU.add))
            do(v.tensor_reduce(top[:, 6:7], PS[:, 5, 16:24], X, ALU.max))
            do(v.tensor_scalar(overflow[:], top[:, 6:7], float(P), None, ALU.is_gt), sem("overflow_known"))

            def one_hot(i):
                for n in range(NT):
                    v.tensor_scalar(onehot[:, n, :], cst("slotid"), slotof[:, n, bass.ds(i, 1)], None, ALU.is_equal)
                    ins = v.tensor_scalar(gated[:, n, :], cst("slotid"), slotof[:, n, bass.ds(i, 1)],
                                          gates[:, n, bass.ds(i, 1)], ALU.is_equal, ALU.mult)
                ins.then_inc(sem("onehot_ready"), 1)

            def take_gathered(i, part):
                dve.wait_ge(sem("gather_mm"), 2 * i + (part + 1))
                v.tensor_tensor(gathered[part], PS[:, 7 - part, :].rearrange("p (k n) -> p k n", k=4),
                                last(vec("g11")[:, 4 * part:4 * part + 4], P), ALU.mult).then_inc(sem("gathered"), 1)
                dve.wait_ge(sem("gathered_high"), 2 * i + (part + 1))
                v.tensor_tensor(hTe_low[:, 4 * part:4 * part + 4, :], gathered[part], hTe_high[:, 4 * part:4 * part + 4, :],
                                ALU.subtract).then_inc(sem("gathered_low"), 1)

            def take_scatter_matrix(i):
                dve.wait_ge(sem("scatT_mm"), i + 1)
                v.tensor_copy(scatT, PS[:, 7, 0:2 * P]).then_inc(sem("scatT_ready"), 1)

            one_hot(0)
            take_gathered(0, 0)
            take_gathered(0, 1)
            take_scatter_matrix(0)

            def low(m, i):
                moe_unit_here(dve, m, i)
                dve.wait_ge(sem("high_ready"), PER_E * i + (m + 1))
                wh, wl = split_unit(m)
                v.tensor_tensor(wl, moe_unit(m), wh, ALU.subtract).then_inc(sem("low_ready"), 1)

            def expert(i, following):
                def hidden_low(j):
                    dve.wait_ge(sem("hidT_high"), ECH * i + (j + 1))
                    v.tensor_tensor(hidT_low, PS[:, 6, :].rearrange("p (f n) -> p f n", f=4), hidT_high,
                                    ALU.subtract).then_inc(sem("hidT_low"), 1)

                for j in range(ECH):
                    for key in (("w1", j, 0), ("w1", j, 1), ("w3", j, 0), ("w3", j, 1)):
                        if moe_at[key] >= PAIRS:
                            low(moe_at[key], i)
                    if j:
                        hidden_low(j - 1)
                        for h in range(2):
                            low(moe_at[("w2", j - 1, h)], i)
                    if j == 2:
                        one_hot(i + 1)
                    dve.wait_ge(sem("silu_ready"), ECH * i + (j + 1))
                    dve.wait_ge(sem("unit_used"), PER_E * i + (moe_at[("w3", j, 1)] + 1))
                    v.tensor_tensor(hidE, siluE, PS[:, 2 * (j % 2) + 1, :], ALU.mult).then_inc(sem("hidden_ready"), 1)
                for h in range(2):
                    low(moe_at[("w2", ECH - 1, h)], i)
                hidden_low(ECH - 1)
                if following:
                    low(0, i + 1)
                take_gathered(i + 1, 0)
                if following:
                    low(1, i + 1)
                    low(2, i + 1)
                take_gathered(i + 1, 1)
                for n in range(NT):
                    for h in range(2):
                        q = 2 * n + h
                        dve.wait_ge(sem("scatter_mm"), 4 * i + (q + 1))
                        xs = x[:, n, h * 512:(h + 1) * 512]
                        v.tensor_tensor(xs, xs, PS[:, (4, 5, 2, 3)[q], :], ALU.add).then_inc(sem("scattered"), 1)
                take_scatter_matrix(i + 1)
                dve.wait_ge(sem("scattered"), 4 * i + 4)
                dve.wait_ge(sem("scatT_ready"), i + 2)

            def experts(base):
                for m in range(PAIRS):
                    low(m, base)
                with dve.Fori(0, NE - 1) as e:
                    expert(e + base if base else e, True)
                expert(base + NE - 1, False)

            experts(0)
            dve.wait_ge(sem("overflow_known"), 1)
            more = dve.value_load(overflow[0:1, 0:1])
            with dve.If(more > 0):
                experts(NE)
            do(v.memset(ss, 0.0), sem("experts_over"))
            norm_scale(4, out_sb)
            do(v.memset(top[:, 7:8], 0.0))
            dve.wait_ge(sem("final_gain_loaded"), 16)
            for n in range(NT):
                v.tensor_tensor(out_sb[:, n, :], out_sb[:, n, :], final_gain, ALU.mult).then_inc(sem("out_ready"), 1)


_DIRECT = ["x", "rwkv_wr", "rwkv_wk", "rwkv_wv", "rwkv_w1", "rwkv_w2", "rwkv_a1", "rwkv_a2", "rwkv_g1", "rwkv_g2",
           "rwkv_wo", "w_kv", "attn_wq", "attn_wo", "ffn_w1", "ffn_w3", "ffn_w2", "moe_router", "moe_w1", "moe_w3", "moe_w2"]


def kernel(**inputs):
    import concourse.bacc as bacc
    from concourse.bass_utils import run_bass_kernel_spmd

    a = {k: np.ascontiguousarray(v) for k, v in inputs.items()}
    arrays = {n: a[n] for n in _DIRECT}
    named = {"g00": a["norm_gain"][0, 0], "g01": a["norm_gain"][0, 1], "g10": a["norm_gain"][1, 0],
             "g11": a["norm_gain"][1, 1], "kvg": a["kv_norm_gain"], "w0": a["rwkv_w0"][0], "a0": a["rwkv_a0"][0],
             "k_k": a["rwkv_k_k"][0], "k_a": a["rwkv_k_a"][0], "r_k": a["rwkv_r_k"][0].reshape(D),
             "lnw": a["rwkv_lnx_w"][0], "lnb": a["rwkv_lnx_b"][0]}
    for m in range(6):
        named[f"mu{m}"] = a["rwkv_mu"][0, m]
    arrays["vectors"] = np.ascontiguousarray(np.concatenate([named[n].reshape(KC, P).T for n in VECS], axis=1))
    arrays["final_gain_rows"] = np.ascontiguousarray(np.broadcast_to(a["final_norm_gain"], (P, D)))
    arrays["router_bias_rows"] = np.ascontiguousarray(np.broadcast_to(a["moe_router_bias"][0], (P, NE)))
    arrays["const_tables"] = np.ascontiguousarray(np.concatenate(list(constant_tables().values()), axis=1))
    arrays["distance_tables"] = distance_tables()

    nc = bacc.Bacc("TRN2", target_bir_lowering=False, num_devices=1)
    aps = {n: nc.dram_tensor(f"in_{n}", v.shape, mybir.dt.from_np(v.dtype), kind="ExternalInput").ap()
           for n, v in arrays.items()}
    out = nc.dram_tensor("out_x", (1, S, D), F32, kind="ExternalOutput").ap()
    trunk(nc, aps, out)
    r = run_bass_kernel_spmd(nc, [{f"in_{n}": v for n, v in arrays.items()}], core_ids=[0])
    return r.results[0]["out_x"]
```

```python
import math
from contextlib import ExitStack

import numpy as np

import concourse.bass as bass
from concourse import mybir

F32 = mybir.dt.float32
F32R = mybir.dt.float32r
I32 = mybir.dt.int32
ALU = mybir.AluOpType
ACT = mybir.ActivationFunctionType
X = mybir.AxisListType.X

P = 128
D = 1024
S = 256
NT = S // P
KC = D // P
HS = 64
CH = 64
NCH = S // CH
GROUPS = 4
LEVELS = 6
FF = 2816
FT = FF // P
FE = 3584
NE = 8
ECH = FE // 512
QD = 1536
QT_N = QD // P
SLOTS = 8
RING = 7
PAIRS = 3
FCH = -(-FT // 4)
LORA_COLS = ((0, 64), (64, 128), (128, 256))
LORA2_BANKS = (6, 7, 4, 5, 0, 1, 2, 3)
NORM_BANK = (4, 1)
WO_BANKS = (2, 3, 6, 7)
DOWN_BANKS = (6, 7, 2, 3)
UNIT = 2048
RMS_EPS = 1e-5
GN_EPS = 64e-5
BIG = -3.0e30
DECAY = -math.exp(-0.5)

VECS = ["g00", "g01", "g10", "g11", "kvg", "mu0", "mu1", "mu2", "mu3", "mu4", "mu5",
        "w0", "a0", "k_k", "k_a", "r_k", "lnw", "lnb"]
VCOL = {n: 8 * i for i, n in enumerate(VECS)}


def constant_tables():
    p = np.arange(P)
    s = p % CH
    t = np.arange(CH)
    tabs = {}
    tabs["ident"] = np.eye(P)
    tabs["ones"] = np.ones((P, P))
    tabs["headones"] = (p[:, None] // HS == p[None, :] // HS)
    tabs["before"] = s[:, None] < t[None, :]
    tabs["upto"] = s[:, None] <= t[None, :]
    for lev in range(LEVELS):
        m = 1 << lev
        tabs[f"level{lev}"] = ((p[:, None] // (2 * m) == p[None, :] // (2 * m))
                               & (p[:, None] // m % 2 == 1) & (p[None, :] // m % 2 == 0))
    tabs["eye64x2"] = s[:, None] == s[None, :]
    half = np.stack([p < HS, p >= HS], 1).astype(np.float64)
    tabs["half"] = half
    tabs["half8"] = half * HS ** -0.5
    tabs["earlier"] = p[:, None] < p[None, :]
    tabs["slotid"] = np.tile(p[None, :], (P, 1))
    e = np.arange(NE)
    tabs["tie"] = np.tile((e[None, :] < e[:, None]).reshape(1, -1), (P, 1))
    tabs["carry"] = np.tile((np.arange(512) % CH != 0)[None, :], (P, 1))
    return {k: v.astype(np.float32) for k, v in tabs.items()}


def distance_tables():
    out = []
    for qt in range(NT):
        q = qt * P + np.arange(P)[:, None]
        k = np.arange(P * (qt + 1))[None, :]
        dist = q - k
        for window, dil in ((128, 1), (512, 4), (2048, 16)):
            seen = (dist >= 0) & (dist % dil == 0) & (dist <= window)
            out.append(np.where(seen, -dist, BIG))
    return np.concatenate(out, 1).astype(np.float32)


def slopes():
    n = 3 * SLOTS
    return np.exp2(-8.0 * (np.arange(n, dtype=np.float32) + 1.0) / n).reshape(3, SLOTS)


CONST_SHAPES = {k: v.shape[1] for k, v in constant_tables().items()}
CCOL = {}
_at = 0
for _k, _n in CONST_SHAPES.items():
    CCOL[_k] = _at
    _at += _n
NCONST = _at
NDIST = 3 * P + 3 * 2 * P


class Own:

    def __init__(self, eng, sem):
        self.eng, self.sem, self.count = eng, sem, {}
        self.base = {}

    def do(self, ins, sem=None):
        key = sem if sem is not None else self.sem
        name = str(key)
        self.count[name] = self.count.get(name, 0) + 1
        ins.then_inc(key, 1)
        self.eng.wait_ge(key, self.base.get(name, 0) + self.count[name])

    def at(self, sem=None):
        return self.count.get(str(sem if sem is not None else self.sem), 0)


def trunk(nc, A, out):
    ctx = ExitStack()
    with ctx:
        def sb(name, shape, dt=F32):
            return ctx.enter_context(nc.sbuf_tensor(name, shape, dt))

        def sb_at(name, n):
            base = -(-nc.sbuf_base // 32) * 32
            t = sb(name, [P, n])
            return t, base

        def rounded(name, at, n):
            return nc.alloc_sbuf_tensor_at(name, [P, n], F32R, offset=at)

        sems = {}

        def sem(name):
            if name not in sems:
                sems[name] = ctx.enter_context(nc.semaphore(name))
            return sems[name]

        C = sb("consts", [P, NCONST])
        V = sb("vectors", [P, 8 * len(VECS)])
        x = sb("x_residual", [P, NT, D])
        SPLIT_AT = RING * UNIT
        EXTRA_AT = SPLIT_AT + 2 * PAIRS * UNIT
        BIG_N = EXTRA_AT + 5120
        BIGB, big_base = sb_at("ring_and_scan", BIG_N)
        PERS, pers_base = sb_at("phase_buffers", 8 * 2048 + 32)
        small = sb("small", [P, 256])
        PS = ctx.enter_context(nc.psum_tensor("psum", [P, 8, 512], F32))

        def cst(name):
            return C[:, CCOL[name]:CCOL[name] + CONST_SHAPES[name]]

        def vec(name):
            return V[:, VCOL[name]:VCOL[name] + 8]

        ident, ones = cst("ident"), cst("ones")

        def half(p):
            return C[:, CCOL["half"] + p:CCOL["half"] + p + 1]

        def half8(p):
            return C[:, CCOL["half8"] + p:CCOL["half8"] + p + 1]

        def pers(at, n):
            return PERS[:, at:at + n]

        HT_, L0_, L1_, R_, K_, A_, LD_, VN_ = [0] + [2080 + 2048 * i for i in range(7)]
        extra = BIGB[:, EXTRA_AT:BIG_N]

        gateT = sb("gateT", [P, S])
        loraT = [extra[:, 2048:2048 + S], extra[:, 2048 + S:2048 + 2 * S], gateT[:]]
        hT = pers(HT_, 8 * 257).rearrange("p (c t) -> p c t", c=8)
        lerp = extra[:, 3072:5120].rearrange("p (c t) -> p c t", c=8)
        mixed = [[rounded(f"mix_{w}_{q}", pers_base + 4 * o, 2048)[:, :].rearrange("p (c t) -> p c t", c=8)
                  for w, o in zip(("high", "low"), at)] for q, at in enumerate(((L0_, L1_), (A_, LD_)))]
        dxT = extra[:, 0:2048].rearrange("p (c t) -> p c t", c=8)
        rT, kT, aT, ldT = [pers(o, 2048).rearrange("p (c t) -> p c t", c=8) for o in (R_, K_, A_, LD_)]
        vT = pers(VN_, 2048).rearrange("p (c t) -> p c t", c=8)
        gate_w = pers(L1_, D)

        def nat(at):
            return pers(at, 2048).rearrange("p (n d) -> p n d", n=NT)

        def featT(at):
            return pers(at, 2048).rearrange("p (c t) -> p c t", c=8)

        ss = small[:, 0:2]
        std = small[:, 2:4]
        rstd = small[:, 4:6]
        one_minus_ka = small[:, 40:48]
        decayC = [small[:, 104 + 8 * i:112 + 8 * i] for i in range(GROUPS)]
        negmax, denom, rden = [small[:, 160 + 4 * i:163 + 4 * i] for i in range(3)]

        def w_slot(n):
            return BIGB[:, (n % RING) * UNIT:(n % RING + 1) * UNIT]

        def kview(w):
            return w.rearrange("(k p) n -> p k n", p=P)

        units = []
        free_at = []

        split_unit_of = []
        used_at = []

        def split_free(used=None):
            split_unit_of.append(len(units))
            used_at.append(used if used else
                           ("split_used", 1 + sum(name == "split_used" for name, _ in used_at)))
            return "split_low", len(used_at)

        def cols_units(w, c0, cw, free):
            per = UNIT // cw
            for k0 in range(0, KC, per):
                free_at.append(free if free else split_free())
                units.append([((per, cw), slice(0, per), None, kview(w)[:, k0:k0 + per, c0:c0 + cw])])

        wr, wk, wv, wo_r = (A[n][0] for n in ("rwkv_wr", "rwkv_wk", "rwkv_wv", "rwkv_wo"))
        for w in (wr, wk):
            for ch in range(2):
                cols_units(w, 512 * ch, 512, None)
        S_LORA1 = len(used_at)
        free_at.append(split_free())
        units.append([((8, 256), slice(0, 8), slice(0, 64), kview(A["rwkv_w1"][0])),
                      ((8, 256), slice(0, 8), slice(64, 128), kview(A["rwkv_a1"][0])),
                      ((8, 256), slice(0, 8), slice(128, 256), kview(A["rwkv_g1"][0]))])
        for ch in range(2):
            cols_units(wv, 512 * ch, 512, None)
        U_LORA2 = len(units)
        free_at.append(("lora2_mm", 8))
        units.append([("rows64", 0, A["rwkv_w2"][0]), ("rows64", 1, A["rwkv_a2"][0])])
        U_SCAN = len(units)
        S_FFN = len(used_at)
        for c0 in range(0, FF, 512):
            cw = min(512, FF - c0)
            for w in ("ffn_w1", "ffn_w3"):
                cols_units(A[w][0], c0, cw, None)
        S_FFN2 = len(used_at)
        assert S_FFN2 == S_FFN + 4 * FCH - 2
        for f0 in range(0, FT, 2):
            free_at.append(split_free(("x_mm", 8) if f0 == FT - 2 else None))
            units.append([((2, D), slice(0, 2), None, kview(A["ffn_w2"][0])[:, f0:f0 + 2, :])])
        S_ATT = len(used_at)
        for ch in range(2 * QD // 512):
            cols_units(A["w_kv"], 512 * ch, 512, None)
        for ch in range(QD // 512):
            cols_units(A["attn_wq"][0], 512 * ch, 512, None)
        U_MOE = len(units)

        slot_sem = [sem(f"slot{i}_loaded") for i in range(RING)]
        loaded_at = []
        slot_total = [0] * RING
        for n, u in enumerate(units):
            slot_total[n % RING] += 16 * len(u)
            loaded_at.append(slot_total[n % RING])

        def unit_cols(n, per, cw):
            return w_slot(n)[:, 0:per * cw].rearrange("p (k n) -> p k n", k=per)

        moe_order = []
        for j in range(ECH):
            moe_order += [("w1", j, 0), ("w1", j, 1), ("w3", j, 0), ("w3", j, 1)]
            if j:
                moe_order += [("w2", j - 1, 0), ("w2", j - 1, 1)]
        moe_order += [("w2", ECH - 1, 0), ("w2", ECH - 1, 1)]
        PER_E = len(moe_order)
        assert PER_E % RING == 0
        moe_at = {key: n for n, key in enumerate(moe_order)}
        REUSE = PER_E // RING

        def split_ahead(j):
            keys = [("w1", j, 0), ("w1", j, 1)] if j != 1 else []
            keys += [("w3", j, 0), ("w3", j, 1)]
            keys += [("w1", 1, 0), ("w1", 1, 1)] if j == 0 else []
            return [moe_at[key] for key in keys if moe_at[key] >= PAIRS]

        def weights_here(pe, n):
            pe.wait_ge(slot_sem[n % RING], loaded_at[n])

        def moe_slot(key):
            return (U_MOE + moe_at[key]) % RING

        def moe_unit(m):
            return unit_cols(U_MOE + m, 2, D) if moe_order[m][0] == "w2" else unit_cols(U_MOE + m, 4, 512)

        def moe_unit_here(eng, m, i):
            s = (U_MOE + m) % RING
            eng.wait_ge(slot_sem[s], 16 * REUSE * i + (slot_total[s] + 16 * (m // RING + 1)))

        def split_shape(s):
            return units[split_unit_of[s]][0][0]

        def pre_split(s):
            return [w[:, :].rearrange("p (k n) -> p k n", k=split_shape(s)[0]) for w in split[s % PAIRS]]

        class SetBuf:
            pass

        sets = []
        for si in range(2):
            o = [si * (BIG_N // 2)]

            def take(n):
                r = BIGB[:, o[0]:o[0] + n]
                o[0] += n
                return r

            b = SetBuf()
            bd = lambda v: v.rearrange("p (m h t) -> p m h t", m=8, h=2)
            full = lambda v: v.rearrange("p (m n) -> p m n", m=8)
            b.Abd, b.Rbd, b.BhN, b.KhN = [take(1024) for _ in range(4)]
            b.BhN, b.KhN = full(b.BhN), full(b.KhN)
            b.N, b.Lk, b.Mb, b.Mk = [take(1024) for _ in range(4)]
            b.Bbd, b.Kbd = [take(1024) for _ in range(2)]
            b.Z, b.X = full(b.Bbd), full(b.Kbd)
            b.Y, b.V, b.Yd = [full(take(1024)) for _ in range(3)]
            b.S, b.Sd, b.U0, b.U = [take(256).rearrange("p (c n) -> p c n", c=2) for _ in range(4)]
            b.yT, b.sq, b.gate = [take(512) for _ in range(3)]
            b.bd = bd
            b.full = full
            sets.append(b)
        assert o[0] <= BIG_N, o[0]

        compact = pers(HT_, 2048).rearrange("p (q g n) -> p q g n", q=2, g=2)
        compact_ar = pers(HT_, 2048).rearrange("p (q g m t) -> p q g m t", q=2, g=2, m=8)
        scale_buf = [pers(L0_ + 1024 + 512 * i, 512) for i in range(2)]
        rk_buf = [pers(L1_ + 1024 + 512 * i, 512) for i in range(2)]

        def groups(gp):
            return [(2 * gp + si, si, sets[si], 4 * si) for si in range(2)]

        def flat(v):
            return v.rearrange("p c t -> p (c t)")

        def c8(v):
            return v.rearrange("p c (j t) -> p (c j) t", t=CH)

        def s8(v):
            return v.rearrange("p (m t) -> p m t", t=CH)

        def bc(v, shape):
            return v.to_broadcast(shape)

        def mid(v, n):
            return v.unsqueeze(1).to_broadcast([P, n, v.shape[1]])

        def last(v, n):
            return v.unsqueeze(2).to_broadcast([P, v.shape[1], n])

        rwkv_wo = [[pers(o, 2048).rearrange("p (k n) -> p k n", k=4) for o in (K_ + 4096 * h, K_ + 4096 * h + 2048)]
                   for h in range(2)]
        zT = featT(L0_)

        def rounded_T(name, at, n=D // P):
            return rounded(name, at, n * S).rearrange("p (c t) -> p c t", c=n)

        in_pers = lambda at: pers_base + 4 * at
        in_extra = lambda at: big_base + 4 * (EXTRA_AT + at)
        ffn_raw = extra[:, 0:2048].rearrange("p (c t) -> p c t", c=8)
        ffn_in = [rounded_T("ffn_in_high", in_pers(K_)), rounded_T("ffn_in_low", in_pers(HT_))]
        silu_sb = [extra[:, 1024 * i:1024 * i + 1024].rearrange("p (b t) -> p b t", b=4) for i in range(2)]
        hidden = [extra[:, 2048 + 1024 * i:3072 + 1024 * i].rearrange("p (b t) -> p b t", b=4) for i in range(2)]
        actT = [rounded_T("ffn_hidden_high", in_pers(A_), FT), rounded_T("ffn_hidden_low", in_pers(L0_), FT)]
        kv_raw, q_raw = featT(LD_), featT(VN_)
        kv_in = [rounded_T("kv_in_high", in_pers(HT_)), rounded_T("kv_in_low", in_pers(L0_))]
        q_in = [rounded_T("q_in_high", in_extra(0)), rounded_T("q_in_low", in_extra(2048))]
        dist = pers(HT_, NDIST)
        kTa = pers(L1_, QT_N * S).rearrange("p (f t) -> p f t", f=QT_N)
        vNa = pers(L1_ + QT_N * S, NT * QD).rearrange("p (n d) -> p n d", n=NT)
        qTa = pers(L1_ + 2 * QT_N * S, QT_N * 2 * S).rearrange("p (f h t) -> p f h t", f=QT_N, h=2)
        prob = [extra[:, 0:768], extra[:, 768:1536], pers(HT_ + NDIST, 768)]
        probT = [extra[:, 1536 + 768 * i:1536 + 768 * i + 768] for i in range(2)]
        attn_wo = [w.rearrange("p (k n) -> p k n", k=2) for w in (extra[:, 3072:5120], pers(L1_, 2048))]
        oT = pers(L0_ + 1024, 4 * S).rearrange("p (c t) -> p c t", c=4)
        hN = nat(L1_)
        hTm = featT(K_)
        router = pers(HT_, 64).rearrange("p (k e) -> p k e", k=KC)
        router_bias = pers(HT_ + 64, 8)
        logits = pers(HT_ + 80, 16).rearrange("p (n e) -> p n e", n=NT)
        expl = pers(HT_ + 96, 16).rearrange("p (n e) -> p n e", n=NT)
        chosen = pers(HT_ + 112, 16).rearrange("p (n e) -> p n e", n=NT)
        gates = pers(HT_ + 128, 17 * NT).rearrange("p (n e) -> p n e", n=NT)
        slotof = pers(HT_ + 168, 17 * NT).rearrange("p (n e) -> p n e", n=NT)
        beats, ties = [pers(HT_ + 400 + 128 * i, 128).rearrange("p (n e j) -> p n e j", n=NT, e=NE) for i in range(2)]
        nrank = pers(HT_ + 656, 16).rearrange("p (n e) -> p n e", n=NT)
        top = pers(HT_ + 344, 8)
        overflow = sb("overflow", [P, 1], I32)
        final_gain = pers(HT_ + 1024, 1024)
        onehot = pers(L0_, 256).rearrange("p (n s) -> p n s", n=NT)
        gated = pers(L0_ + 256, 256).rearrange("p (n s) -> p n s", n=NT)
        scatT = pers(L0_ + 512, 256)
        siluE = pers(L0_ + 768, 512)
        hidE = pers(L0_ + 1280, 512)
        out_sb = nat(R_)
        hTe_high, hTe_low = [rounded(f"tokens_{w}", pers_base + 4 * (A_ + 1024 * q), 1024).rearrange("p (k n) -> p k n", k=KC)
                             for q, w in enumerate(("high", "low"))]
        hidT_high, hidT_low = [rounded(f"hidden_{w}", pers_base + 4 * (A_ + 2048 + 512 * q), 512)
                               .rearrange("p (f n) -> p f n", f=4) for q, w in enumerate(("high", "low"))]
        gathered = [pers(A_ + 3072 + 512 * q, 512).rearrange("p (k n) -> p k n", k=4) for q in range(2)]
        split = [[rounded(f"weights_{w}_{q}", big_base + 4 * (SPLIT_AT + (2 * q + z) * UNIT), UNIT)
                  for z, w in enumerate(("high", "low"))] for q in range(PAIRS)]

        def split_unit(m):
            k = 2 if moe_order[m][0] == "w2" else 4
            return [w[:, :].rearrange("p (k n) -> p k n", k=k) for w in split[m % PAIRS]]
        ySB = pers(LD_, 1024)
        NORM_XN = [nat(L0_), nat(L1_), nat(L1_), hN]
        SQUARES = [nat(L0_), nat(L1_), nat(L1_), extra[:, 0:2048].rearrange("p (n d) -> p n d", n=NT), nat(R_)]

        block = ctx.enter_context(nc.Block())

        @block.sync
        def _(sp):
            sp.dma_start(x[:], A["x"][0].rearrange("(n p) d -> p n d", p=P)).then_inc(sem("x_loaded"), 16)
            sp.dma_start(C[:], A["const_tables"]).then_inc(sem("consts_loaded"), 16)
            sp.dma_start(V[:], A["vectors"]).then_inc(sem("vectors_loaded"), 16)
            for n, u in enumerate(units):
                if n == U_SCAN:
                    sp.wait_ge(sem("K_ready"), GROUPS)
                    sp.wait_ge(sem("vbd_ready"), GROUPS)
                    sp.wait_ge(sem("bonus_taken"), GROUPS)
                    for ch in range(2):
                        for h in range(2):
                            sp.dma_start(rwkv_wo[h][ch], kview(wo_r)[:, 4 * h:4 * h + 4, 512 * ch:512 * ch + 512]
                                         ).then_inc(sem("rwkv_wo_loaded"), 16)
                    sp.wait_ge(sem("scan_over"), 1)
                if n >= RING:
                    sp.wait_ge(sem(free_at[n - RING][0]), free_at[n - RING][1])
                for part in u:
                    if part[0] == "rows64":
                        dst = w_slot(n)[0:64, part[1] * D:(part[1] + 1) * D]
                        src = part[2]
                    else:
                        (per, cw), ks, cs, src = part
                        dst = unit_cols(n, per, cw)[:, ks, cs if cs is not None else slice(0, cw)]
                    sp.dma_start(dst, src).then_inc(slot_sem[n % RING], 16)

            wview = {w: A[f"moe_{w}"].rearrange("a e (k p) n -> (a e) p k n", p=P) for w in ("w1", "w3")}
            w2_tiles = A["moe_w2"].rearrange("a e (k p) n -> p (a e k) n", p=P)

            def load_unit(e, m, name, value):
                w, j, h = moe_order[m]
                s = (U_MOE + m) % RING
                if w == "w2":
                    dst = unit_cols(s, 2, D)
                    src = w2_tiles[:, bass.ds(e * (FE // P) + 4 * j + 2 * h, 2), :]
                else:
                    dst = unit_cols(s, 4, 512)
                    src = wview[w][e, :, 4 * h:4 * h + 4, 512 * j:512 * j + 512]
                sp.wait_ge(sem(name), value)
                sp.dma_start(dst, src).then_inc(slot_sem[s], 16)

            def expert_units(e, i, ms):
                for m in ms:
                    load_unit(e, m, "low_ready", PER_E * i + (m - RING) % PER_E + 1)

            def stream_experts(i0):
                with sp.Fori(0, NE - 1) as e:
                    i = e + i0 if i0 else e
                    following = sp.snap(e + 1)
                    expert_units(e, i, range(RING, PER_E))
                    expert_units(following, i, range(RING))
                expert_units(NE - 1, i0 + NE - 1, range(RING, PER_E))

            for m in range(RING):
                load_unit(0, m, *free_at[U_MOE + m - RING])
            stream_experts(0)
            sp.wait_ge(sem("overflow_known"), 1)
            more = sp.value_load(overflow[0:1, 0:1])
            with sp.If(more > 0):
                expert_units(0, NE - 1, range(RING))
                stream_experts(NE)
            for n in range(NT):
                sp.wait_ge(sem("out_ready"), n + 1)
                sp.dma_start(out[0].rearrange("(n p) d -> p n d", p=P)[:, n, :],
                             out_sb[:, n, :]).then_inc(sem("out_stored"), 16)
            sp.wait_ge(sem("out_stored"), 16 * NT)

        @block.gpsimd
        def _(pool):
            pool.wait_ge(sem(used_at[S_LORA1][0]), used_at[S_LORA1][1])
            pool.dma_start(gate_w, A["rwkv_g2"][0]).then_inc(sem("gate_w_loaded"), 16)
            pool.wait_ge(sem(used_at[S_ATT + 11][0]), used_at[S_ATT + 11][1])
            pool.dma_start(dist[:], A["distance_tables"]).then_inc(sem("dist_loaded"), 16)
            pool.wait_ge(sem(used_at[-1][0]), used_at[-1][1])
            pool.dma_start(attn_wo[0], kview(A["attn_wo"][0])[:, 0:2, :]).then_inc(sem("attn_wo_loaded"), 16)
            pool.wait_ge(sem("scores_mm"), NT * SLOTS)
            pool.dma_start(attn_wo[1], kview(A["attn_wo"][0])[:, 2:4, :]).then_inc(sem("attn_wo_loaded"), 16)
            pool.wait_ge(sem("x_added"), 12)
            pool.dma_start(router, kview(A["moe_router"][0])).then_inc(sem("router_loaded"), 16)
            pool.dma_start(router_bias, A["router_bias_rows"]).then_inc(sem("router_loaded"), 16)
            pool.dma_start(final_gain, A["final_gain_rows"]).then_inc(sem("final_gain_loaded"), 16)

        @block.tensor
        def _(pe):
            mm = nc.tensor.matmul

            def norm_transposes(k):
                pe.wait_ge(sem("norm_scaled"), k + 1)
                src = NORM_XN[k]
                for b in range(4):
                    for q in range(4):
                        c, n = 2 * b + q // 2, q % 2
                        ins = nc.tensor.transpose(PS[:, b, q * P:(q + 1) * P], src[:, n, c * P:(c + 1) * P], ident)
                    ins.then_inc(sem("norm_transposed"), 1)

            pe.wait_ge(sem("consts_loaded"), 16)
            norm_transposes(0)

            def norm_sums(gp):
                for si in range(2):
                    g = 2 * gp + si
                    pe.wait_ge(sem("kk_squared"), g + 1)
                    if gp:
                        pe.wait_ge(sem("v_taken"), si + 1)
                    mm(PS[:, 4 * si + (0 if gp else NORM_BANK[si]), :], cst("headones"), scale_buf[si],
                       start=True, stop=True).then_inc(sem("kk_norm_mm"), 1)

            def split_products(s, jobs, used=True):
                pe.wait_ge(sem("split_low"), s + 1)
                for o_, (ah, al), (bh, bl), first, final in jobs:
                    mm(o_, ah, bh, start=first, stop=False)
                    mm(o_, ah, bl, start=False, stop=False)
                    ins = mm(o_, al, bh, start=False, stop=final)
                    if final and not used:
                        ins.then_inc(sem("x_mm"), 1)
                if used:
                    ins.then_inc(sem("split_used"), 1)

            def products_T(s, k0, nf, src, out):
                w = pre_split(s)
                per = split_shape(s)[0]
                split_products(s, [(out(f), [v[:, k, f * P:(f + 1) * P] for v in w], [v[:, k0 + k, :] for v in src],
                                    k0 + k == 0, k0 + k == KC - 1) for f in range(nf) for k in range(per)])

            def norm_sums(gp):
                for si in range(2):
                    g = 2 * gp + si
                    pe.wait_ge(sem("kk_squared"), g + 1)
                    if gp:
                        pe.wait_ge(sem("v_taken"), si + 1)
                    else:
                        pe.wait_ge(sem("proj_evac"), 8)
                    mm(PS[:, 4 * si + (0 if gp else NORM_BANK[si]), :], cst("headones"), scale_buf[si],
                       start=True, stop=True).then_inc(sem("kk_norm_mm"), 1)

            def proj_chunk(s0, mix, bank, hs=range(2)):
                for h in hs:
                    pe.wait_ge(sem("mix_low"), 2 * mix + h + 1)
                    products_T(s0 + h, 4 * h, 4, mixed[mix % 2], lambda f: PS[:, bank + f, 0:S])

            for t in range(4):
                if t >= 2:
                    pe.wait_ge(sem("proj_evac"), t - 1)
                proj_chunk(2 * t, t // 2, 4 * (t % 2))
            pe.wait_ge(sem("proj_evac"), 3)
            pe.wait_ge(sem("split_low"), S_LORA1 + 1)
            wh, wl = pre_split(S_LORA1)
            for i, (lo, hi) in enumerate(LORA_COLS):
                pe.wait_ge(sem("mix_low"), 2 * (2 + i) + 2)
                mh, ml = mixed[i % 2]
                for k in range(KC):
                    o_ = PS[0:hi - lo, i, 0:S]
                    mm(o_, wh[:, k, lo:hi], mh[:, k, :], start=(k == 0), stop=False)
                    mm(o_, wh[:, k, lo:hi], ml[:, k, :], start=False, stop=False)
                    ins = mm(o_, wl[:, k, lo:hi], mh[:, k, :], start=False, stop=(k == KC - 1))
                ins.then_inc(sem("lora1_mm" if i < 2 else "split_used"), 1)
            pe.wait_ge(sem("proj_evac"), 4)
            proj_chunk(S_LORA1 + 1, 5, 4)
            pe.wait_ge(sem("proj_evac"), 7)
            proj_chunk(S_LORA1 + 3, 5, 0, [0])
            norm_sums(0)
            proj_chunk(S_LORA1 + 3, 5, 0, [1])
            weights_here(pe, U_LORA2)
            for q, b in enumerate(LORA2_BANKS):
                i, f2 = divmod(q, 4)
                if q == 2:
                    pe.wait_ge(sem("kk_root"), 2)
                elif q == 4:
                    pe.wait_ge(sem("proj_evac"), 9)
                for fi in range(2):
                    f = 2 * f2 + fi
                    ins = mm(PS[:, b, fi * S:(fi + 1) * S],
                             w_slot(U_LORA2)[0:64, i * D + f * P:i * D + (f + 1) * P], loraT[i][0:64, :],
                             start=True, stop=True)
                ins.then_inc(sem("lora2_mm"), 1)

            def cols(bank, m):
                return PS[:, bank + m // 4, (m % 4) * P:(m % 4 + 1) * P]

            def blocks(v, m):
                return v[:, m * P:(m + 1) * P]

            def bonus_sums(gp):
                for g, si, b, bank in groups(gp):
                    pe.wait_ge(sem("rk_ready"), g + 1)
                    if gp == 0:
                        pe.wait_ge(sem("tails_taken"), 2 + si + 1)
                    mm(PS[:, bank + (3 if gp else 0), :], cst("headones"), rk_buf[si], start=True, stop=True
                       ).then_inc(sem("bonus_mm"), 1)

            def y_transposes(gp):
                for g, si, b, bank in groups(gp):
                    if gp < 1:
                        pe.wait_ge(sem("tails_taken"), 4 * (gp + 1) + si + 1)
                    for m in range(8):
                        ins = nc.tensor.transpose(cols(bank, m), b.Yd[:, m], ident)
                    ins.then_inc(sem("yT_mm"), 1)

            def mean_and_gate(gp):
                for g, si, b, bank in groups(gp):
                    if g == 0:
                        pe.wait_ge(sem("gate_w_loaded"), 16)
                    pe.wait_ge(sem("yT_ready"), g + 1)
                    if gp < 1:
                        pe.wait_ge(sem("v_taken"), g + 3)
                    mm(PS[:, bank, :], cst("headones"), b.yT, start=True, stop=True).then_inc(sem("mean_mm"), 1)
                    for c in range(2):
                        f = 2 * g + c
                        ins = mm(PS[:, bank + 1, c * S:(c + 1) * S], gate_w[:, f * P:(f + 1) * P], gateT[:],
                                 start=True, stop=True)
                    ins.then_inc(sem("gate_mm"), 1)

            def variance(gp):
                for g, si, b, bank in groups(gp):
                    pe.wait_ge(sem("y_squared"), g + 1)
                    mm(PS[:, bank, :], cst("headones"), b.sq, start=True, stop=True).then_inc(sem("var_mm"), 1)

            def output_product(ks):
                for k in ks:
                    if k == 0:
                        pe.wait_ge(sem("rwkv_wo_loaded"), 16 * 4)
                    pe.wait_ge(sem("z_ready"), k // 2 + 1)
                    for n in range(NT):
                        for ch in range(2):
                            ins = mm(PS[:, WO_BANKS[2 * n + ch], :], zT[:, k, n * P:(n + 1) * P],
                                     rwkv_wo[k // 4][ch][:, k % 4, :], start=(k == 0), stop=(k == KC - 1))
                            if k == KC - 1:
                                ins.then_inc(sem("x_mm"), 1)

            def LX(gp, lev):
                for g, si, b, bank in groups(gp):
                    if lev:
                        pe.wait_ge(sem("X_ready"), gp * 2 * (LEVELS - 1) + 2 * (lev - 1) + si + 1)
                        pe.wait_ge(sem("Y_ready"), gp * 2 * LEVELS + 2 * (lev - 1) + si + 1)
                    else:
                        pe.wait_ge(sem("b_masked"), g + 1)
                    for m in range(8):
                        if lev:
                            ins = mm(cols(bank + 2, m), blocks(b.N, m), b.X[:, m], start=True, stop=True)
                        else:
                            ins = nc.tensor.transpose(cols(bank + 2, m), blocks(b.N, m), ident)
                    ins.then_inc(sem("LX_mm"), 1)

            def ZY(gp, lev):
                for g, si, b, bank in groups(gp):
                    pe.wait_ge(sem("Z_ready"), gp * 2 * LEVELS + 2 * lev + si + 1)
                    for m in range(8):
                        if lev:
                            ins = mm(cols(bank + 2, m), b.Z[:, m], b.Y[:, m], start=True, stop=True)
                        else:
                            ins = nc.tensor.transpose(cols(bank + 2, m), b.Z[:, m], ident)
                    ins.then_inc(sem("ZY_mm"), 1)

            for gp in range(2):
                gs = groups(gp)
                for g, si, b, bank in gs:
                    pe.wait_ge(sem("B_ready"), g + 1)
                    if gp:
                        pe.wait_ge(sem("bonus_taken"), g + 1)
                    if gp:
                        pe.wait_ge(sem("y_taken"), 2 * NCH * gp - 1 + si)
                    for m in range(8):
                        ins = mm(cols(bank + 2, m).rearrange("p (q t) -> p q t", q=2), blocks(b.Bbd, m),
                                 compact_ar[:, :, si, m, :], start=True, stop=True)
                    ins.then_inc(sem("gram_b_mm"), 1)
                for g, si, b, bank in gs:
                    for m in range(8):
                        ins = nc.tensor.transpose(cols(bank, m), blocks(b.Bbd, m), ident)
                    ins.then_inc(sem("tailsT_mm"), 1)
                if gp:
                    y_transposes(gp - 1)
                for g, si, b, bank in gs:
                    pe.wait_ge(sem("K_ready"), g + 1)
                    pe.wait_ge(sem("tails_taken"), 4 * gp + si + 1)
                    if gp:
                        pe.wait_ge(sem("yT_ready"), g - 1)
                    for m in range(8):
                        ins = mm(cols(bank, m).rearrange("p (q t) -> p q t", q=2), blocks(b.Kbd, m),
                                 compact_ar[:, :, si, m, :], start=True, stop=True)
                    ins.then_inc(sem("gram_k_mm"), 1)
                LX(gp, 0)
                ZY(gp, 0)
                for g, si, b, bank in gs:
                    pe.wait_ge(sem("k_masked"), g + 1)
                    for m in range(8):
                        ins = nc.tensor.transpose(cols(bank, m), blocks(b.Kbd, m), ident)
                    ins.then_inc(sem("tailsT_mm"), 1)
                if gp == 0:
                    bonus_sums(0)
                for g, si, b, bank in gs:
                    pe.wait_ge(sem("vbd_ready"), g + 1)
                    if gp == 0:
                        pe.wait_ge(sem("bonus_taken"), g + 1)
                    pe.wait_ge(sem("tails_taken"), 4 * gp + 2 + si + 1)
                    for m in range(8):
                        ins = nc.tensor.transpose(cols(bank, m), b.V[:, m], ident)
                    ins.then_inc(sem("v_mm"), 1)
                for lev in range(1, LEVELS):
                    LX(gp, lev)
                    if gp == 0 and lev == 1:
                        norm_sums(1)
                    if gp and lev == 1:
                        mean_and_gate(gp - 1)
                    if lev < LEVELS - 1:
                        if gp and lev == 1:
                            variance(gp - 1)
                        for g, si, b, bank in gs:
                            pe.wait_ge(sem("Z_ready"), gp * 2 * LEVELS + 2 * lev + si + 1)
                            if lev == 1:
                                pe.wait_ge(sem("v_taken"), g + 1)
                                if gp == 0:
                                    pe.wait_ge(sem("kk_root"), g + 3)
                                else:
                                    pe.wait_ge(sem("gn_var"), g - 1)
                                    pe.wait_ge(sem("gate_taken"), g - 1)
                            for m in range(8):
                                ins = mm(cols(bank, m), b.Y[:, m], b.Z[:, m], start=True, stop=True)
                            ins.then_inc(sem("XZ_mm"), 1)
                    ZY(gp, lev)
                for j in range(NCH):
                    q0 = gp * 2 * NCH + 2 * j
                    for g, si, b, bank in gs:
                        if j == 0:
                            pe.wait_ge(sem("Y_ready"), gp * 2 * LEVELS + 2 * (LEVELS - 1) + si + 1)
                            pe.wait_ge(sem("ARbd_ready"), g + 1)
                        pe.wait_ge(sem("state_ready"), gp * 2 * NCH + 2 * j + si + 1)
                        for c in range(2):
                            m = 4 * c + j
                            o_ = PS[:, bank + 1, c * P:(c + 1) * P]
                            mm(o_, blocks(b.Abd, m), b.S[:, c], start=True, stop=False)
                            ins = mm(o_, blocks(b.Lk, m), b.V[:, m], start=False, stop=True)
                        ins.then_inc(sem("U0_mm"), 1)
                    for g, si, b, bank in gs:
                        pe.wait_ge(sem("U0_ready"), q0 + si + 1)
                        for c in range(2):
                            ins = mm(PS[:, bank + 1, S + c * P:S + (c + 1) * P], b.Y[:, 4 * c + j], b.U0[:, c],
                                     start=True, stop=True)
                        ins.then_inc(sem("U_mm"), 1)
                    if gp == 0 and j == 1:
                        bonus_sums(1)
                    for g, si, b, bank in gs:
                        pe.wait_ge(sem("U_ready"), q0 + si + 1)
                        if j < NCH - 1:
                            for c in range(2):
                                m = 4 * c + j
                                o_ = PS[:, bank, c * P:(c + 1) * P]
                                mm(o_, b.BhN[:, m], b.U[:, c], start=True, stop=False)
                                ins = mm(o_, b.KhN[:, m], b.V[:, m], start=False, stop=True)
                            ins.then_inc(sem("S_mm"), 1)
                        if j:
                            pe.wait_ge(sem("y_taken"), q0 + si - 1)
                        for c in range(2):
                            m = 4 * c + j
                            o_ = PS[:, bank + 2, c * P:(c + 1) * P]
                            mm(o_, blocks(b.Rbd, m), b.S[:, c], start=True, stop=False)
                            mm(o_, blocks(b.Mb, m), b.U[:, c], start=False, stop=False)
                            ins = mm(o_, blocks(b.Mk, m), b.V[:, m], start=False, stop=True)
                        ins.then_inc(sem("y_mm"), 1)
            for g, si, b, bank in groups(1):
                pe.wait_ge(sem("y_taken"), 2 * NCH * 2 - 1 + si)
            y_transposes(1)
            mean_and_gate(1)
            output_product(range(0, 1))
            variance(1)
            output_product(range(1, KC))

            norm_transposes(1)
            s = S_FFN
            for c in range(FCH):
                nf, per = split_shape(s)[1] // P, split_shape(s)[0]
                if c >= 2:
                    pe.wait_ge(sem("ffn_hidden"), c - 1)
                for which in range(2):
                    for h in range(KC // per):
                        if c == 0 and which == 0:
                            pe.wait_ge(sem("in_low"), h + 1)
                        products_T(s, h * per, nf, ffn_in,
                                   lambda f: PS[:, 4 * (c % 2) + f, which * S:(which + 1) * S])
                        s += 1
            pe.wait_ge(sem("ffn_hidden"), FCH - 1)
            for i in range(FT // 2):
                pe.wait_ge(sem("ffn_low"), i // 2 + 1)
                w = pre_split(s)
                split_products(s, [(PS[:, DOWN_BANKS[2 * n + h], :],
                                    [v[:, 2 * i + k, n * P:(n + 1) * P] for v in actT],
                                    [v[:, k, h * 512:(h + 1) * 512] for v in w],
                                    i == 0 and k == 0, i == FT // 2 - 1 and k == 1)
                                   for k in range(2) for n in range(NT) for h in range(2)], used=i < FT // 2 - 1)
                s += 1

            norm_transposes(2)
            for t in range(9):
                if t >= 2:
                    pe.wait_ge(sem("att_proj_evac"), t - 1)
                src = kv_in if t < 6 else q_in
                for h in range(2):
                    if t in (0, 6):
                        pe.wait_ge(sem("in_low"), 2 + (2 if t else 0) + h + 1)
                    if t // 3 == 1:
                        w = pre_split(s)
                        split_products(s, [(PS[:, 4 * (t % 2) + n, :], [v[:, 4 * h + k, n * P:(n + 1) * P] for v in src],
                                            [v[:, k, :] for v in w], h == 0 and k == 0, h == 1 and k == 3)
                                           for n in range(NT) for k in range(4)])
                    else:
                        products_T(s, 4 * h, 4, src, lambda f: PS[:, 4 * (t % 2) + f, 0:S])
                    s += 1
            pe.wait_ge(sem("att_proj_evac"), 9)
            NI = NT * SLOTS

            def scores(i):
                hs, qt = divmod(i, NT)
                nk = (qt + 1) * P
                if i >= 2:
                    pe.wait_ge(sem("scores_taken"), i - 1)
                o_ = PS[:, 2 * (i % 2):2 * (i % 2) + 2, :].rearrange("p b n -> p (b n)")
                for br in range(3):
                    f = 4 * br + hs // 2
                    ins = mm(o_[:, br * nk:(br + 1) * nk], qTa[:, f, hs % 2, qt * P:(qt + 1) * P], kTa[:, f, 0:nk],
                             start=True, stop=True)
                ins.then_inc(sem("scores_mm"), 1)

            def prob_transposes(i):
                nb = 3 * (i % 2 + 1)
                pe.wait_ge(sem("prob_ready"), i + 1)
                if i >= 1:
                    pe.wait_ge(sem("probT_ready"), i)
                o_ = PS[:, 4:6, :].rearrange("p b n -> p (b n)")
                for q in range(nb):
                    ins = nc.tensor.transpose(o_[:, q * P:(q + 1) * P], prob[i % 3][:, q * P:(q + 1) * P], ident)
                ins.then_inc(sem("probT_mm"), 1)

            def values(i):
                hs, qt = divmod(i, NT)
                pe.wait_ge(sem("probT_ready"), i + 1)
                if i % 4 == 0 and i >= 8:
                    pe.wait_ge(sem("oT_ready"), i // 4 - 1)
                nb = 3 * (qt + 1)
                rows = slice(HS * (hs % 2), HS * (hs % 2 + 1))
                for q in range(nb):
                    br, kt = divmod(q, qt + 1)
                    col = (br * SLOTS + hs) * HS
                    ins = mm(PS[rows, 6 + i // 4 % 2, qt * P:(qt + 1) * P], vNa[:, kt, col:col + HS],
                             probT[i % 2][:, q * P:(q + 1) * P], start=(q == 0), stop=(q == nb - 1))
                ins.then_inc(sem("values_mm"), 1)

            scores(0)
            scores(1)
            for i in range(NI):
                if i + 2 < NI:
                    scores(i + 2)
                prob_transposes(i)
                if i >= 1:
                    values(i - 1)
            values(NI - 1)
            pe.wait_ge(sem("oT_ready"), NI // 4)
            pe.wait_ge(sem("attn_wo_loaded"), 32)
            for n in range(NT):
                for h in range(2):
                    for k in range(4):
                        ins = mm(PS[:, 2 + 2 * h + n, :], oT[:, k, n * P:(n + 1) * P],
                                 attn_wo[k // 2][:, k % 2, h * 512:(h + 1) * 512],
                                 start=(k == 0), stop=(k == 3))
                    ins.then_inc(sem("x_mm"), 1)

            norm_transposes(3)
            pe.wait_ge(sem("normT_ready"), 20)
            pe.wait_ge(sem("router_loaded"), 32)
            for n in range(NT):
                for k in range(KC):
                    ins = mm(PS[:, 4, n * 8:n * 8 + 8], hTm[:, k, n * P:(n + 1) * P], router[:, k, :],
                             start=(k == 0), stop=(k == KC - 1))
            ins.then_inc(sem("logits_mm"), 1)
            pe.wait_ge(sem("chosen_ready"), 1)
            mm(PS[:, 5, 0:8], cst("earlier"), chosen[:, 0, :], start=True, stop=True)
            mm(PS[:, 5, 8:16], cst("earlier"), chosen[:, 1, :], start=True, stop=False)
            mm(PS[:, 5, 8:16], ones, chosen[:, 0, :], start=False, stop=True)
            mm(PS[:, 5, 16:24], ones, chosen[:, 0, :], start=True, stop=False)
            mm(PS[:, 5, 16:24], ones, chosen[:, 1, :], start=False, stop=True).then_inc(sem("ranks_mm"), 1)

            def gather(i, part):
                bank = 7 - part
                for k in range(4):
                    for n in range(NT):
                        ins = mm(PS[:, bank, k * P:(k + 1) * P], hN[:, n, (4 * part + k) * P:(4 * part + k + 1) * P],
                                 onehot[:, n, :], start=(n == 0), stop=(n == NT - 1))
                ins.then_inc(sem("gather_mm"), 1)

            def scatter_matrix():
                for n in range(NT):
                    ins = nc.tensor.transpose(PS[:, 7, n * P:(n + 1) * P], gated[:, n, :], ident)
                ins.then_inc(sem("scatT_mm"), 1)

            def experts(base):
                with pe.Fori(0, NE) as e:
                    i = e + base if base else e

                    def product(m, out, highs, lows, first, final):
                        pe.wait_ge(sem("low_ready"), PER_E * i + (m + 1))
                        wh, wl = split_unit(m)
                        for k in range(len(highs)):
                            for h, o_ in enumerate(out):
                                cs = slice(h * 512, (h + 1) * 512)
                                mm(o_, highs[k], wh[:, k, cs], start=(first and k == 0), stop=False)
                                mm(o_, highs[k], wl[:, k, cs], start=False, stop=False)
                                ins = mm(o_, lows[k], wh[:, k, cs], start=False, stop=(final and k == len(highs) - 1))
                        ins.then_inc(sem("unit_used"), 1)

                    def up(j, which):
                        if which == 0:
                            if j == 0:
                                pe.wait_ge(sem("gathered_low"), 2 * i + 2)
                            elif j == 1:
                                pe.wait_ge(sem("scatT_ready"), i + 1)
                            else:
                                pe.wait_ge(sem("hidden_ready"), ECH * i + (j - 1))
                        for h in range(2):
                            ks = range(4 * h, 4 * h + 4)
                            product(moe_at[(("w1", "w3")[which], j, h)], [PS[:, 2 * (j % 2) + which, :]],
                                    [hTe_high[:, k, :] for k in ks], [hTe_low[:, k, :] for k in ks], h == 0, h == 1)

                    def hidden_transposes(j):
                        pe.wait_ge(sem("hidden_ready"), ECH * i + (j + 1))
                        for q in range(4):
                            ins = nc.tensor.transpose(PS[:, 6, q * P:(q + 1) * P], hidE[:, q * P:(q + 1) * P], ident)
                        ins.then_inc(sem("hidT_mm"), 1)

                    def down(j):
                        pe.wait_ge(sem("hidT_low"), ECH * i + (j + 1))
                        for h in range(2):
                            qs = range(2 * h, 2 * h + 2)
                            product(moe_at[("w2", j, h)], [PS[:, 4, :], PS[:, 5, :]],
                                    [hidT_high[:, q, :] for q in qs], [hidT_low[:, q, :] for q in qs],
                                    j == 0 and h == 0, j == ECH - 1 and h == 1)

                    for j in range(ECH):
                        up(j, 0)
                        if j:
                            hidden_transposes(j - 1)
                        up(j, 1)
                        if j:
                            down(j - 1)
                    hidden_transposes(ECH - 1)
                    pe.wait_ge(sem("onehot_ready"), i + 2)
                    gather(i, 0)
                    down(ECH - 1)
                    gather(i, 1)
                    pe.wait_ge(sem("y_ready"), i + 1)
                    for n in range(NT):
                        for h in range(2):
                            mm(PS[:, (4, 5, 2, 3)[2 * n + h], :], scatT[:, n * P:(n + 1) * P], ySB[:, h * 512:(h + 1) * 512],
                               start=True, stop=True).then_inc(sem("scatter_mm"), 1)
                    pe.wait_ge(sem("gathered_low"), 2 * i + 3)
                    scatter_matrix()

            pe.wait_ge(sem("onehot_ready"), 1)
            gather(0, 0)
            gather(0, 1)
            pe.wait_ge(sem("gathered_low"), 1)
            scatter_matrix()
            experts(0)
            pe.wait_ge(sem("overflow_known"), 1)
            more = pe.value_load(overflow[0:1, 0:1])
            with pe.If(more > 0):
                experts(NE)

        @block.scalar
        def _(act):
            a_ = nc.scalar.activation

            def norm_stats(k, added=0):
                for n in range(NT):
                    if added:
                        act.wait_ge(sem("x_added"), added - 2 * (NT - 1 - n))
                    ins = a_(SQUARES[k][:, n, :], x[:, n, :], ACT.Square, accum_out=ss[:, n:n + 1])
                ins.then_inc(sem("squares_summed"), 1)
                act.wait_ge(sem("mean_ready"), k + 1)
                a_(std, ss, ACT.Sqrt).then_inc(sem("root_ready"), 1)

            act.wait_ge(sem("x_loaded"), 16)
            norm_stats(0)

            two_banks = lambda bank: PS[:, bank:bank + 2, :].rearrange("p b n -> p (b n)")
            allof = lambda v: v.rearrange("p m n -> p (m n)")

            def squares(gp):
                for g, si, b, bank in groups(gp):
                    act.wait_ge(sem("kk_ready"), g + 1)
                    a_(scale_buf[si], compact[:, 0, si, :], ACT.Square).then_inc(sem("kk_squared"), 1)

            def roots(gp):
                for g, si, b, bank in groups(gp):
                    act.wait_ge(sem("kk_norm_mm"), g + 1)
                    a_(scale_buf[si], PS[:, bank + (0 if gp else NORM_BANK[si]), :], ACT.Sqrt).then_inc(sem("kk_root"), 1)

            act.wait_ge(sem("vectors_loaded"), 16)

            def take(dst, src, func=ACT.Copy, **kw):
                return a_(dst, src, func, **kw)

            def split_high(s):
                if s < len(used_at):
                    n = split_unit_of[s]
                    weights_here(act, n)
                    if s >= PAIRS:
                        act.wait_ge(sem(used_at[s - PAIRS][0]), used_at[s - PAIRS][1])
                    a_(pre_split(s)[0], unit_cols(n, *split_shape(s)), ACT.Copy).then_inc(sem("split_high"), 1)

            def mix_high(i):
                if i >= 2:
                    name, value = (used_at[3], used_at[7], ("lora1_mm", 1), ("lora1_mm", 2))[i - 2]
                    act.wait_ge(sem(name), value)
                for h in range(2):
                    act.wait_ge(sem("lerp_ready"), 2 * i + h + 1)
                    ks = slice(4 * h, 4 * h + 4)
                    a_(mixed[i % 2][0][:, ks, :], lerp[:, ks, :], ACT.Copy).then_inc(sem("mix_high"), 1)

            def take_chunk(dst, ch, s, bank):
                act.wait_ge(sem(used_at[s][0]), used_at[s][1])
                take(dst[:, 4 * ch:4 * ch + 4, :], PS[:, bank:bank + 4, 0:S]).then_inc(sem("proj_evac"), 1)

            def take_lora(i, name, value, func):
                act.wait_ge(sem(name), value)
                rows = LORA_COLS[i][1] - LORA_COLS[i][0]
                take(loraT[i][0:rows, :], PS[0:rows, i, 0:S], func).then_inc(sem("proj_evac"), 1)

            split_high(0)
            split_high(1)
            mix_high(0)
            split_high(2)
            mix_high(1)
            split_high(3)
            take_chunk(rT, 0, 1, 0)
            split_high(4)
            split_high(5)
            take_chunk(rT, 1, 3, 4)
            mix_high(2)
            split_high(6)
            split_high(7)
            take_chunk(kT, 0, 5, 0)
            split_high(8)
            split_high(9)
            take_chunk(kT, 1, 7, 4)
            mix_high(3)
            split_high(10)
            mix_high(4)
            take_lora(0, "lora1_mm", 1, ACT.Tanh)
            mix_high(5)
            take_lora(1, "lora1_mm", 2, ACT.Copy)
            take_lora(2, *used_at[S_LORA1], ACT.Sigmoid)
            split_high(11)
            squares(0)
            split_high(12)
            take_chunk(vT, 0, 10, 4)
            roots(0)
            take_chunk(vT, 1, 12, 0)
            for q, b in enumerate(LORA2_BANKS):
                i, f2 = divmod(q, 4)
                act.wait_ge(sem("lora2_mm"), q + 1)
                for fi in range(2):
                    c = 2 * f2 + fi
                    ins = take((ldT, aT)[i][:, c, :], PS[:, b, fi * S:(fi + 1) * S], ACT.Sigmoid,
                               bias=vec(("w0", "a0")[i])[:, c:c + 1])
                ins.then_inc(sem("proj_evac"), 1)

            def decays(gp):
                for g, si, b, bank in groups(gp):
                    cum, before = compact[:, 1, si, :], flat(ldT[:, 2 * g:2 * g + 2, :])
                    act.wait_ge(sem("cum_before"), g + 1)
                    a_(before, before, ACT.Exp).then_inc(sem("decays"), 1)
                    a_(decayC[g], s8(cum)[:, :, CH - 1], ACT.Exp).then_inc(sem("decays"), 1)
                    act.wait_ge(sem("kk_scaled"), g + 1)
                    a_(scale_buf[si], cum, ACT.Exp, scale=-1.0).then_inc(sem("decays"), 1)
                    act.wait_ge(sem("decays"), 4 * g + 3)
                    a_(cum, cum, ACT.Exp).then_inc(sem("decays"), 1)

            def take_y(gp):
                for g, si, b, bank in groups(gp):
                    act.wait_ge(sem("yT_mm"), g + 1)
                    pv = two_banks(bank).rearrange("p (m h t) -> p m h t", m=8, h=2)
                    for h in range(2):
                        r = slice(h * HS, (h + 1) * HS)
                        ins = a_(s8(b.yT)[r], pv[r, :, h, :], ACT.Copy)
                    ins.then_inc(sem("yT_ready"), 1)

            def take_gate(gp):
                for g, si, b, bank in groups(gp):
                    act.wait_ge(sem("gate_mm"), g + 1)
                    a_(b.gate, PS[:, bank + 1, :], ACT.Copy).then_inc(sem("gate_taken"), 1)

            def y_squares(gp):
                for g, si, b, bank in groups(gp):
                    act.wait_ge(sem("y_centred"), g + 1)
                    a_(b.sq, b.yT, ACT.Square).then_inc(sem("y_squared"), 1)

            def gn_roots(gp):
                for g, si, b, bank in groups(gp):
                    act.wait_ge(sem("gn_var"), g + 1)
                    a_(b.sq, b.sq, ACT.Sqrt).then_inc(sem("gn_root"), 1)

            def expand_v(gp):
                for g, si, b, bank in groups(gp):
                    for h in range(2):
                        ins = a_(b.V[:, :, h * CH:(h + 1) * CH], c8(vT[:, 2 * g:2 * g + 2, :]), ACT.Copy, scale=half(h))
                    ins.then_inc(sem("vbd_ready"), 1)

            def expand_ar(gp):
                for g, si, b, bank in groups(gp):
                    act.wait_ge(sem("AR_ready"), g + 1)
                    for h in range(2):
                        a_(b.bd(b.Abd)[:, :, h, :], compact_ar[:, 0, si], ACT.Copy, scale=half(h))
                        ins = a_(b.bd(b.Rbd)[:, :, h, :], compact_ar[:, 1, si], ACT.Copy, scale=half(h))
                    ins.then_inc(sem("ARbd_ready"), 1)

            decays(0)
            act.wait_ge(sem("scan_open"), 1)
            expand_v(0)
            expand_ar(0)
            for gp in range(2):
                gs = groups(gp)
                for g, si, b, bank in gs:
                    act.wait_ge(sem("tailsT_mm"), 4 * gp + si + 1)
                    a_(allof(b.BhN), two_banks(bank), ACT.Copy).then_inc(sem("tails_taken"), 1)
                if gp:
                    take_y(gp - 1)
                if gp:
                    expand_v(gp)
                for g, si, b, bank in gs:
                    act.wait_ge(sem("tailsT_mm"), 4 * gp + 2 + si + 1)
                    a_(allof(b.KhN), two_banks(bank), ACT.Copy).then_inc(sem("tails_taken"), 1)
                for g, si, b, bank in gs:
                    act.wait_ge(sem("v_mm"), g + 1)
                    a_(allof(b.V), two_banks(bank), ACT.Copy).then_inc(sem("v_taken"), 1)
                if gp:
                    y_squares(gp - 1)
                    take_gate(gp - 1)
                    gn_roots(gp - 1)
                if gp:
                    expand_ar(gp)
                if gp == 0:
                    squares(1)
                    roots(1)
                    decays(1)
                for j in range(NCH):
                    q0 = gp * 2 * NCH + 2 * j
                    for g, si, b, bank in gs:
                        act.wait_ge(sem("U0_mm"), q0 + si + 1)
                        a_(b.U0.rearrange("p c n -> p (c n)"), PS[:, bank + 1, 0:S], ACT.Copy).then_inc(sem("U0_ready"), 1)
                    for g, si, b, bank in gs:
                        act.wait_ge(sem("U_mm"), q0 + si + 1)
                        a_(b.U.rearrange("p c n -> p (c n)"), PS[:, bank + 1, S:2 * S], ACT.Copy).then_inc(sem("U_ready"), 1)
                    for g, si, b, bank in gs:
                        act.wait_ge(sem("y_mm"), q0 + si + 1)
                        a_(b.Yd.rearrange("p (c j) n -> p c j n", c=2)[:, :, j, :],
                           PS[:, bank + 2, 0:2 * P].rearrange("p (c n) -> p c n", c=2), ACT.Copy).then_inc(sem("y_taken"), 1)
            take_y(1)
            y_squares(1)
            take_gate(1)
            gn_roots(1)

            def input_high(i, dst, src, ready):
                for h in range(2):
                    act.wait_ge(sem("normT_ready"), ready[h])
                    a_(dst[:, 4 * h:4 * h + 4, :], src[:, 4 * h:4 * h + 4, :], ACT.Copy).then_inc(sem("in_high"), 1)

            for s in range(S_FFN, S_FFN + PAIRS):
                split_high(s)
            norm_stats(1, 4)
            input_high(0, ffn_in[0], ffn_raw, (6, 8))
            s = S_FFN + PAIRS

            def ffn_banks(c, which):
                nf = min(4, FT - 4 * c)
                return PS[:, 4 * (c % 2):4 * (c % 2) + nf, which * S:(which + 1) * S], nf

            for c in range(FCH):
                last_s = min(S_FFN + 4 * c + 3, S_FFN2 - 1)
                while s < last_s + PAIRS:
                    split_high(s)
                    s += 1
                act.wait_ge(sem("split_used"), last_s + 1)
                b, nf = ffn_banks(c, 0)
                a_(silu_sb[c % 2][:, 0:nf, :], b, ACT.Silu).then_inc(sem("ffn_silu"), 1)
                split_high(s)
                s += 1
                act.wait_ge(sem("ffn_hidden"), c + 1)
                a_(actT[0][:, 4 * c:4 * c + nf, :], hidden[c % 2][:, 0:nf, :], ACT.Copy).then_inc(sem("ffn_high"), 1)
            while s < S_ATT + PAIRS - 1:
                split_high(s)
                s += 1

            norm_stats(2, 8)
            input_high(1, kv_in[0], kv_raw, (11, 15))
            split_high(s)
            s += 1
            input_high(2, q_in[0], q_raw, (16, 16))
            for t in range(9):
                last_s = S_ATT + 2 * t + 1
                while s < last_s + PAIRS:
                    split_high(s)
                    s += 1
                act.wait_ge(sem(used_at[last_s][0]), used_at[last_s][1])
                b0 = 4 * (t % 2)
                if t // 3 == 1:
                    ins = a_(vNa[:, :, (t - 3) * 512:(t - 2) * 512], PS[:, b0:b0 + 2, :], ACT.Copy)
                elif t < 3:
                    ins = a_(kTa[:, 4 * t:4 * t + 4, :], PS[:, b0:b0 + 4, 0:S], ACT.Copy)
                else:
                    for h in range(2):
                        ins = a_(qTa[:, 4 * (t - 6):4 * (t - 6) + 4, h, :], PS[:, b0:b0 + 4, 0:S], ACT.Copy, scale=half8(h))
                ins.then_inc(sem("att_proj_evac"), 1)

            def first_highs(i):
                for m in range(PAIRS):
                    moe_unit_here(act, m, i)
                    if i:
                        act.wait_ge(sem("unit_used"), PER_E * i)
                    else:
                        act.wait_ge(sem(used_at[-1][0]), used_at[-1][1])
                    a_(split_unit(m)[0], moe_unit(m), ACT.Copy).then_inc(sem("high_ready"), 1)

            def softmax_exp(i):
                n = 3 * P * (i % 2 + 1)
                act.wait_ge(sem("max_ready"), i + 1)
                a_(prob[i % 3][:, 0:n], prob[i % 3][:, 0:n], ACT.Exp, bias=negmax[:, i % 3:i % 3 + 1],
                   accum_out=denom[:, i % 3:i % 3 + 1]).then_inc(sem("exp_ready"), 1)

            NI = NT * SLOTS
            softmax_exp(0)
            for i in range(NI):
                n = 3 * P * (i % 2 + 1)
                act.wait_ge(sem("rden_ready"), i + 1)
                a_(prob[i % 3][:, 0:n], prob[i % 3][:, 0:n], ACT.Copy, scale=rden[:, i % 3:i % 3 + 1]).then_inc(sem("prob_ready"), 1)
                if i + 1 < NI:
                    softmax_exp(i + 1)
                act.wait_ge(sem("probT_mm"), i + 1)
                if i >= 2:
                    act.wait_ge(sem("values_mm"), i - 1)
                a_(probT[i % 2][:, 0:n], PS[:, 4:6, :].rearrange("p b n -> p (b n)")[:, 0:n],
                   ACT.Copy).then_inc(sem("probT_ready"), 1)
            first_highs(0)
            norm_stats(3, 12)
            act.wait_ge(sem("topneg_ready"), 1)
            for n in range(NT):
                ins = a_(expl[:, n, :], logits[:, n, :], ACT.Exp, bias=top[:, n:n + 1])
            ins.then_inc(sem("expl_ready"), 1)

            def gathered_high(i, part):
                act.wait_ge(sem("gathered"), 2 * i + (part + 1))
                a_(hTe_high[:, 4 * part:4 * part + 4, :], gathered[part], ACT.Copy).then_inc(sem("gathered_high"), 1)

            def high(m, i):
                moe_unit_here(act, m, i)
                act.wait_ge(sem("unit_used"), PER_E * i + (m - PAIRS + 1))
                a_(split_unit(m)[0], moe_unit(m), ACT.Copy).then_inc(sem("high_ready"), 1)

            def expert(i, following):
                def take_hidden(j):
                    act.wait_ge(sem("hidT_mm"), ECH * i + (j + 1))
                    if j:
                        act.wait_ge(sem("unit_used"), PER_E * i + (moe_at[("w2", j - 1, 1)] + 1))
                    a_(hidT_high, PS[:, 6, :].rearrange("p (f n) -> p f n", f=4), ACT.Copy).then_inc(sem("hidT_high"), 1)

                for j in range(ECH):
                    for m in split_ahead(j)[:2 if j == 0 else None]:
                        high(m, i)
                    act.wait_ge(sem("unit_used"), PER_E * i + (moe_at[("w1", j, 1)] + 1))
                    if j:
                        act.wait_ge(sem("hidden_ready"), ECH * i + j)
                    a_(siluE, PS[:, 2 * (j % 2), :], ACT.Silu).then_inc(sem("silu_ready"), 1)
                    if j == 0:
                        high(split_ahead(0)[2], i)
                    if j:
                        take_hidden(j - 1)
                        for h in range(2):
                            high(moe_at[("w2", j - 1, h)], i)
                for h in range(2):
                    high(moe_at[("w2", ECH - 1, h)], i)
                take_hidden(ECH - 1)
                if following:
                    high(0, i + 1)
                gathered_high(i + 1, 0)
                if following:
                    high(1, i + 1)
                act.wait_ge(sem("unit_used"), PER_E * i + PER_E)
                a_(ySB, PS[:, 4:6, :].rearrange("p b n -> p (b n)"), ACT.Copy).then_inc(sem("y_ready"), 1)
                gathered_high(i + 1, 1)
                if following:
                    high(2, i + 1)

            def experts(base):
                if base:
                    first_highs(base)
                with act.Fori(0, NE - 1) as e:
                    expert(e + base if base else e, True)
                expert(base + NE - 1, False)

            gathered_high(0, 0)
            gathered_high(0, 1)
            experts(0)
            act.wait_ge(sem("overflow_known"), 1)
            more = act.value_load(overflow[0:1, 0:1])
            with act.If(more > 0):
                experts(NE)
            act.wait_ge(sem("experts_over"), 1)
            norm_stats(4)

        @block.vector
        def _(dve):
            v = nc.vector
            own = Own(dve, sem("dve_step"))
            do = own.do

            def norm_scale(k, dst):
                dve.wait_ge(sem("squares_summed"), k + 1)
                do(v.tensor_scalar(ss, ss, 1.0 / D, RMS_EPS, ALU.mult, ALU.add), sem("mean_ready"))
                dve.wait_ge(sem("root_ready"), k + 1)
                do(v.reciprocal(rstd, std))
                for n in range(NT):
                    ins = v.tensor_scalar(dst[:, n, :], x[:, n, :], rstd[:, n:n + 1], None, ALU.mult)
                return ins

            def norm_take(k, targets):
                for b in range(4):
                    dve.wait_ge(sem("norm_transposed"), 4 * k + b + 1)
                    for t, (dst, gain) in enumerate(targets):
                        do(v.tensor_tensor(dst[:, 2 * b:2 * b + 2, :], PS[:, b, :].rearrange("p (c t) -> p c t", c=2),
                                           last(vec(gain)[:, 2 * b:2 * b + 2], S), ALU.mult), sem("normT_ready"))

            do(v.memset(hT[:, :, 0:1], 0.0))
            norm_scale(0, NORM_XN[0]).then_inc(sem("norm_scaled"), 1)
            dve.wait_ge(sem("vectors_loaded"), 16)
            norm_take(0, [(hT[:, :, 1:S + 1], "g00")])
            do(v.tensor_tensor(dxT, hT[:, :, 0:S], hT[:, :, 1:S + 1], ALU.subtract))
            def split_low(s):
                if s < len(used_at):
                    n = split_unit_of[s]
                    weights_here(dve, n)
                    dve.wait_ge(sem("split_high"), s + 1)
                    wh, wl = pre_split(s)
                    v.tensor_tensor(wl, unit_cols(n, *split_shape(s)), wh, ALU.subtract).then_inc(sem("split_low"), 1)

            def mix(i):
                mu = (0, 2, 1, 4, 5, 3)[i]
                if i:
                    dve.wait_ge(sem("mix_low"), 2 * i)
                for h in range(2):
                    for c in range(4 * h, 4 * h + 4):
                        ins = v.scalar_tensor_tensor(out=lerp[:, c, :], in0=dxT[:, c, :], scalar=vec(f"mu{mu}")[:, c:c + 1],
                                                     in1=hT[:, c, 1:S + 1], op0=ALU.mult, op1=ALU.add)
                    ins.then_inc(sem("lerp_ready"), 1)
                for h in range(2):
                    dve.wait_ge(sem("mix_high"), 2 * i + h + 1)
                    ks = slice(4 * h, 4 * h + 4)
                    v.tensor_tensor(mixed[i % 2][1][:, ks, :], lerp[:, ks, :], mixed[i % 2][0][:, ks, :], ALU.subtract
                                    ).then_inc(sem("mix_low"), 1)

            split_low(0)
            mix(0)
            split_low(1)
            mix(1)
            for s in (2, 3, 4, 5):
                split_low(s)
            mix(2)
            for s in (6, 7, 8, 9):
                split_low(s)
            mix(3)
            split_low(10)
            mix(4)
            mix(5)
            split_low(11)
            do(v.tensor_scalar(one_minus_ka, vec("k_a"), -1.0, 1.0, ALU.mult, ALU.add))
            stt = v.scalar_tensor_tensor
            two = lambda w: w.rearrange("p (c t) -> p c t", c=2)
            product = lambda bank: PS[:, bank:bank + 2, :].rearrange("p b (m n) -> p (b m) n", m=4)

            def scale_k(gs):
                for g, si, b, bank in gs:
                    G = slice(2 * g, 2 * g + 2)
                    if g > 1:
                        dve.wait_ge(sem("ARbd_ready"), g - 1)
                    do(v.tensor_tensor(two(compact[:, 0, si, :]), kT[:, G, :], last(vec("k_k")[:, G], S), ALU.mult), sem("kk_ready"))

            def mix_a(gs):
                for g, si, b, bank in gs:
                    rk = rk_buf[si]
                    for c in range(2):
                        ins = v.tensor_scalar(rk[:, c * S:(c + 1) * S], aT[:, 2 * g + c, :],
                                              vec("k_a")[:, 2 * g + c:2 * g + c + 1],
                                              one_minus_ka[:, 2 * g + c:2 * g + c + 1], ALU.mult, ALU.add)
                    do(ins)

            def mix_k(gs):
                for g, si, b, bank in gs:
                    G = slice(2 * g, 2 * g + 2)
                    rk = rk_buf[si]
                    do(v.tensor_tensor(flat(kT[:, G, :]), flat(kT[:, G, :]), rk, ALU.mult))
                    do(v.tensor_tensor(rk, flat(rT[:, G, :]), flat(kT[:, G, :]), ALU.mult))
                    do(v.tensor_tensor(two(rk), two(rk), last(vec("r_k")[:, G], S), ALU.mult), sem("rk_ready"))

            def sum_decays(gs):
                for g, si, b, bank in gs:
                    ld, cum = flat(ldT[:, 2 * g:2 * g + 2, :]), compact[:, 1, si, :]
                    do(v.tensor_scalar(ld, ld, DECAY, None, ALU.mult))
                    do(v.tensor_tensor_scan(cum, cst("carry"), ld, 0.0, ALU.mult, ALU.add))
                    do(v.tensor_tensor(ld, cum, ld, ALU.subtract), sem("cum_before"))

            def halves(view, h):
                return view[:, h * S:(h + 1) * S]

            def invert_norm(gs, hs=range(2)):
                for g, si, b, bank in gs:
                    dve.wait_ge(sem("kk_root"), g + 1)
                    for h in hs:
                        n = halves(scale_buf[si], h)
                        do(v.tensor_scalar(n, n, 1e-12, None, ALU.max))
                        do(v.reciprocal(n, n))

            def norm_k(gs):
                for g, si, b, bank in gs:
                    kk = compact[:, 0, si, :]
                    do(v.tensor_tensor(kk, kk, scale_buf[si], ALU.mult), sem("kk_scaled"))

            def make_b(gs):
                for g, si, b, bank in gs:
                    a = flat(aT[:, 2 * g:2 * g + 2, :])
                    do(v.tensor_tensor(a, compact[:, 0, si, :], a, ALU.mult))

            def bonus(gs):
                for g, si, b, bank in gs:
                    dve.wait_ge(sem("bonus_mm"), g + 1)
                    G = slice(2 * g, 2 * g + 2)
                    v.tensor_tensor(flat(rT[:, G, :]), flat(vT[:, G, :]), PS[:, bank + (3 if g > 1 else 0), :], ALU.mult
                                    ).then_inc(sem("bonus_taken"), 1)

            def decay_arb(gs):
                for g, si, b, bank in gs:
                    G = slice(2 * g, 2 * g + 2)
                    a = flat(aT[:, G, :])
                    dve.wait_ge(sem("decays"), 4 * g + 1)
                    stt(out=compact[:, 0, si, :], in0=compact[:, 0, si, :], scalar=-1.0, in1=flat(ldT[:, G, :]),
                        op0=ALU.mult, op1=ALU.mult)
                    dve.wait_ge(sem("decays"), 4 * g + 3)
                    v.tensor_tensor(a, a, scale_buf[si], ALU.mult).then_inc(sem("b_decayed"), 1)
                    dve.wait_ge(sem("decays"), 4 * g + 4)
                    v.tensor_tensor(compact[:, 1, si, :], flat(rT[:, G, :]), compact[:, 1, si, :], ALU.mult
                                    ).then_inc(sem("AR_ready"), 1)

            def decay_k(gs):
                for g, si, b, bank in gs:
                    k = flat(kT[:, 2 * g:2 * g + 2, :])
                    v.tensor_tensor(k, k, scale_buf[si], ALU.mult).then_inc(sem("k_decayed"), 1)

            def expand(gs, which):
                src, decayed, ready = ((aT, "b_decayed", "B_ready"), (kT, "k_decayed", "K_ready"))[which]
                for g, si, b, bank in gs:
                    dve.wait_ge(sem(decayed), g + 1)
                    dve.wait_ge(sem("AR_ready"), g + 1)
                    if g > 1:
                        dve.wait_ge(sem("ZY_mm"), 2 * LEVELS)
                    for h in range(2):
                        ins = v.tensor_scalar(b.bd((b.Bbd, b.Kbd)[which])[:, :, h, :], c8(src[:, 2 * g:2 * g + 2, :]),
                                              half(h), None, ALU.mult)
                    ins.then_inc(sem(ready), 1)

            def mask(gp, which):
                for g, si, b, bank in groups(gp):
                    m1, m2 = ((b.N, b.Mb), (b.Lk, b.Mk))[which]
                    dve.wait_ge(sem(("gram_b_mm", "gram_k_mm")[which]), g + 1)
                    src = bank + 2 - 2 * which
                    pv = PS[:, src:src + 2, :].rearrange("p b (m q t) -> p (b m) q t", m=4, q=2)
                    for h in range(2):
                        stt(out=b.bd(m1)[:, :, h, :], in0=pv[:, :, 0, :], scalar=half(h), in1=mid(cst("before"), 8),
                            op0=ALU.mult, op1=ALU.mult)
                        ins = stt(out=b.bd(m2)[:, :, h, :], in0=pv[:, :, 1, :], scalar=half(h), in1=mid(cst("upto"), 8),
                                  op0=ALU.mult, op1=ALU.mult)
                    ins.then_inc(sem(("b_masked", "k_masked")[which]), 1)

            def take_Z(gp, lev):
                for g, si, b, bank in groups(gp):
                    dve.wait_ge(sem("LX_mm"), gp * 2 * LEVELS + 2 * lev + si + 1)
                    do(v.tensor_tensor(b.Z, product(bank + 2), mid(cst(f"level{lev}"), 8), ALU.mult), sem("Z_ready"))

            def grow_X(gp, lev):
                for g, si, b, bank in groups(gp):
                    if lev == 0:
                        dve.wait_ge(sem("tailsT_mm"), 4 * gp + 2 + si + 1)
                        do(v.tensor_tensor(b.X, b.Z, mid(ident, 8), ALU.add), sem("X_ready"))
                    elif lev < LEVELS - 1:
                        dve.wait_ge(sem("XZ_mm"), gp * 2 * (LEVELS - 2) + 2 * (lev - 1) + si + 1)
                        do(v.tensor_tensor(b.X, b.X, product(bank), ALU.add), sem("X_ready"))

            def grow_Y(gp, lev):
                for g, si, b, bank in groups(gp):
                    dve.wait_ge(sem("ZY_mm"), gp * 2 * LEVELS + 2 * lev + si + 1)
                    do(v.tensor_tensor(b.Y, mid(ident, 8) if lev == 0 else b.Y, product(bank + 2), ALU.add), sem("Y_ready"))

            def centre(gp):
                for g, si, b, bank in groups(gp):
                    dve.wait_ge(sem("mean_mm"), g + 1)
                    do(stt(out=b.yT, in0=PS[:, bank, :], scalar=-1.0 / HS, in1=b.yT, op0=ALU.mult, op1=ALU.add),
                       sem("y_centred"))

            def take_variance(gp):
                for g, si, b, bank in groups(gp):
                    dve.wait_ge(sem("var_mm"), g + 1)
                    do(v.tensor_scalar(b.sq, PS[:, bank, :], 1.0 / HS, GN_EPS, ALU.mult, ALU.add), sem("gn_var"))

            def invert_deviation(gs, hs=range(2)):
                for g, si, b, bank in gs:
                    dve.wait_ge(sem("gn_root"), g + 1)
                    for h in hs:
                        do(v.reciprocal(halves(b.sq, h), halves(b.sq, h)))

            def scale_y(gs):
                for g, si, b, bank in gs:
                    do(v.tensor_tensor(b.yT, b.yT, b.sq, ALU.mult))
                    for c in range(2):
                        f = 2 * g + c
                        ins = v.tensor_scalar(b.yT[:, c * S:(c + 1) * S], b.yT[:, c * S:(c + 1) * S],
                                              vec("lnw")[:, f:f + 1], vec("lnb")[:, f:f + 1], ALU.mult, ALU.add)
                    do(ins)

            def finish_z(gs):
                for g, si, b, bank in gs:
                    G = slice(2 * g, 2 * g + 2)
                    do(v.tensor_tensor(b.yT, b.yT, flat(rT[:, G, :]), ALU.add))
                    dve.wait_ge(sem("gate_taken"), g + 1)
                    do(v.tensor_tensor(flat(zT[:, G, :]), b.yT, b.gate, ALU.mult), sem("z_ready"))

            dve.wait_ge(sem(used_at[S_LORA1][0]), used_at[S_LORA1][1])
            first, second = groups(0), groups(1)
            dve.wait_ge(sem("proj_evac"), 4)
            scale_k(first)
            split_low(12)
            invert_norm(first)
            norm_k(first)
            dve.wait_ge(sem("proj_evac"), 13)
            sum_decays(first)
            dve.wait_ge(sem("lora2_mm"), 8)
            dve.wait_ge(sem("proj_evac"), 17)
            do(v.memset(negmax, 0.0), sem("scan_open"))
            mix_a(first)
            make_b(first)
            decay_arb(first)
            expand(first, 0)
            mix_k(first)
            decay_k(first)
            expand(first, 1)
            for gp in range(2):
                gs = groups(gp)
                mask(gp, 0)
                for g, si, b, bank in gs:
                    v.memset(b.Sd, 0.0)
                    do(v.memset(b.S, 0.0), sem("state_ready"))
                for g, si, b, bank in gs:
                    dve.wait_ge(sem("tailsT_mm"), 4 * gp + si + 1)
                take_Z(gp, 0)
                mask(gp, 1)
                grow_Y(gp, 0)
                grow_X(gp, 0)
                if gp == 0:
                    bonus(first)
                    scale_k(second)
                for lev in range(1, LEVELS):
                    take_Z(gp, lev)
                    if gp and lev == 1:
                        centre(gp - 1)
                        take_variance(gp - 1)
                    grow_X(gp, lev)
                    if gp == 0:
                        if lev == 1:
                            mix_a(second)
                        elif lev == 2:
                            invert_norm([second[0]], [1])
                        elif lev == 3:
                            invert_norm([second[1]], [0])
                        elif lev == 4:
                            norm_k([second[1]])
                        else:
                            sum_decays([second[1]])
                    elif lev in (2, 3):
                        invert_deviation([first[lev - 2]], [0])
                    elif lev in (4, 5):
                        scale_y([first[lev - 4]])
                    grow_Y(gp, lev)
                    if gp == 0:
                        if lev == 1:
                            invert_norm([second[0]], [0])
                        elif lev == 2:
                            norm_k([second[0]])
                        elif lev == 3:
                            invert_norm([second[1]], [1])
                        elif lev == 4:
                            sum_decays([second[0]])
                        else:
                            mix_k([second[0]])
                    elif lev in (2, 3):
                        invert_deviation([first[lev - 2]], [1])
                    elif lev in (4, 5):
                        finish_z([first[lev - 4]])
                if gp == 0:
                    mix_k([second[1]])
                for j in range(NCH - 1):
                    for g, si, b, bank in gs:
                        dve.wait_ge(sem("S_mm"), gp * 2 * (NCH - 1) + 2 * j + si + 1)
                        dve.wait_ge(sem("y_mm"), gp * 2 * NCH + 2 * j + si + 1)
                        d = lambda c: decayC[g][:, 4 * c + j:4 * c + j + 1]
                        for c in range(2):
                            ins = stt(out=b.S[:, c, :], in0=PS[:, bank, c * P:(c + 1) * P], scalar=d(c),
                                      in1=b.Sd[:, c, :], op0=ALU.mult, op1=ALU.add)
                        do(ins, sem("state_ready"))
                    if j < NCH - 2:
                        for g, si, b, bank in gs:
                            for c in range(2):
                                ins = v.tensor_scalar(b.Sd[:, c, :], b.S[:, c, :],
                                                      decayC[g][:, 4 * c + j + 1:4 * c + j + 2], None, ALU.mult)
                            do(ins)
                    if gp == 0:
                        if j == 0:
                            make_b(second)
                            decay_arb([second[0]])
                        elif j == 1:
                            decay_arb([second[1]])
                            expand(second, 0)
                        else:
                            decay_k(second)
                            bonus(second)
                            expand(second, 1)
            centre(1)
            take_variance(1)
            for g in second:
                invert_deviation([g])
                scale_y([g])
                finish_z([g])
            do(v.memset(negmax, 0.0), sem("scan_over"))

            added = [0]

            def add_to_x(banks, between=None):
                for q, bank in enumerate(banks):
                    if q == 2 and between:
                        between()
                    n, h = divmod(q, 2)
                    dve.wait_ge(sem("x_mm"), added[0] + (q + 1))
                    ins = v.tensor_tensor(x[:, n, h * 512:(h + 1) * 512], x[:, n, h * 512:(h + 1) * 512], PS[:, bank, :], ALU.add)
                    do(ins, sem("x_added"))
                added[0] += 4

            def input_low(i, dst, src):
                for h in range(2):
                    dve.wait_ge(sem("in_high"), 2 * i + h + 1)
                    ks = slice(4 * h, 4 * h + 4)
                    v.tensor_tensor(dst[1][:, ks, :], src[:, ks, :], dst[0][:, ks, :], ALU.subtract).then_inc(sem("in_low"), 1)

            add_to_x(WO_BANKS, between=lambda: (split_low(S_FFN), split_low(S_FFN + 1)))
            norm_scale(1, NORM_XN[1]).then_inc(sem("norm_scaled"), 1)
            split_low(S_FFN + 2)
            norm_take(1, [(ffn_raw, "g01")])
            input_low(0, ffn_in, ffn_raw)
            s = S_FFN + PAIRS
            for c in range(FCH):
                last_s = min(S_FFN + 4 * c + 3, S_FFN2 - 1)
                while s < last_s + PAIRS:
                    split_low(s)
                    s += 1
                nf = min(4, FT - 4 * c)
                dve.wait_ge(sem("ffn_silu"), c + 1)
                dve.wait_ge(sem("split_used"), last_s + 1)
                v.tensor_tensor(hidden[c % 2][:, 0:nf, :], silu_sb[c % 2][:, 0:nf, :],
                                PS[:, 4 * (c % 2):4 * (c % 2) + nf, S:2 * S], ALU.mult).then_inc(sem("ffn_hidden"), 1)
                split_low(s)
                s += 1
                dve.wait_ge(sem("ffn_high"), c + 1)
                fs = slice(4 * c, 4 * c + nf)
                dve.wait_ge(sem("ffn_hidden"), c + 1)
                v.tensor_tensor(actT[1][:, fs, :], hidden[c % 2][:, 0:nf, :], actT[0][:, fs, :],
                                ALU.subtract).then_inc(sem("ffn_low"), 1)
            while s < S_ATT + PAIRS - 1:
                split_low(s)
                s += 1
            add_to_x(DOWN_BANKS)
            norm_scale(2, NORM_XN[2]).then_inc(sem("norm_scaled"), 1)
            norm_take(2, [(kv_raw, "kvg"), (q_raw, "g10")])
            input_low(1, kv_in, kv_raw)
            split_low(s)
            s += 1
            input_low(2, q_in, q_raw)
            while s < len(used_at):
                split_low(s)
                s += 1
            def low(m, i):
                moe_unit_here(dve, m, i)
                dve.wait_ge(sem("high_ready"), PER_E * i + (m + 1))
                wh, wl = split_unit(m)
                v.tensor_tensor(wl, moe_unit(m), wh, ALU.subtract).then_inc(sem("low_ready"), 1)

            sl = slopes()
            NI = NT * SLOTS

            def invert_denominator(i):
                dve.wait_ge(sem("exp_ready"), i + 1)
                do(v.reciprocal(rden[:, i % 3:i % 3 + 1], denom[:, i % 3:i % 3 + 1]), sem("rden_ready"))

            def take_output(c):
                dve.wait_ge(sem("values_mm"), 4 * c + 4)
                v.tensor_copy(oT[:, c, :], PS[:, 6 + c % 2, 0:S]).then_inc(sem("oT_ready"), 1)

            dve.wait_ge(sem("dist_loaded"), 16)
            for i in range(NI):
                hs, qt = divmod(i, NT)
                nk = (qt + 1) * P
                dve.wait_ge(sem("scores_mm"), i + 1)
                if i >= 3:
                    dve.wait_ge(sem("probT_mm"), i - 2)
                pr = prob[i % 3]
                sc = PS[:, 2 * (i % 2):2 * (i % 2) + 2, :].rearrange("p b n -> p (b n)")
                for br in range(3):
                    d0 = (3 * P if qt else 0) + br * nk
                    ins = stt(out=pr[:, br * nk:(br + 1) * nk], in0=dist[:, d0:d0 + nk], scalar=float(sl[br, hs]),
                              in1=sc[:, br * nk:(br + 1) * nk], op0=ALU.mult, op1=ALU.add)
                do(ins, sem("scores_taken"))
                if i >= 1:
                    invert_denominator(i - 1)
                do(v.tensor_reduce(negmax[:, i % 3:i % 3 + 1], pr[:, 0:3 * nk], X, ALU.max, negate=True), sem("max_ready"))
                if i % 4 == 2 and i >= 6:
                    take_output(i // 4 - 1)
            invert_denominator(NI - 1)
            take_output(NI // 4 - 1)
            for m in range(PAIRS):
                low(m, 0)
            dve.wait_ge(sem("x_mm"), 12)
            for q, (n, h) in enumerate(((0, 0), (0, 1), (1, 0), (1, 1))):
                do(v.tensor_tensor(x[:, n, h * 512:(h + 1) * 512], x[:, n, h * 512:(h + 1) * 512], PS[:, 2 + 2 * h + n, :],
                                   ALU.add), sem("x_added"))
            norm_scale(3, hN).then_inc(sem("norm_scaled"), 1)
            norm_take(3, [(hTm, "g11")])
            dve.wait_ge(sem("router_loaded"), 32)
            dve.wait_ge(sem("logits_mm"), 1)
            do(v.tensor_tensor(logits, PS[:, 4, 0:NT * NE].rearrange("p (n e) -> p n e", n=NT), mid(router_bias, NT), ALU.add))
            do(v.tensor_reduce(top[:, 0:NT], logits, X, ALU.max, negate=True), sem("topneg_ready"))
            others = logits.unsqueeze(2).to_broadcast([P, NT, NE, NE])
            own_logit = logits.unsqueeze(3).to_broadcast([P, NT, NE, NE])
            first_wins = cst("tie").rearrange("p (e j) -> p e j", e=NE).unsqueeze(1).to_broadcast([P, NT, NE, NE])
            v.tensor_tensor(beats, others, own_logit, ALU.is_gt)
            do(v.tensor_tensor(ties, others, own_logit, ALU.is_equal))
            do(v.tensor_tensor(ties, ties, first_wins, ALU.mult))
            do(v.tensor_tensor(beats, beats, ties, ALU.add))
            do(v.tensor_reduce(nrank, beats, X, ALU.add))
            do(v.tensor_scalar(chosen, nrank, 2.0, None, ALU.is_lt), sem("chosen_ready"))
            dve.wait_ge(sem("expl_ready"), 1)
            do(v.memset(gates, 0.0))
            do(v.tensor_tensor(expl, expl, chosen, ALU.mult))
            do(v.tensor_reduce(top[:, 2:4], expl, X, ALU.add))
            do(v.reciprocal(top[:, 4:6], top[:, 2:4]))
            for r in range(2):
                ins = v.tensor_tensor(gates[:, :, r * NE:(r + 1) * NE], expl, last(top[:, 4:6], NE), ALU.mult)
            do(v.memset(slotof, -1.0))
            do(v.tensor_scalar(expl, chosen, 1000.0, -1000.0, ALU.mult, ALU.add))
            dve.wait_ge(sem("ranks_mm"), 1)
            do(v.tensor_tensor(nrank, PS[:, 5, 0:NT * NE].rearrange("p (n e) -> p n e", n=NT), chosen, ALU.mult))
            do(v.tensor_tensor(slotof[:, :, 0:NE], nrank, expl, ALU.add))
            do(v.tensor_scalar(slotof[:, :, NE:2 * NE], slotof[:, :, 0:NE], -float(P), None, ALU.add))
            do(v.tensor_reduce(top[:, 6:7], PS[:, 5, 16:24], X, ALU.max))
            do(v.tensor_scalar(overflow[:], top[:, 6:7], float(P), None, ALU.is_gt), sem("overflow_known"))

            def one_hot(i):
                for n in range(NT):
                    v.tensor_scalar(onehot[:, n, :], cst("slotid"), slotof[:, n, bass.ds(i, 1)], None, ALU.is_equal)
                    ins = v.tensor_scalar(gated[:, n, :], cst("slotid"), slotof[:, n, bass.ds(i, 1)],
                                          gates[:, n, bass.ds(i, 1)], ALU.is_equal, ALU.mult)
                ins.then_inc(sem("onehot_ready"), 1)

            def take_gathered(i, part):
                dve.wait_ge(sem("gather_mm"), 2 * i + (part + 1))
                v.tensor_tensor(gathered[part], PS[:, 7 - part, :].rearrange("p (k n) -> p k n", k=4),
                                last(vec("g11")[:, 4 * part:4 * part + 4], P), ALU.mult).then_inc(sem("gathered"), 1)
                dve.wait_ge(sem("gathered_high"), 2 * i + (part + 1))
                v.tensor_tensor(hTe_low[:, 4 * part:4 * part + 4, :], gathered[part], hTe_high[:, 4 * part:4 * part + 4, :],
                                ALU.subtract).then_inc(sem("gathered_low"), 1)

            def take_scatter_matrix(i):
                dve.wait_ge(sem("scatT_mm"), i + 1)
                v.tensor_copy(scatT, PS[:, 7, 0:2 * P]).then_inc(sem("scatT_ready"), 1)

            one_hot(0)
            take_gathered(0, 0)
            take_gathered(0, 1)
            take_scatter_matrix(0)

            def expert(i, following):
                def hidden_low(j):
                    dve.wait_ge(sem("hidT_high"), ECH * i + (j + 1))
                    v.tensor_tensor(hidT_low, PS[:, 6, :].rearrange("p (f n) -> p f n", f=4), hidT_high,
                                    ALU.subtract).then_inc(sem("hidT_low"), 1)

                for j in range(ECH):
                    for m in split_ahead(j):
                        low(m, i)
                    if j:
                        hidden_low(j - 1)
                        for h in range(2):
                            low(moe_at[("w2", j - 1, h)], i)
                    if j == 2:
                        one_hot(i + 1)
                    dve.wait_ge(sem("silu_ready"), ECH * i + (j + 1))
                    dve.wait_ge(sem("unit_used"), PER_E * i + (moe_at[("w3", j, 1)] + 1))
                    v.tensor_tensor(hidE, siluE, PS[:, 2 * (j % 2) + 1, :], ALU.mult).then_inc(sem("hidden_ready"), 1)
                for h in range(2):
                    low(moe_at[("w2", ECH - 1, h)], i)
                hidden_low(ECH - 1)
                if following:
                    low(0, i + 1)
                take_gathered(i + 1, 0)
                if following:
                    low(1, i + 1)
                take_gathered(i + 1, 1)
                if following:
                    low(2, i + 1)
                for n in range(NT):
                    for h in range(2):
                        q = 2 * n + h
                        dve.wait_ge(sem("scatter_mm"), 4 * i + (q + 1))
                        xs = x[:, n, h * 512:(h + 1) * 512]
                        v.tensor_tensor(xs, xs, PS[:, (4, 5, 2, 3)[q], :], ALU.add).then_inc(sem("scattered"), 1)
                take_scatter_matrix(i + 1)
                dve.wait_ge(sem("scattered"), 4 * i + 4)
                dve.wait_ge(sem("scatT_ready"), i + 2)

            def experts(base):
                if base:
                    for m in range(PAIRS):
                        low(m, base)
                with dve.Fori(0, NE - 1) as e:
                    expert(e + base if base else e, True)
                expert(base + NE - 1, False)

            experts(0)
            dve.wait_ge(sem("overflow_known"), 1)
            more = dve.value_load(overflow[0:1, 0:1])
            with dve.If(more > 0):
                experts(NE)
            do(v.memset(ss, 0.0), sem("experts_over"))
            norm_scale(4, out_sb)
            do(v.memset(top[:, 7:8], 0.0))
            dve.wait_ge(sem("final_gain_loaded"), 16)
            for n in range(NT):
                v.tensor_tensor(out_sb[:, n, :], out_sb[:, n, :], final_gain, ALU.mult).then_inc(sem("out_ready"), 1)


_DIRECT = ["x", "rwkv_wr", "rwkv_wk", "rwkv_wv", "rwkv_w1", "rwkv_w2", "rwkv_a1", "rwkv_a2", "rwkv_g1", "rwkv_g2",
           "rwkv_wo", "w_kv", "attn_wq", "attn_wo", "ffn_w1", "ffn_w3", "ffn_w2", "moe_router", "moe_w1", "moe_w3", "moe_w2"]


def kernel(**inputs):
    import concourse.bacc as bacc
    from concourse.bass_utils import run_bass_kernel_spmd

    a = {k: np.ascontiguousarray(v) for k, v in inputs.items()}
    arrays = {n: a[n] for n in _DIRECT}
    named = {"g00": a["norm_gain"][0, 0], "g01": a["norm_gain"][0, 1], "g10": a["norm_gain"][1, 0],
             "g11": a["norm_gain"][1, 1], "kvg": a["kv_norm_gain"], "w0": a["rwkv_w0"][0], "a0": a["rwkv_a0"][0],
             "k_k": a["rwkv_k_k"][0], "k_a": a["rwkv_k_a"][0], "r_k": a["rwkv_r_k"][0].reshape(D),
             "lnw": a["rwkv_lnx_w"][0], "lnb": a["rwkv_lnx_b"][0]}
    for m in range(6):
        named[f"mu{m}"] = a["rwkv_mu"][0, m]
    arrays["vectors"] = np.ascontiguousarray(np.concatenate([named[n].reshape(KC, P).T for n in VECS], axis=1))
    arrays["final_gain_rows"] = np.ascontiguousarray(np.broadcast_to(a["final_norm_gain"], (P, D)))
    arrays["router_bias_rows"] = np.ascontiguousarray(np.broadcast_to(a["moe_router_bias"][0], (P, NE)))
    arrays["const_tables"] = np.ascontiguousarray(np.concatenate(list(constant_tables().values()), axis=1))
    arrays["distance_tables"] = distance_tables()

    nc = bacc.Bacc("TRN2", target_bir_lowering=False, num_devices=1)
    aps = {n: nc.dram_tensor(f"in_{n}", v.shape, mybir.dt.from_np(v.dtype), kind="ExternalInput").ap()
           for n, v in arrays.items()}
    out = nc.dram_tensor("out_x", (1, S, D), F32, kind="ExternalOutput").ap()
    trunk(nc, aps, out)
    r = run_bass_kernel_spmd(nc, [{f"in_{n}": v for n, v in arrays.items()}], core_ids=[0])
    return r.results[0]["out_x"]
```
